# Optimizing a Trainium2 kernel written in Bass

```python
import jax, jax.numpy as jnp
from jax import lax
import numpy as np

D_MODEL = 1024
BATCH = 1
SEQ = 256
DEPTH = 2

MEM_LEN = 256
N_MIXERS = 2
SB_HEADS = 12
SB_HEAD_DIM = 64
SB_WIDTH = SB_HEADS * SB_HEAD_DIM
SB_BLOCK = 128
DN_HEADS = 6
DN_HEAD_DIM = 128
DN_WIDTH = DN_HEADS * DN_HEAD_DIM
DN_CONV = 4
DN_CHUNK = 64
XA_HEADS = 4
XA_HEAD_DIM = 64
XA_WIDTH = XA_HEADS * XA_HEAD_DIM
MIX_WIDTH = SB_WIDTH + XA_WIDTH
SB_IN = 3 * SB_WIDTH + XA_WIDTH
DN_IN = 4 * DN_WIDTH + 2 * DN_HEADS + XA_WIDTH
D_FF = 3584
N_EXPERTS = 8
TOP_K = 2
MOE_BLOCK = 128
EPS = 1e-6

kernel_name = "hybrid_sb_gdn_xattn_moe"

F32 = jnp.float32

def rmsnorm(x, g):
    xf = x.astype(F32)
    y = xf * lax.rsqrt(jnp.mean(xf * xf, axis=-1, keepdims=True) + EPS) * g.astype(F32)
    return y.astype(x.dtype)

def l2norm(x):
    return x * lax.rsqrt(jnp.sum(x * x, axis=-1, keepdims=True) + EPS)

def causal_depthwise_conv(x, w):
    c = x.shape[-1]
    return lax.conv_general_dilated(
        x, w[:, None, :].astype(x.dtype), window_strides=(1,),
        padding=[(w.shape[0] - 1, 0)], dimension_numbers=('NWC', 'WIO', 'NWC'),
        feature_group_count=c)

def stick_breaking_attention(q, k, v):
    b, s, h, d = q.shape
    nb = s // SB_BLOCK
    scale = d ** -0.5
    kf = k.astype(F32).transpose(0, 2, 1, 3)
    vt = v.transpose(0, 2, 1, 3)
    qb = q.reshape(b, nb, SB_BLOCK, h, d).transpose(1, 0, 3, 2, 4)
    key_pos = jnp.arange(s)

    def block(args):
        q_blk, blk = args
        q_pos = blk * SB_BLOCK + jnp.arange(SB_BLOCK)
        z = jnp.einsum('bhqd,bhkd->bhqk', q_blk.astype(F32), kf) * scale
        causal = key_pos[None, :] < q_pos[:, None]
        log_1m = jnp.where(causal, jax.nn.log_sigmoid(-z), 0.0)
        after = lax.cumsum(log_1m, axis=3, reverse=True) - log_1m
        a = jnp.where(causal, jnp.exp(jax.nn.log_sigmoid(z) + after), 0.0)
        return jnp.einsum('bhqk,bhkd->bhqd', a.astype(vt.dtype), vt)

    o = lax.map(block, (qb, jnp.arange(nb)))
    return o.transpose(1, 0, 3, 2, 4).reshape(b, s, h * d)

def gated_delta_rule(q, k, v, g, beta):
    b, s, h, dk = q.shape
    dv = v.shape[-1]
    c = DN_CHUNK
    n = s // c

    def to_chunks(t):
        return t.reshape(b, n, c, h, t.shape[-1]).transpose(0, 3, 1, 2, 4)

    def to_chunks_s(t):
        return t.reshape(b, n, c, h).transpose(0, 3, 1, 2)

    qc, kc, vc = to_chunks(q), to_chunks(k), to_chunks(v)
    gc = lax.cumsum(to_chunks_s(g), axis=3)
    bc = to_chunks_s(beta)
    kb = kc * bc[..., None]
    vb = vc * bc[..., None]
    tri = jnp.tril(jnp.ones((c, c), bool))
    strict = jnp.tril(jnp.ones((c, c), bool), -1)
    decay = jnp.exp(jnp.where(tri, gc[..., :, None] - gc[..., None, :], -jnp.inf))
    kk = jnp.einsum('bhncd,bhnsd->bhncs', kb, kc) * decay
    lower = jnp.where(strict, kk, 0.0) + jnp.eye(c, dtype=F32)
    rhs = jnp.concatenate([vb, kb * jnp.exp(gc)[..., None]], axis=-1)
    sol = lax.linalg.triangular_solve(lower, rhs, left_side=True, lower=True, unit_diagonal=True)
    u, w = sol[..., :dv], sol[..., dv:]
    qk = jnp.where(tri, jnp.einsum('bhncd,bhnsd->bhncs', qc, kc) * decay, 0.0)
    q_dec = qc * jnp.exp(gc)[..., None]
    g_last = gc[..., -1]
    k_dec = kc * jnp.exp(g_last[..., None] - gc)[..., None]

    def step(state, xs):
        q_d, qk_c, u_c, w_c, k_d, gl = xs
        v_new = u_c - jnp.einsum('bhck,bhkv->bhcv', w_c, state)
        o = jnp.einsum('bhck,bhkv->bhcv', q_d, state) + jnp.einsum('bhcs,bhsv->bhcv', qk_c, v_new)
        state = state * jnp.exp(gl)[..., None, None] + jnp.einsum('bhck,bhcv->bhkv', k_d, v_new)
        return state, o

    xs = tuple(jnp.moveaxis(t, 2, 0) for t in (q_dec, qk, u, w, k_dec, g_last))
    s0 = jnp.zeros((b, h, dk, dv), F32)
    _, o = lax.scan(step, s0, xs)
    return o.transpose(1, 0, 3, 2, 4).reshape(b, s, h, dv)

def stick_breaking_mixer(hn, w_in, q_gain, k_gain):
    b, s, _ = hn.shape
    proj = hn @ w_in
    q = proj[..., :SB_WIDTH].reshape(b, s, SB_HEADS, SB_HEAD_DIM)
    k = proj[..., SB_WIDTH:2 * SB_WIDTH].reshape(b, s, SB_HEADS, SB_HEAD_DIM)
    v = proj[..., 2 * SB_WIDTH:3 * SB_WIDTH].reshape(b, s, SB_HEADS, SB_HEAD_DIM)
    xq = proj[..., 3 * SB_WIDTH:]
    o = stick_breaking_attention(rmsnorm(q, q_gain), rmsnorm(k, k_gain), v)
    return o, xq

def deltanet_mixer(hn, w_in, conv_w, a_log, dt_bias, o_gain):
    b, s, _ = hn.shape
    proj = hn @ w_in
    qkv = jax.nn.silu(causal_depthwise_conv(proj[..., :3 * DN_WIDTH], conv_w)).astype(F32)
    gate = proj[..., 3 * DN_WIDTH:4 * DN_WIDTH].reshape(b, s, DN_HEADS, DN_HEAD_DIM).astype(F32)
    a = proj[..., 4 * DN_WIDTH:4 * DN_WIDTH + DN_HEADS].astype(F32)
    bb = proj[..., 4 * DN_WIDTH + DN_HEADS:4 * DN_WIDTH + 2 * DN_HEADS].astype(F32)
    xq = proj[..., 4 * DN_WIDTH + 2 * DN_HEADS:]
    q = qkv[..., :DN_WIDTH].reshape(b, s, DN_HEADS, DN_HEAD_DIM)
    k = qkv[..., DN_WIDTH:2 * DN_WIDTH].reshape(b, s, DN_HEADS, DN_HEAD_DIM)
    v = qkv[..., 2 * DN_WIDTH:].reshape(b, s, DN_HEADS, DN_HEAD_DIM)
    q = l2norm(q) * (DN_HEAD_DIM ** -0.5)
    k = l2norm(k)
    beta = jax.nn.sigmoid(bb)
    g = -jnp.exp(a_log.astype(F32)) * jax.nn.softplus(a + dt_bias.astype(F32))
    o = gated_delta_rule(q, k, v, g, beta)
    o = rmsnorm(o, o_gain) * jax.nn.silu(gate)
    return o.reshape(b, s, DN_WIDTH).astype(hn.dtype), xq

def memory_cross_attention(xq, mem_kv, q_gain, k_gain):
    b, s, _ = xq.shape
    m = mem_kv.shape[1]
    q = rmsnorm(xq.reshape(b, s, XA_HEADS, XA_HEAD_DIM), q_gain)
    k = rmsnorm(mem_kv[..., :XA_WIDTH].reshape(b, m, XA_HEADS, XA_HEAD_DIM), k_gain)
    v = mem_kv[..., XA_WIDTH:].reshape(b, m, XA_HEADS, XA_HEAD_DIM)
    sc = jnp.einsum('bshd,bmhd->bhsm', q.astype(F32), k.astype(F32)) * (XA_HEAD_DIM ** -0.5)
    p = jax.nn.softmax(sc, axis=-1)
    o = jnp.einsum('bhsm,bmhd->bshd', p.astype(v.dtype), v)
    return o.reshape(b, s, XA_WIDTH)

def swiglu(x, w_gate, w_up, w_down):
    return (jax.nn.silu(x @ w_gate) * (x @ w_up)) @ w_down

def moe_swiglu(h, router, w_gate, w_up, w_down):
    b, s, d = h.shape
    t = b * s
    x = h.reshape(t, d)
    logits = x.astype(F32) @ router.astype(F32)
    top_logit, top_idx = lax.top_k(logits, TOP_K)
    top_w = jax.nn.softmax(top_logit, axis=-1)
    n_assign = t * TOP_K
    flat_e = top_idx.reshape(-1)
    flat_tok = jnp.repeat(jnp.arange(t, dtype=jnp.int32), TOP_K)
    flat_w = top_w.reshape(-1)
    order = jnp.argsort(flat_e)
    se, stok, sw = flat_e[order], flat_tok[order], flat_w[order]
    counts = jnp.bincount(flat_e, length=N_EXPERTS)
    padded = (counts + MOE_BLOCK - 1) // MOE_BLOCK * MOE_BLOCK
    start = jnp.cumsum(counts) - counts
    pend = jnp.cumsum(padded)
    pstart = pend - padded
    dest = pstart[se] + jnp.arange(n_assign) - start[se]
    nblk = -(-n_assign // MOE_BLOCK) + N_EXPERTS
    cap = nblk * MOE_BLOCK
    tok_buf = jnp.zeros((cap,), jnp.int32).at[dest].set(stok)
    w_buf = jnp.zeros((cap,), F32).at[dest].set(sw)
    blk_e = jnp.minimum(jnp.searchsorted(pend, jnp.arange(nblk) * MOE_BLOCK, side='right'), N_EXPERTS - 1)

    def block(args):
        tok, wt, e = args
        xb = x[tok]
        y = swiglu(xb, w_gate[e], w_up[e], w_down[e])
        return y * wt[:, None].astype(y.dtype)

    y = lax.map(block, (tok_buf.reshape(nblk, MOE_BLOCK), w_buf.reshape(nblk, MOE_BLOCK), blk_e))
    out = jax.ops.segment_sum(y.reshape(cap, d), tok_buf, num_segments=t)
    return out.reshape(b, s, d)

def setup_inputs(seed: int = 0) -> dict:
    key = jax.random.key(seed)
    ks = iter(jax.random.split(key, 32))
    n_sb = (DEPTH + 1) // 2
    n_dn = DEPTH // 2
    n_dense = (DEPTH + 1) // 2
    n_moe = DEPTH // 2

    def dense(shape, fan_in):
        return jax.random.normal(next(ks), shape, F32) * (fan_in ** -0.5)

    def gain(shape):
        return 1.0 + 0.02 * jax.random.normal(next(ks), shape, F32)

    x = jax.random.normal(next(ks), (BATCH, SEQ, D_MODEL), F32)
    mem = jax.random.normal(next(ks), (BATCH, MEM_LEN, D_MODEL), F32)
    mix_norm = gain((DEPTH, D_MODEL))
    ffn_norm = gain((DEPTH, D_MODEL))
    mem_norm = gain((DEPTH, D_MODEL))
    w_mem_kv = dense((DEPTH, D_MODEL, 2 * XA_WIDTH), D_MODEL)
    xa_q_norm = gain((DEPTH, XA_HEAD_DIM))
    xa_k_norm = gain((DEPTH, XA_HEAD_DIM))
    w_out = dense((DEPTH, MIX_WIDTH, D_MODEL), MIX_WIDTH)
    sb_w_in = dense((n_sb, D_MODEL, SB_IN), D_MODEL)
    sb_q_norm = gain((n_sb, SB_HEAD_DIM))
    sb_k_norm = gain((n_sb, SB_HEAD_DIM))
    dn_w_in = dense((n_dn, D_MODEL, DN_IN), D_MODEL)
    dn_conv = dense((n_dn, DN_CONV, 3 * DN_WIDTH), DN_CONV)
    dn_a_log = jnp.log(jax.random.uniform(next(ks), (n_dn, DN_HEADS), F32, 1.0, 16.0))
    dt = jnp.exp(jax.random.uniform(next(ks), (n_dn, DN_HEADS), F32, float(np.log(1e-3)), float(np.log(1e-1))))
    dn_dt_bias = jnp.log(jnp.expm1(dt))
    dn_o_norm = gain((n_dn, DN_HEAD_DIM))
    ffd_w_gate = dense((n_dense, D_MODEL, D_FF), D_MODEL)
    ffd_w_up = dense((n_dense, D_MODEL, D_FF), D_MODEL)
    ffd_w_down = dense((n_dense, D_FF, D_MODEL), D_FF)
    moe_router = dense((n_moe, D_MODEL, N_EXPERTS), D_MODEL)
    moe_w_gate = dense((n_moe, N_EXPERTS, D_MODEL, D_FF), D_MODEL)
    moe_w_up = dense((n_moe, N_EXPERTS, D_MODEL, D_FF), D_MODEL)
    moe_w_down = dense((n_moe, N_EXPERTS, D_FF, D_MODEL), D_FF)
    return {"x": x, "mem": mem, "mix_norm": mix_norm, "ffn_norm": ffn_norm, "mem_norm": mem_norm,
            "w_mem_kv": w_mem_kv, "xa_q_norm": xa_q_norm, "xa_k_norm": xa_k_norm, "w_out": w_out,
            "sb_w_in": sb_w_in, "sb_q_norm": sb_q_norm, "sb_k_norm": sb_k_norm,
            "dn_w_in": dn_w_in, "dn_conv": dn_conv, "dn_a_log": dn_a_log, "dn_dt_bias": dn_dt_bias,
            "dn_o_norm": dn_o_norm, "ffd_w_gate": ffd_w_gate, "ffd_w_up": ffd_w_up, "ffd_w_down": ffd_w_down,
            "moe_router": moe_router, "moe_w_gate": moe_w_gate, "moe_w_up": moe_w_up, "moe_w_down": moe_w_down}

def reference(x, mem, mix_norm, ffn_norm, mem_norm, w_mem_kv, xa_q_norm, xa_k_norm, w_out,
              sb_w_in, sb_q_norm, sb_k_norm, dn_w_in, dn_conv, dn_a_log, dn_dt_bias, dn_o_norm,
              ffd_w_gate, ffd_w_up, ffd_w_down, moe_router, moe_w_gate, moe_w_up, moe_w_down):
    h = x
    for i in range(DEPTH):
        j = i // N_MIXERS
        hn = rmsnorm(h, mix_norm[i])
        if i % N_MIXERS == 0:
            mix, xq = stick_breaking_mixer(hn, sb_w_in[j], sb_q_norm[j], sb_k_norm[j])
        else:
            mix, xq = deltanet_mixer(hn, dn_w_in[j], dn_conv[j], dn_a_log[j], dn_dt_bias[j], dn_o_norm[j])
        mem_kv = rmsnorm(mem, mem_norm[i]) @ w_mem_kv[i]
        xa = memory_cross_attention(xq, mem_kv, xa_q_norm[i], xa_k_norm[i])
        h = h + jnp.concatenate([mix, xa], axis=-1) @ w_out[i]
        hn = rmsnorm(h, ffn_norm[i])
        c = i // 2
        if i % 2 == 0:
            h = h + swiglu(hn, ffd_w_gate[c], ffd_w_up[c], ffd_w_down[c])
        else:
            h = h + moe_swiglu(hn, moe_router[c], moe_w_gate[c], moe_w_up[c], moe_w_down[c])
    return h


_drawn_inputs = setup_inputs


def setup_inputs(seed=0):
    import zlib

    import numpy as np

    out = dict(_drawn_inputs(seed))
    spreads = {}
    factors = {'mem_norm': 8.0,
     'xa_q_norm': 8.0,
     'xa_k_norm': 4.91,
     'sb_q_norm': 4.175,
     'sb_k_norm': 4.207,
     'dn_o_norm': 26.002,
     'ffn_norm': 3.042}
    for name, (base, spread) in spreads.items():
        noise = np.random.default_rng([zlib.crc32(name.encode()), seed]).standard_normal(out[name].shape)
        drawn = base * np.exp(spread * noise) if base else spread * noise
        out[name] = __import__('jax').numpy.asarray(drawn.astype(out[name].dtype))
    for name, factor in factors.items():
        out[name] = (out[name] * factor).astype(out[name].dtype)
    return out
```

```python
from contextlib import ExitStack

import numpy as np

import concourse.bass as bass
from concourse import mybir

P = 128
D = 1024
S = 256
NT = S // P
KC = D // P
HD = 64
SBH, XAH, DNH = 12, 4, 6
SBW, XAW, DNW = SBH * HD, XAH * HD, DNH * P
SB_IN = 3 * SBW + XAW
DN_IN = 4 * DNW + 2 * DNH + XAW
FF = 3584
NE = 8
GF = 256
NG = FF // GF
SLOTS = 7
SLOT = 2 * KC * GF + GF // P * D
CAP = 96
NPB = -(-S // CAP)
EPS = 1e-6
ASLOT = KC * 512
ASLOTS = 3
NEG = -1.0e30

F32 = mybir.dt.float32
BF16 = mybir.dt.bfloat16
I32 = mybir.dt.int32
ALU = mybir.AluOpType
ACT = mybir.ActivationFunctionType
X_AXIS = mybir.AxisListType.X


def hybrid_kernel(nc, x, mem, mix_norm, ffn_norm, mem_norm, w_mem_kv, xa_q_norm, xa_k_norm, w_out,
                  sb_w_in, sb_q_norm, sb_k_norm, dn_w_in, dn_conv, dn_a_log, dn_dt_bias, dn_o_norm,
                  ffd_w_gate, ffd_w_up, ffd_w_down, moe_router, moe_w_gate, moe_w_up, moe_w_down, out):
    with ExitStack() as ctx:
        def sb(name, shape, dt=F32):
            return ctx.enter_context(nc.sbuf_tensor(name, shape, dt))

        layer_sems = []

        def sem(name):
            return ctx.enter_context(nc.semaphore(name))

        def lsem(name):
            h = layer_sems[0].enter_context(nc.semaphore(name))
            layer_sems[1].append(h)
            return h

        def next_layer():
            if layer_sems:
                with nc.Block() as block:
                    @block.gpsimd
                    def _(pool):
                        for h in layer_sems[1]:
                            pool.sem_clear(h)
                layer_sems[0].close()
            layer_sems[:] = [ctx.enter_context(ExitStack()), []]

        s_y = sem("s_y")
        next_layer()

        X = sb("X", [P, NT, D])
        hT = sb("hT", [P, KC, S])
        xn = sb("xn", [P, NT, D])
        gain = sb("gain", [P, 2, D])
        junk = sb("junk", [P, D], BF16)
        stat = sb("stat", [P, 3, 8])
        epsc = sb("epsc", [P, 1])
        ident = sb("ident", [P, P])
        ones = sb("ones", [P, P])
        upincl = sb("upincl", [P, P])
        upstrict = sb("upstrict", [P, P])
        ring = sb("ring", [P, SLOTS * SLOT])
        PS = ctx.enter_context(nc.psum_tensor("PS", [P, 8, 512], F32))

        class Scratch:
            def __init__(self):
                self.at = ASLOTS * ASLOT

            def tile(self, parts, *shape):
                n = int(np.prod(shape))
                v = ring[0:parts, self.at:self.at + n]
                self.at += n
                assert self.at <= SLOTS * SLOT, (self.at, SLOTS * SLOT)
                names = "abc"[:len(shape)]
                if len(shape) == 1:
                    return v
                return v.rearrange("p (" + " ".join(names) + ") -> p " + " ".join(names),
                                   **{c: k for c, k in zip(names[1:], shape[1:])})

        def aslot(n, cols):
            at = (n % ASLOTS) * ASLOT
            return ring[:, at:at + KC * cols].rearrange("p (c f) -> p c f", c=KC)

        def k_rows(w):
            return w.rearrange("(c p) f -> p c f", p=P)

        s_chain = {}

        def linker(eng, name):
            if name not in s_chain:
                s_chain[name] = [sem(f"s_{name}_chain"), 0]
            c = s_chain[name]

            def link(ins):
                c[1] += 1
                ins.then_inc(c[0], 1)
                eng.wait_ge(c[0], c[1])
            return link

        class NormTranspose:
            def __init__(self, tag, units, keep_rows=False, transpose=True):
                self.units = units
                self.s_sq, self.s_ms, self.s_rstd, self.s_xn = (lsem(f"{tag}_{n}") for n in ("sq", "ms", "rstd", "xn"))
                self.s_tr, self.s_eva, self.s_evd = (lsem(f"{tag}_{n}") for n in ("tr", "eva", "evd"))

            def act_squares(self, act, link):
                for u, (src, g, dst, ready) in enumerate(self.units):
                    act.wait_ge(*ready)
                    if u >= 1:
                        act.wait_ge(self.s_sq, u)
                    act.activation(junk[:], src, ACT.Square, accum_out=stat[:, 0, u:u + 1]).then_inc(self.s_sq, 1)

            def act_rstd(self, act, link):
                n = len(self.units)
                act.wait_ge(self.s_ms, 1)
                link(act.activation(stat[:, 2, 0:n], stat[:, 1, 0:n], ACT.Ln))
                act.activation(stat[:, 2, 0:n], stat[:, 2, 0:n], ACT.Exp, scale=-0.5).then_inc(self.s_rstd, 1)

            def act_evacuate(self, act):
                for u, (src, g, dst, ready) in enumerate(self.units):
                    act.wait_ge(self.s_tr, 2 * u + 1)
                    act.activation(dst[:, 0:4, :], PS[:, 0, :].rearrange("p (c t) -> p c t", c=4),
                                   ACT.Copy).then_inc(self.s_eva, 1)

            def dve_rows(self, dve):
                n = len(self.units)
                dve.wait_ge(self.s_sq, n)
                dve.tensor_scalar(stat[:, 1, 0:n], stat[:, 0, 0:n], 1.0 / D, EPS, ALU.mult, ALU.add).then_inc(self.s_ms, 1)
                dve.wait_ge(self.s_rstd, 1)
                for u, (src, g, dst, ready) in enumerate(self.units):
                    if u >= NT:
                        self.dve_evacuate_one(dve, u - NT)
                    dve.scalar_tensor_tensor(out=xn[:, u % NT, :], in0=src, scalar=stat[:, 2, u:u + 1], in1=g,
                                             op0=ALU.mult, op1=ALU.mult).then_inc(self.s_xn, 1)
                for u in range(max(0, n - NT), n):
                    self.dve_evacuate_one(dve, u)

            def dve_evacuate_one(self, dve, u):
                dve.wait_ge(self.s_tr, 2 * u + 2)
                dve.tensor_copy(self.units[u][2][:, 4:8, :],
                                PS[:, 1, :].rearrange("p (c t) -> p c t", c=4)).then_inc(self.s_evd, 1)

            def pe(self, pe):
                for u in range(len(self.units)):
                    pe.wait_ge(self.s_xn, u + 1)
                    for half, freed in ((0, self.s_eva), (1, self.s_evd)):
                        if u >= 1:
                            pe.wait_ge(freed, u)
                        for c in range(4):
                            mm = pe.transpose(PS[:, half, c * P:(c + 1) * P],
                                              xn[:, u % NT, (4 * half + c) * P:(4 * half + c + 1) * P], ident[:])
                        mm.then_inc(self.s_tr, 1)

            def ready(self, eng, units):
                eng.wait_ge(self.s_eva, units)
                eng.wait_ge(self.s_evd, units)

        class CrossPrep:
            def __init__(self, tag, q_tok, kv_tok, qT, kT, sq, st, gq, gk, banks):
                self.q_tok, self.kv_tok, self.qT, self.kT = q_tok, kv_tok, qT, kT
                self.sq, self.st, self.gq, self.gk, self.banks = sq, st, gq, gk, banks
                self.s_sq, self.s_ms, self.s_rstd, self.s_n = (lsem(f"{tag}_{n}") for n in ("sq", "ms", "rstd", "n"))
                self.s_tr, self.s_eva = lsem(f"{tag}_tr"), lsem(f"{tag}_eva")

            def act(self, act, link, ready):
                ready(act)
                act.activation(self.sq[:, :, 0:XAW], self.q_tok, ACT.Square).then_inc(self.s_sq, 1)
                act.activation(self.sq[:, :, XAW:2 * XAW], self.kv_tok[:, :, 0:XAW], ACT.Square).then_inc(self.s_sq, 1)
                act.wait_ge(self.s_ms, 1)
                link(act.activation(self.st[:, 1], self.st[:, 1], ACT.Ln))
                act.activation(self.st[:, 1], self.st[:, 1], ACT.Exp, scale=-0.5).then_inc(self.s_rstd, 1)

            def dve(self, dve, link, ready):
                dve.wait_ge(self.s_sq, 2)
                link(dve.tensor_reduce(self.st[:, 0].rearrange("p (t h) -> p t h", t=NT),
                                       self.sq.rearrange("p t (h d) -> p t h d", d=HD), X_AXIS, ALU.add))
                dve.tensor_scalar(self.st[:, 1], self.st[:, 0], 1.0 / HD, EPS, ALU.mult, ALU.add).then_inc(self.s_ms, 1)
                dve.wait_ge(self.s_rstd, 1)
                ready(dve)
                r = self.st[:, 1].rearrange("p (t h) -> p t h", t=NT)
                for v, h0 in ((self.q_tok, 0), (self.kv_tok[:, :, 0:XAW], XAH)):
                    for t in range(NT):
                        w = v[:, t, :].rearrange("p (h d) -> p h d", d=HD)
                        dve.tensor_tensor(w, w, r[:, t, h0:h0 + XAH].unsqueeze(2).to_broadcast([P, XAH, HD]),
                                          ALU.mult).then_inc(self.s_n, 1)

            def pe(self, pe, freed):
                for j in range(4):
                    pe.wait_ge(self.s_n, 2 * NT)
                    freed(pe, j)
                    src = self.q_tok if j < 2 else self.kv_tok
                    for i in range(2):
                        h = 2 * (j % 2) + i
                        for t in range(NT):
                            mm = pe.transpose(PS[0:HD, self.banks[j], (i * NT + t) * P:(i * NT + t + 1) * P],
                                              src[:, t, h * HD:(h + 1) * HD], ident[:])
                    mm.then_inc(self.s_tr, 1)

            def act_evacuate(self, act):
                for j in range(4):
                    act.wait_ge(self.s_tr, j + 1)
                    dst = (self.qT if j < 2 else self.kT)[:, 2 * (j % 2):2 * (j % 2) + 2, :]
                    act.activation(dst, PS[0:HD, self.banks[j], :].rearrange("p (h t) -> p h t", h=2), ACT.Copy,
                                   scale=(self.gq if j < 2 else self.gk)).then_inc(self.s_eva, 1)

        class Cross:
            def __init__(self, tag, qT, kT, v_tok, mix, c0, tmp):
                self.qT, self.kT, self.v, self.mix, self.c0 = qT, kT, v_tok, mix, c0
                self.prob, self.probT, self.st = tmp
                self.s_s, self.s_max, self.s_p, self.s_pt, self.s_pe, self.s_o, self.s_mix, self.s_rec = (
                    lsem(f"{tag}_{n}") for n in ("scores", "max", "probs", "probsT", "probsT_out", "o", "mix", "rec"))
                self.units = [(h, t) for h in range(XAH) for t in range(NT)]

            def pe(self, pe, begin):
                n = len(self.units)
                begin(pe)
                for i in range(n + 2):
                    if i < n:
                        h, t = self.units[i]
                        if i >= 2:
                            pe.wait_ge(self.s_p, i - 1)
                        pe.matmul(PS[:, i % 2, 0:S], self.qT[:, h, t * P:(t + 1) * P], self.kT[:, h, :],
                                  start=True, stop=True).then_inc(self.s_s, 1)
                    if 1 <= i <= n:
                        j = i - 1
                        pe.wait_ge(self.s_p, j + 1)
                        if j >= 2:
                            pe.wait_ge(self.s_pe, j - 1)
                        for m in range(NT):
                            mm = pe.transpose(PS[:, 2 + j % 2, m * P:(m + 1) * P],
                                              self.prob[:, j % 2, m * P:(m + 1) * P], ident[:])
                        mm.then_inc(self.s_pt, 1)
                    if i >= 2:
                        j = i - 2
                        h, t = self.units[j]
                        pe.wait_ge(self.s_pe, j + 1)
                        if j >= 2:
                            pe.wait_ge(self.s_mix, j - 1)
                        for m in range(NT):
                            mm = pe.matmul(PS[:, 4 + j % 2, 0:HD], self.probT[:, j % 2, m * P:(m + 1) * P],
                                           self.v[:, m, h * HD:(h + 1) * HD], start=(m == 0), stop=(m == NT - 1))
                        mm.then_inc(self.s_o, 1)

            def act(self, act):
                n = len(self.units)
                for i in range(n + 1):
                    if i < n:
                        act.wait_ge(self.s_max, i + 1)
                        if i >= 2:
                            act.wait_ge(self.s_pt, i - 1)
                        act.activation(self.prob[:, i % 2, :], PS[:, i % 2, 0:S], ACT.Exp,
                                       bias=self.st[:, 0, i:i + 1],
                                       accum_out=self.st[:, 1, i:i + 1]).then_inc(self.s_p, 1)
                    if i >= 1:
                        j = i - 1
                        act.wait_ge(self.s_pt, j + 1)
                        if j >= 2:
                            act.wait_ge(self.s_o, j - 1)
                        act.activation(self.probT[:, j % 2, :], PS[:, 2 + j % 2, 0:S], ACT.Copy).then_inc(self.s_pe, 1)

            def dve(self, dve):
                n = len(self.units)
                for i in range(n + 2):
                    if i < n:
                        dve.wait_ge(self.s_s, i + 1)
                        dve.tensor_reduce(self.st[:, 0, i:i + 1], PS[:, i % 2, 0:S], X_AXIS, ALU.max,
                                          negate=True).then_inc(self.s_max, 1)
                    if i >= 2:
                        j = i - 2
                        h, t = self.units[j]
                        dve.wait_ge(self.s_p, j + 1)
                        dve.reciprocal(self.st[:, 2, j:j + 1], self.st[:, 1, j:j + 1]).then_inc(self.s_rec, 1)
                        dve.wait_ge(self.s_rec, j + 1)
                        dve.wait_ge(self.s_o, j + 1)
                        dve.tensor_scalar(self.mix[:, t, self.c0 + h * HD:self.c0 + (h + 1) * HD],
                                          PS[:, 4 + j % 2, 0:HD], self.st[:, 2, j:j + 1], None,
                                          ALU.mult).then_inc(self.s_mix, 1)

        class OutProjection:
            def __init__(self, tag, mix, slots, s_w):
                self.mix, self.slots, self.s_w = mix, slots, s_w
                self.s_tr, self.s_eva, self.s_evd, self.s_y, self.s_x = (
                    lsem(f"{tag}_{n}") for n in ("tr", "eva", "evd", "y", "x"))

            def pe(self, pe, ready):
                ready(pe)
                for t in range(NT):
                    for half, freed in ((0, self.s_eva), (1, self.s_evd)):
                        if t >= 1:
                            pe.wait_ge(freed, t)
                        for c in range(4):
                            k = 4 * half + c
                            mm = pe.transpose(PS[:, 6 + half, c * P:(c + 1) * P], self.mix[:, t, k * P:(k + 1) * P], ident[:])
                        mm.then_inc(self.s_tr, 1)
                for half in range(2):
                    self.s_w(pe, half)
                    for t in range(NT):
                        pe.wait_ge(self.s_eva, t + 1)
                        pe.wait_ge(self.s_evd, t + 1)
                        for k in range(KC):
                            mm = pe.matmul(PS[:, 2 * half + t, :], hT[:, k, t * P:(t + 1) * P], self.slots[half][:, k, :],
                                           start=(k == 0), stop=(k == KC - 1))
                        mm.then_inc(self.s_y, 1)

            def act(self, act):
                for t in range(NT):
                    act.wait_ge(self.s_tr, 2 * t + 1)
                    act.activation(hT[:, 0:4, t * P:(t + 1) * P], PS[:, 6, :].rearrange("p (c t) -> p c t", c=4),
                                   ACT.Copy).then_inc(self.s_eva, 1)

            def dve(self, dve):
                for t in range(NT):
                    dve.wait_ge(self.s_tr, 2 * t + 2)
                    dve.tensor_copy(hT[:, 4:8, t * P:(t + 1) * P],
                                    PS[:, 7, :].rearrange("p (c t) -> p c t", c=4)).then_inc(self.s_evd, 1)
                for half in range(2):
                    for t in range(NT):
                        dve.wait_ge(self.s_y, 2 * half + t + 1)
                        xv = X[:, t, half * 512:(half + 1) * 512]
                        dve.tensor_tensor(xv, xv, PS[:, 2 * half + t, :], ALU.add).then_inc(self.s_x, 1)

        def row(v, n):
            return v.rearrange("(a n) -> a n", a=1).to_broadcast([P, n])

        def col(v):
            return v.rearrange("(p a) -> p a", a=1)

        sc = Scratch()
        memr = sc.tile(P, NT, D)
        memT = sc.tile(P, KC, S)
        proj = sc.tile(P, NT, SB_IN)
        kv_tok = sc.tile(P, NT, 2 * XAW)
        qT = sc.tile(HD, SBH, S)
        kT = sc.tile(HD, SBH, S)
        xqT = sc.tile(HD, XAH, S)
        xkT = sc.tile(HD, XAH, S)
        mix = sc.tile(P, NT, D)
        sqs = sc.tile(P, 2 * SBW)
        sqx = sc.tile(P, NT, 2 * XAW)
        hst = sc.tile(P, NT, 2, 2 * SBH)
        xst = sc.tile(P, 2, NT * 2 * XAH)
        gcol = sc.tile(HD, 8)
        negup = sc.tile(P, P)
        negones = sc.tile(P, P)
        diag0 = sc.tile(P, 3, P)
        diagneg = sc.tile(P, P)
        xtmp = (sc.tile(P, 2, S), sc.tile(P, 2, S), sc.tile(P, 3, 8))
        flat = ring[:, ASLOTS * ASLOT:ASLOTS * ASLOT + 2 * NT * D].rearrange("p (k b n) -> p k b n", k=4, b=2)
        habs, hln, hL, hA = (flat[:, i, :, 0:384] for i in range(4))

        s_x, s_mem, s_gain, s_gcol = lsem("s_x"), lsem("s_mem"), sem("s_gain"), lsem("s_gcol")
        s_gain_ffn0, s_gain_mem1, s_gain_mix1, s_gain_ffn1 = (sem(f"s_gain_{n}") for n in ("ffn0", "mem1", "mix1", "ffn1"))
        s_const, s_const2 = sem("s_const"), sem("s_const2")
        s_aw = [sem(f"s_aw{i}") for i in range(ASLOTS)]
        loads0 = [(w_mem_kv[0], 512)] + [(sb_w_in[0][:, c * 512:(c + 1) * 512], 512) for c in range(SB_IN // 512)] + \
                 [(w_out[0][:, c * 512:(c + 1) * 512], 512) for c in range(2)]
        QK = 384
        loads1 = [(w_mem_kv[1], 512)] + [(dn_w_in[0][:, c * QK:(c + 1) * QK], QK) for c in range(8)] + \
                 [(dn_w_in[0][:, 4 * DNW:DN_IN], DN_IN - 4 * DNW)] + [(w_out[1][:, c * 512:(c + 1) * 512], 512) for c in range(2)]
        loads = loads0 + loads1
        N0 = len(loads0)

        def attention_loads(sp, first, last, phase):
            for n in range(first, last):
                if n - ASLOTS >= phase:
                    sp.wait_ge(*load_read[n - ASLOTS])
                w, cols = loads[n]
                sp.dma_start(aslot(n, cols), k_rows(w)).then_inc(s_aw[n % ASLOTS], 16)

        def weights_in(pe, n):
            pe.wait_ge(s_aw[n % ASLOTS], 16 * (n // ASLOTS + 1))
            return aslot(n, loads[n][1])

        norm_a = NormTranspose("na", [
            (memr[:, 0, :], gain[:, 1, :], memT[:, :, 0:P], (s_mem, 16)),
            (memr[:, 1, :], gain[:, 1, :], memT[:, :, P:S], (s_mem, 16)),
            (X[:, 0, :], gain[:, 0, :], hT[:, :, 0:P], (s_x, 16)),
            (X[:, 1, :], gain[:, 0, :], hT[:, :, P:S], (s_x, 16))])
        s_pj, s_pja, s_pjd = lsem("a_proj"), lsem("a_proj_act"), lsem("a_proj_dve")
        s_hsq, s_hms, s_hrs, s_hn, s_g8 = lsem("a_hsq"), lsem("a_hms"), lsem("a_hrs"), lsem("a_hn"), lsem("a_g8")
        s_ht, s_hta, s_htd = lsem("a_ht"), lsem("a_ht_act"), lsem("a_ht_dve")
        jobs_a = [(memT, 0, t, kv_tok[:, t, :]) for t in range(NT)] + \
                 [(hT, 1 + c, t, proj[:, t, c * 512:(c + 1) * 512]) for c in range(SB_IN // 512) for t in range(NT)]
        NJ = len(jobs_a)
        cross0 = CrossPrep("cp0", proj[:, :, 3 * SBW:SB_IN], kv_tok, xqT, xkT, sqx, xst, gcol[:, 4:5], gcol[:, 3:4], (0, 1, 2, 3))
        NHJ = SBH // 2

        load_read = [(s_pj, NT * (n + 1)) for n in range(N0 - 2)]

        with nc.Block() as block:
            @block.sync
            def _(sp):
                sp.dma_start(memr, mem[0].rearrange("(t p) d -> p t d", p=P)).then_inc(s_mem, 16)
                sp.dma_start(X[:], x[0].rearrange("(t p) d -> p t d", p=P)).then_inc(s_x, 16)
                sp.dma_start(gain[:, 1, :], row(mem_norm[0], D)).then_inc(s_gain, 16)
                sp.dma_start(gain[:, 0, :], row(mix_norm[0], D)).then_inc(s_gain, 16)
                attention_loads(sp, 0, 2, 0)
                for i, g in enumerate((sb_q_norm[0], sb_k_norm[0], xa_q_norm[0], xa_k_norm[0])):
                    sp.dma_start(gcol[:, i:i + 1], col(g)).then_inc(s_gcol, 16)
                attention_loads(sp, 2, N0, 0)

            @block.gpsimd
            def _(pool):
                link = linker(pool, "pool")
                pool.memset(epsc[:], EPS).then_inc(s_const, 1)
                link(pool.memset(ident[:], 0.0))
                pool.affine_select(out=ident[:], in_=ident[:], compare_op=ALU.not_equal, fill=1.0, base=0,
                                   pattern=[[-1, P]], channel_multiplier=1).then_inc(s_const, 1)
                for v, val in ((ones[:], 1.0), (negones, -1.0), (diag0.rearrange("p a b -> p (a b)"), 1.0)):
                    link(pool.memset(v, val))
                pool.affine_select(out=upincl[:], in_=ones[:], compare_op=ALU.is_ge, fill=0.0, base=0,
                                   pattern=[[1, P]], channel_multiplier=-1).then_inc(s_const2, 1)
                link(pool.affine_select(out=upstrict[:], in_=ones[:], compare_op=ALU.is_gt, fill=0.0, base=0,
                                        pattern=[[1, P]], channel_multiplier=-1))
                pool.affine_select(out=negup, in_=negones, compare_op=ALU.is_ge, fill=0.0, base=0,
                                   pattern=[[-1, P]], channel_multiplier=1).then_inc(s_const2, 1)
                link(pool.memset(diagneg, 0.0))
                pool.affine_select(out=diagneg, in_=diagneg, compare_op=ALU.is_gt, fill=NEG, base=0,
                                   pattern=[[1, P]], channel_multiplier=-1).then_inc(s_const2, 1)
                for a in (0, 2):
                    pool.tensor_copy(diag0[:, a, :], upstrict[:]).then_inc(s_const2, 1)

            @block.scalar
            def _(act):
                link = linker(act, "act")
                act.preload_act_table_set("natural_log_exp_and_others")
                norm_a.act_squares(act, link)
                norm_a.act_rstd(act, link)
                norm_a.act_evacuate(act)
                for n in range(0, NJ, 2):
                    act.wait_ge(s_pj, n + 1)
                    act.activation(jobs_a[n][3], PS[:, 2 + n % 6, :], ACT.Copy).then_inc(s_pja, 1)
                cross0.act(act, link, lambda e: (e.wait_ge(s_pja, NJ // 2), e.wait_ge(s_pjd, NJ // 2)))
                for t in range(NT):
                    if t >= 1:
                        act.wait_ge(s_hms, t)
                    act.activation(sqs, proj[:, t, 0:2 * SBW], ACT.Square).then_inc(s_hsq, 1)
                    act.wait_ge(s_hms, t + 1)
                    link(act.activation(hst[:, t, 1, :], hst[:, t, 1, :], ACT.Ln))
                    act.activation(hst[:, t, 1, :], hst[:, t, 1, :], ACT.Exp, scale=-0.5).then_inc(s_hrs, 1)
                act.wait_ge(s_g8, 1)
                cross0.act_evacuate(act)
                for j in range(NHJ):
                    act.wait_ge(s_ht, 2 * j + 1)
                    act.activation(qT[:, 2 * j:2 * j + 2, :], PS[0:HD, 4 + (2 * j) % 4, :].rearrange("p (h t) -> p h t", h=2),
                                   ACT.Copy, scale=gcol[:, 5:6]).then_inc(s_hta, 1)

            @block.vector
            def _(dve):
                link = linker(dve, "dve")
                dve.wait_ge(s_gain, 32)
                norm_a.dve_rows(dve)
                for n in range(1, NJ, 2):
                    dve.wait_ge(s_pj, n + 1)
                    dve.tensor_copy(jobs_a[n][3], PS[:, 2 + n % 6, :]).then_inc(s_pjd, 1)
                dve.wait_ge(s_gcol, 64)
                for src, dst in ((2, 4), (0, 5)):
                    g = dve.tensor_scalar(gcol[:, dst:dst + 1], gcol[:, src:src + 1], HD ** -0.5, None, ALU.mult)
                g.then_inc(s_g8, 1)
                cross0.dve(dve, link, lambda e: e.wait_ge(s_pja, NJ // 2))
                for t in range(NT):
                    dve.wait_ge(s_hsq, t + 1)
                    link(dve.tensor_reduce(hst[:, t, 0, :], sqs.rearrange("p (h d) -> p h d", d=HD), X_AXIS, ALU.add))
                    dve.tensor_scalar(hst[:, t, 1, :], hst[:, t, 0, :], 1.0 / HD, EPS, ALU.mult, ALU.add).then_inc(s_hms, 1)
                    dve.wait_ge(s_hrs, t + 1)
                    w = proj[:, t, 0:2 * SBW].rearrange("p (h d) -> p h d", d=HD)
                    dve.tensor_tensor(w, w, hst[:, t, 1, :].unsqueeze(2).to_broadcast([P, 2 * SBH, HD]),
                                      ALU.mult).then_inc(s_hn, 1)
                for j in range(NHJ):
                    dve.wait_ge(s_ht, 2 * j + 2)
                    dve.tensor_scalar(kT[:, 2 * j:2 * j + 2, :], PS[0:HD, 4 + (2 * j + 1) % 4, :].rearrange("p (h t) -> p h t", h=2),
                                      gcol[:, 1:2], None, ALU.mult).then_inc(s_htd, 1)

            @block.tensor
            def _(pe):
                pe.wait_ge(s_const, 2)
                norm_a.pe(pe)
                for n, (rows, load, t, dst) in enumerate(jobs_a):
                    if rows is memT:
                        norm_a.ready(pe, 2)
                    else:
                        norm_a.ready(pe, 4)
                    w = weights_in(pe, load)
                    if n >= 6:
                        pe.wait_ge(s_pja if n % 2 == 0 else s_pjd, (n - 6) // 2 + 1)
                    for k in range(KC):
                        mm = pe.matmul(PS[:, 2 + n % 6, :], rows[:, k, t * P:(t + 1) * P], w[:, k, :],
                                       start=(k == 0), stop=(k == KC - 1))
                    mm.then_inc(s_pj, 1)
                cross0.pe(pe, lambda e, j: (e.wait_ge(s_pja, NJ // 2), e.wait_ge(s_pjd, NJ // 2)) if j == 0 else None)
                for j in range(2 * NHJ):
                    pe.wait_ge(s_hn, NT)
                    if j >= 4:
                        pe.wait_ge(s_hta if j % 2 == 0 else s_htd, (j - 4) // 2 + 1)
                    base = (j % 2) * SBW
                    for i in range(2):
                        h = 2 * (j // 2) + i
                        for t in range(NT):
                            mm = pe.transpose(PS[0:HD, 4 + j % 4, (i * NT + t) * P:(i * NT + t + 1) * P],
                                              proj[:, t, base + h * HD:base + (h + 1) * HD], ident[:])
                    mm.then_inc(s_ht, 1)

        s_z, s_ab, s_ex, s_ln, s_Lr, s_L, s_cum, s_a, s_o, s_oe = (
            lsem(f"b_{n}") for n in ("z", "abs", "exp", "ln", "Lraw", "L", "cum", "a", "o", "o_out"))
        xa0 = Cross("xa0", xqT, xkT, kv_tok[:, :, XAW:2 * XAW], mix, SBW, xtmp)
        op0 = OutProjection("op0", mix, [aslot(N0 - 2, 512), aslot(N0 - 1, 512)], lambda pe, half: weights_in(pe, N0 - 2 + half))
        v_tok = proj[:, :, 2 * SBW:3 * SBW]

        with nc.Block() as block:
            @block.tensor
            def _(pe):
                pe.wait_ge(s_const2, 5)
                for i in range(SBH + 2):
                    if i < SBH:
                        z = PS[:, i % 3, :]
                        if i >= 3:
                            pe.wait_ge(s_a, i - 2)
                        pe.matmul(z[:, 0:S], kT[:, i, 0:P], qT[:, i, :], start=True, stop=True, skip_group_check=True)
                        pe.matmul(z[:, S:S + P], kT[:, i, P:S], qT[:, i, P:S], start=False, stop=True,
                                  skip_group_check=True).then_inc(s_z, 1)
                    if 1 <= i <= SBH:
                        j = i - 1
                        z, L = PS[:, j % 3, :], hL[:, j % 2, :]
                        pe.wait_ge(s_L, j + 1)
                        for o, w, r in ((z[:, 0:S], negup, L[:, 0:S]), (z[:, P:S], negones, L[:, S:S + P]),
                                        (z[:, S:S + P], negup, L[:, S:S + P]), (z[:, 0:P], ident[:], diagneg),
                                        (z[:, S:S + P], ident[:], diagneg)):
                            mm = pe.matmul(o, w, r, start=False, stop=True, skip_group_check=True)
                        mm.then_inc(s_cum, 1)
                    if i >= 2:
                        j = i - 2
                        pe.wait_ge(s_a, j + 1)
                        if j >= 2:
                            pe.wait_ge(s_oe, j - 1)
                        o, A = PS[:, 3 + j % 2, :], hA[:, j % 2, :]
                        vh = slice(j * HD, (j + 1) * HD)
                        pe.matmul(o[:, 0:HD], A[:, 0:P], v_tok[:, 0, vh], start=True, stop=True)
                        pe.matmul(o[:, HD:2 * HD], A[:, P:S], v_tok[:, 0, vh], start=True, stop=False)
                        pe.matmul(o[:, HD:2 * HD], A[:, S:S + P], v_tok[:, 1, vh], start=False, stop=True).then_inc(s_o, 1)
                xa0.pe(pe, lambda e: (e.wait_ge(s_a, SBH), e.wait_ge(s_oe, SBH)))
                op0.pe(pe, lambda e: (e.wait_ge(xa0.s_mix, 2 * XAH), e.wait_ge(s_oe, SBH)))

            @block.scalar
            def _(act):
                for i in range(SBH + 1):
                    if i < SBH:
                        act.wait_ge(s_z, i + 1)
                        if i >= 2:
                            act.wait_ge(s_Lr, i - 1)
                        act.activation(habs[:, i % 2, :], PS[:, i % 3, 0:384], ACT.Abs).then_inc(s_ab, 1)
                        act.wait_ge(s_ab, i + 1)
                        act.activation(habs[:, i % 2, :], habs[:, i % 2, :], ACT.Exp, scale=-1.0).then_inc(s_ex, 1)
                        act.wait_ge(s_ex, i + 1)
                        act.activation(hln[:, i % 2, :], habs[:, i % 2, :], ACT.Ln, bias=1.0).then_inc(s_ln, 1)
                    if i >= 1:
                        j = i - 1
                        act.wait_ge(s_cum, j + 1)
                        if j >= 2:
                            act.wait_ge(s_o, j - 1)
                        act.activation(hA[:, j % 2, :], PS[:, j % 3, 0:384], ACT.Exp).then_inc(s_a, 1)
                xa0.act(act)
                op0.act(act)

            @block.vector
            def _(dve):
                for i in range(SBH + 2):
                    if i < SBH:
                        dve.wait_ge(s_ln, i + 1)
                        if i >= 2:
                            dve.wait_ge(s_cum, i - 1)
                        dve.scalar_tensor_tensor(out=hL[:, i % 2, :], in0=PS[:, i % 3, 0:384], scalar=0.0, in1=hln[:, i % 2, :],
                                                 op0=ALU.max, op1=ALU.add).then_inc(s_Lr, 1)
                        dve.wait_ge(s_Lr, i + 1)
                        dve.tensor_tensor(hL[:, i % 2, :], hL[:, i % 2, :], diag0.rearrange("p a b -> p (a b)"),
                                          ALU.mult).then_inc(s_L, 1)
                    if i >= 2:
                        j = i - 2
                        dve.wait_ge(s_o, j + 1)
                        dve.tensor_copy(mix[:, :, j * HD:(j + 1) * HD],
                                        PS[:, 3 + j % 2, 0:2 * HD].rearrange("p (t d) -> p t d", t=NT)).then_inc(s_oe, 1)
                xa0.dve(dve)
                op0.dve(dve)

            @block.sync
            def _(sp):
                sp.dma_start(gain[:, 0, :], row(ffn_norm[0], D)).then_inc(s_gain_ffn0, 16)

        s_w = [sem(f"s_w{i}") for i in range(SLOTS)]
        NB = GF // P

        def slot_views(s):
            v = ring[:, s * SLOT:(s + 1) * SLOT]
            n = KC * GF
            return (v[:, 0:n].rearrange("p (c f) -> p c f", c=KC), v[:, n:2 * n].rearrange("p (c f) -> p c f", c=KC),
                    v[:, 2 * n:SLOT].rearrange("p (b d) -> p b d", b=NB))

        def load_group(sp, s, wg, wu, wd, g):
            vg, vu, vd = slot_views(s)
            sp.dma_start(vg, k_rows(wg)[:, :, g * GF:(g + 1) * GF]).then_inc(s_w[s], 16)
            sp.dma_start(vu, k_rows(wu)[:, :, g * GF:(g + 1) * GF]).then_inc(s_w[s], 16)
            sp.dma_start(vd, wd.rearrange("(g b p) d -> g p b d", b=NB, p=P)[g]).then_inc(s_w[s], 16)

        norm_c = NormTranspose("nc", [(X[:, t, :], gain[:, 0, :], hT[:, :, t * P:(t + 1) * P], (op0.s_x, 4)) for t in range(NT)])
        sgb = xn[:, 0, 0:2 * S].rearrange("p (b t) -> p b t", b=2)
        hb = xn[:, 1, 0:2 * S].rearrange("p (b t) -> p b t", b=2)
        s_gu, s_sg, s_h, s_dn, s_xc = lsem("c_gu"), lsem("c_silu"), lsem("c_h"), lsem("c_down"), lsem("c_x")
        NBLK = NG * NB

        with nc.Block() as block:
            @block.sync
            def _(sp):
                sp.dma_start(gain[:, 1, :], row(mem_norm[1], D)).then_inc(s_gain_mem1, 16)
                for g in range(NG):
                    if g >= SLOTS:
                        sp.wait_ge(s_dn, NB * (g - SLOTS + 1))
                    load_group(sp, g % SLOTS, ffd_w_gate[0], ffd_w_up[0], ffd_w_down[0], g)

            @block.scalar
            def _(act):
                link = linker(act, "act")
                norm_c.act_squares(act, link)
                norm_c.act_rstd(act, link)
                norm_c.act_evacuate(act)
                for n in range(NBLK):
                    act.wait_ge(s_gu, n + 1)
                    if n >= 2:
                        act.wait_ge(s_h, n - 1)
                    act.activation(sgb[:, n % 2, :], PS[:, 2 + n % 2, 0:S], ACT.Silu).then_inc(s_sg, 1)

            @block.vector
            def _(dve):
                dve.wait_ge(s_gain_ffn0, 16)
                norm_c.dve_rows(dve)
                for n in range(NBLK):
                    dve.wait_ge(s_sg, n + 1)
                    if n >= 2:
                        dve.wait_ge(s_dn, n - 1)
                    dve.tensor_tensor(hb[:, n % 2, :], sgb[:, n % 2, :], PS[:, 2 + n % 2, S:2 * S], ALU.mult).then_inc(s_h, 1)
                dve.wait_ge(s_dn, NBLK)
                for t in range(NT):
                    xv = X[:, t, :].rearrange("p (a n) -> p a n", a=2)
                    dve.tensor_tensor(xv, xv, PS[:, 4 + 2 * t:6 + 2 * t, :], ALU.add).then_inc(s_xc, 1)

            @block.tensor
            def _(pe):
                norm_c.pe(pe)
                norm_c.ready(pe, NT)
                for n in range(NBLK + 1):
                    if n < NBLK:
                        g, b = n // NB, n % NB
                        vg, vu, _ = slot_views(g % SLOTS)
                        if b == 0:
                            pe.wait_ge(s_w[g % SLOTS], 48 * (g // SLOTS + 1))
                        if n >= 2:
                            pe.wait_ge(s_h, n - 1)
                        for w, c0 in ((vg, 0), (vu, S)):
                            for k in range(KC):
                                mm = pe.matmul(PS[:, 2 + n % 2, c0:c0 + S], w[:, k, b * P:(b + 1) * P], hT[:, k, :],
                                               start=(k == 0), stop=(k == KC - 1))
                        mm.then_inc(s_gu, 1)
                    if n >= 1:
                        m = n - 1
                        g, b = m // NB, m % NB
                        vd = slot_views(g % SLOTS)[2]
                        pe.wait_ge(s_h, m + 1)
                        for t in range(NT):
                            for half in range(2):
                                mm = pe.matmul(PS[:, 4 + 2 * t + half, :], hb[:, m % 2, t * P:(t + 1) * P],
                                               vd[:, b, half * 512:(half + 1) * 512], start=(m == 0), stop=(m == NBLK - 1))
                        mm.then_inc(s_dn, 1)

        next_layer()
        NCH = 3 * DNW // P
        CT_ = 4
        NP_ = NT * DNH
        sd = Scratch()
        qkvT = sd.tile(P, NCH, S)
        gate = sd.tile(P, NT, DNW)
        last = sd.tile(P, NT, 2 * DNH + XAW)
        kv1 = sd.tile(P, NT, 2 * XAW)
        xqT1 = sd.tile(HD, XAH, S)
        xkT1 = sd.tile(HD, XAH, S)
        mix1 = sd.tile(P, NT, D)
        convr = sd.tile(CT_ * NCH, P)
        convw = sd.tile(P, CT_ * NCH)
        alog = sd.tile(P, DNH)
        dtb = sd.tile(P, DNH)
        ogain = sd.tile(P, P)
        gcol1 = sd.tile(HD, 4)
        lowstrict = sd.tile(P, P)
        mask1 = sd.tile(P, P)
        SOLVE = 7
        maskT = sd.tile(P, SOLVE, P)
        tk = sd.tile(P, 12, NP_)
        on = sd.tile(P, 3, NP_)
        xtmp1 = (sd.tile(P, 2, S), sd.tile(P, 2, S), sd.tile(P, 3, 8))
        xst1 = sd.tile(P, 2, NT * 2 * XAH)
        e_at = sd.at
        memr1 = sd.tile(P, NT, D)
        memT1 = sd.tile(P, KC, S)
        yconv = sd.tile(P, 2, S)

        norm_d = NormTranspose("nd", [
            (memr1[:, 0, :], gain[:, 1, :], memT1[:, :, 0:P], None),
            (memr1[:, 1, :], gain[:, 1, :], memT1[:, :, P:S], None),
            (X[:, 0, :], gain[:, 0, :], hT[:, :, 0:P], None),
            (X[:, 1, :], gain[:, 0, :], hT[:, :, P:S], None)])
        s_mem1, s_small = lsem("s_mem1"), lsem("s_small")
        norm_d.units = [(a, b, c, (s_mem1, 16)) for i, (a, b, c, _) in enumerate(norm_d.units)]
        s_cwt, s_cw, s_cv, s_y0, s_y1, s_y2, s_yc, s_si, s_tok, s_toke, s_mask = (
            lsem(f"d_{n}") for n in ("cwt", "cw", "cv", "y0", "y1", "y2", "y", "silu", "tok", "tok_out", "mask"))
        jobs_d = [(memT1, N0, t, kv1[:, t, :], 512, ACT.Copy) for t in range(NT)] + \
                 [(hT, N0 + 7 + c, t, gate[:, t, c * QK:(c + 1) * QK], QK, ACT.Silu) for c in range(2) for t in range(NT)] + \
                 [(hT, N0 + 9, t, last[:, t, :], DN_IN - 4 * DNW, ACT.Copy) for t in range(NT)]
        NTJ = len(jobs_d)
        CPL = QK // P
        op1 = OutProjection("op1", mix1, [aslot(len(loads) - 2, 512), aslot(len(loads) - 1, 512)],
                            lambda pe, half: weights_in(pe, len(loads) - 2 + half))
        load_read[N0 - ASLOTS:] = [None] * (N0 - len(load_read[:N0 - ASLOTS]))
        load_read += [(s_tok, NT)] + \
                     [(s_cv, CPL * (i + 1)) for i in range(6)] + [(s_tok, NT * (i + 2)) for i in range(3)]

        with nc.Block() as block:
            @block.sync
            def _(sp):
                sp.dma_start(memr1, mem[0].rearrange("(t p) d -> p t d", p=P)).then_inc(s_mem1, 16)
                sp.dma_start(gain[:, 0, :], row(mix_norm[1], D)).then_inc(s_gain_mix1, 16)
                sp.dma_start(convr, dn_conv[0].rearrange("j (c p) -> (j c) p", p=P)).then_inc(s_small, 16)
                sp.dma_start(alog, row(dn_a_log[0], DNH)).then_inc(s_small, 16)
                sp.dma_start(dtb, row(dn_dt_bias[0], DNH)).then_inc(s_small, 16)
                sp.dma_start(ogain, row(dn_o_norm[0], P)).then_inc(s_small, 16)
                for i, g in enumerate((xa_q_norm[1], xa_k_norm[1])):
                    sp.dma_start(gcol1[:, i:i + 1], col(g)).then_inc(s_small, 16)
                attention_loads(sp, N0, len(loads), N0)

            @block.gpsimd
            def _(pool):
                link = linker(pool, "pool")
                pool.affine_select(out=lowstrict, in_=ones[:], compare_op=ALU.is_gt, fill=0.0, base=0,
                                   pattern=[[-1, P]], channel_multiplier=1).then_inc(s_mask, 1)
                link(pool.memset(maskT.rearrange("p a b -> p (a b)"), 0.0))
                link(pool.memset(mask1, 0.0))
                pool.affine_select(out=mask1.rearrange("p (a h) -> p a h", h=2)[:, :, 0], in_=mask1.rearrange("p (a h) -> p a h", h=2)[:, :, 0],
                                   compare_op=ALU.not_equal, fill=1.0, base=-1, pattern=[[-2, P // 2]],
                                   channel_multiplier=1).then_inc(s_mask, 1)
                for i in range(SOLVE):
                    s = 1 << i
                    v = maskT[:, i, :].rearrange("p (a h b) -> p a h b", h=2, b=s)[:, :, 1, :]
                    link(pool.memset(v, 1.0))
                    link(pool.affine_select(out=v, in_=v, compare_op=ALU.is_ge, fill=0.0, base=0,
                                            pattern=[[-2 * s, P // (2 * s)], [0, s]], channel_multiplier=1))
                    pool.affine_select(out=v, in_=v, compare_op=ALU.is_ge, fill=0.0, base=s - 1,
                                       pattern=[[2 * s, P // (2 * s)], [0, s]], channel_multiplier=-1).then_inc(s_mask, 1)

            @block.scalar
            def _(act):
                link = linker(act, "act")
                act.preload_act_table_set("natural_log_exp_and_others")
                norm_d.act_squares(act, link)
                norm_d.act_rstd(act, link)
                norm_d.act_evacuate(act)

                def token_job(n):
                    rows, load, t, dst, cols, f = jobs_d[n]
                    act.wait_ge(s_tok, n + 1)
                    act.activation(dst, PS[:, 5 + n % 3, 0:cols], f).then_inc(s_toke, 1)

                for n in range(NT):
                    token_job(n)
                for c in range(NCH):
                    act.wait_ge(s_yc, c + 1)
                    act.activation(qkvT[:, c, :], yconv[:, c % 2, :], ACT.Silu).then_inc(s_si, 1)
                for n in range(NT, NTJ):
                    token_job(n)

            @block.vector
            def _(dve):
                dve.wait_ge(s_gain_mem1, 16)
                dve.wait_ge(s_gain_mix1, 16)
                norm_d.dve_rows(dve)
                dve.wait_ge(s_cwt, 1)
                dve.tensor_copy(convw, PS[:, 7, 0:CT_ * NCH]).then_inc(s_cw, 1)
                dve.wait_ge(s_cw, 1)
                for c in range(NCH):
                    dve.wait_ge(s_cv, c + 1)
                    if c >= 2:
                        dve.wait_ge(s_si, c - 1)
                    xp, y = PS[:, 2 + c % 3, 0:S], yconv[:, c % 2, :]

                    def tap(j):
                        return convw[:, j * NCH + c:j * NCH + c + 1]
                    dve.tensor_scalar(y, xp, tap(3), None, ALU.mult).then_inc(s_y0, 1)
                    for back, before, after in ((1, s_y0, s_y1), (2, s_y1, s_y2), (3, s_y2, s_yc)):
                        dve.wait_ge(before, c + 1)
                        dve.scalar_tensor_tensor(out=y[:, back:S], in0=xp[:, 0:S - back], scalar=tap(3 - back),
                                                 in1=y[:, back:S], op0=ALU.mult, op1=ALU.add).then_inc(after, 1)

            @block.tensor
            def _(pe):
                norm_d.pe(pe)
                pe.wait_ge(s_small, 96)
                pe.transpose(PS[:, 7, 0:CT_ * NCH], convr, ident[0:CT_ * NCH, 0:CT_ * NCH]).then_inc(s_cwt, 1)

                def token_job(n):
                    rows, load, t, dst, cols, f = jobs_d[n]
                    w = weights_in(pe, load)
                    if n == 2:
                        pe.wait_ge(s_cw, 1)
                    if n >= 3:
                        pe.wait_ge(s_toke, n - 2)
                    for k in range(KC):
                        mm = pe.matmul(PS[:, 5 + n % 3, 0:cols], rows[:, k, t * P:(t + 1) * P], w[:, k, :],
                                       start=(k == 0), stop=(k == KC - 1))
                    mm.then_inc(s_tok, 1)

                norm_d.ready(pe, 4)
                for n in range(NT):
                    token_job(n)
                for c in range(NCH):
                    w = weights_in(pe, N0 + 1 + c // CPL)
                    if c >= 3:
                        pe.wait_ge(s_yc, c - 2)
                    for k in range(KC):
                        mm = pe.matmul(PS[:, 2 + c % 3, 0:S], w[:, k, (c % CPL) * P:(c % CPL + 1) * P], hT[:, k, :],
                                       start=(k == 0), stop=(k == KC - 1))
                    mm.then_inc(s_cv, 1)
                for n in range(NT, NTJ):
                    token_job(n)

        sd.at = e_at
        vb = sd.tile(P, NP_, P)
        kdec = sd.tile(P, DNH, P)
        nkbg = sd.tile(P, DNH, P)
        qd = sd.tile(P, DNH, P)
        Dm = sd.tile(P, NP_, P)
        DT = sd.tile(P, NP_, P)
        A = sd.tile(P, NP_, P)
        AT = sd.tile(P, NP_, P)
        T = sd.tile(P, NP_, P)
        TT = sd.tile(P, NP_, P)
        W = Dm
        rg = T
        sq2 = TT.rearrange("p a b -> p (a b)")[:, 0:4 * S].rearrange("p (i a b) -> p i a b", i=2, a=2)
        CT = [qkvT[:, 2 * DNH:3 * DNH, :].rearrange("p c (t n) -> p (c t) n", n=P), A]
        U0, St = T[:, 0:DNH, :], T[:, DNH:NP_, :]
        wT, V1, Osb, Osq = W[:, 0:DNH, :], A[:, 0:DNH, :], AT, T
        sqx1 = vb.rearrange("p a b -> p (a b)")[:, 0:NT * 2 * XAW].rearrange("p (t n) -> p t n", t=NT)
        cross1 = CrossPrep("cp1", last[:, :, 2 * DNH:], kv1, xqT1, xkT1, sqx1, xst1, gcol1[:, 2:3], gcol1[:, 1:2], (6, 7, 6, 7))
        xa1 = Cross("xa1", xqT1, xkT1, kv1[:, :, XAW:2 * XAW], mix1, DNW, xtmp1)
        PQ = 4
        NQ = NP_ // PQ
        e = {n: lsem(f"e_{n}") for n in (
            "g8", "xa", "abs", "exp", "ln", "alog", "eb", "g", "beta", "rg", "gc", "gcs", "egc", "kdarg", "kd", "nb",
            "G", "Darg", "Dexp", "egr", "Dmask", "DTmask", "sq", "sum", "lnr", "r", "qn", "kn", "qd",
            "tr", "vb", "kt", "KK", "KQ", "A", "qk", "At", "AT", "T0", "TT0", "CT", "W", "We", "PP", "Tn", "TTn",
            "U", "Ue", "S", "Se", "wT", "wTe", "V", "Ve", "O", "Oe", "osq", "oms", "ors", "gg", "o1", "mix")}

        def banks4(b):
            return PS[:, b, :].rearrange("p (a n) -> p a n", a=PQ)

        def trio(v, q):
            return v[:, q * PQ:(q + 1) * PQ, :]

        with nc.Block() as block:
            @block.scalar
            def _(act):
                link = linker(act, "act")
                act.preload_act_table_set("natural_log_exp_and_others")
                act.wait_ge(e["xa"], 1)
                act.activation(tk[:, 1, :], tk[:, 0, :], ACT.Abs).then_inc(e["abs"], 1)
                act.wait_ge(e["abs"], 1)
                act.activation(tk[:, 1, :], tk[:, 1, :], ACT.Exp, scale=-1.0).then_inc(e["exp"], 1)
                act.wait_ge(e["exp"], 1)
                act.activation(tk[:, 1, :], tk[:, 1, :], ACT.Ln, bias=1.0).then_inc(e["ln"], 1)
                act.activation(alog, alog, ACT.Exp).then_inc(e["alog"], 1)
                act.activation(tk[:, 3, :].rearrange("p (t h) -> p t h", t=NT), last[:, :, DNH:2 * DNH], ACT.Exp,
                               scale=-1.0).then_inc(e["eb"], 1)
                for h in range(DNH):
                    if h >= 2:
                        act.wait_ge(e["kn"], h - 1)
                    act.activation(sq2[:, h % 2], qkvT[:, h:h + DNH + 1:DNH, :], ACT.Square).then_inc(e["sq"], 1)
                    act.wait_ge(e["sum"], h + 1)
                    act.activation(sq2[:, h % 2], PS[:, 3 + h % 2, :].rearrange("p (a b) -> p a b", a=2), ACT.Ln,
                                   bias=epsc[:]).then_inc(e["lnr"], 1)
                    act.wait_ge(e["lnr"], h + 1)
                    act.activation(sq2[:, h % 2], sq2[:, h % 2], ACT.Exp, scale=-0.5).then_inc(e["r"], 1)
                act.wait_ge(e["gcs"], 1)
                act.activation(tk[:, 6, :], tk[:, 5, :], ACT.Exp).then_inc(e["egc"], 1)
                act.wait_ge(e["kdarg"], 1)
                act.activation(tk[:, 8, :], tk[:, 8, :], ACT.Exp).then_inc(e["kd"], 1)
                act.wait_ge(e["Darg"], 2 * NP_)
                act.activation(DT, DT, ACT.Exp).then_inc(e["Dexp"], 1)
                act.activation(Dm, Dm, ACT.Exp, scale=-1.0).then_inc(e["Dexp"], 1)
                act.activation(qd[:, 0:2, :], banks4(1)[:, 2:4, :], ACT.Exp).then_inc(e["egr"], 1)
                act.activation(qd[:, 2:6, :], banks4(2), ACT.Exp).then_inc(e["egr"], 1)
                for q in range(NQ):
                    act.wait_ge(e["tr"], q + 1)
                    if q == 0:
                        act.wait_ge(e["beta"], 1)
                    for i in range(PQ):
                        p = q * PQ + i
                        act.activation(vb[:, p, :], banks4(5 + q)[:, i, :], ACT.Copy, scale=tk[:, 4, p:p + 1]).then_inc(e["vb"], 1)
                for q in range(NQ):
                    act.wait_ge(e["At"], q + 1)
                    act.activation(trio(AT, q), banks4(5 + q), ACT.Copy).then_inc(e["AT"], 1)
                for j in range((SOLVE - 1) * NQ):
                    act.wait_ge(e["W"], j + 1)
                    act.activation(trio(W, j % NQ), banks4(j % 2), ACT.Copy).then_inc(e["We"], 1)
                act.wait_ge(e["U"], 1)
                act.activation(U0[:, 0:4, :], banks4(0), ACT.Copy).then_inc(e["Ue"], 1)
                act.activation(U0[:, 4:6, :], banks4(1)[:, 0:2, :], ACT.Copy).then_inc(e["Ue"], 1)
                act.wait_ge(e["S"], 1)
                act.activation(St[:, 0:4, :], banks4(4), ACT.Copy).then_inc(e["Se"], 1)
                act.activation(St[:, 4:6, :], banks4(5)[:, 0:2, :], ACT.Copy).then_inc(e["Se"], 1)
                act.wait_ge(e["V"], 1)
                act.activation(V1[:, 0:4, :], banks4(0), ACT.Copy).then_inc(e["Ve"], 1)
                act.activation(V1[:, 4:6, :], banks4(1)[:, 0:2, :], ACT.Copy).then_inc(e["Ve"], 1)
                for t, b in ((0, 6), (1, 2)):
                    act.wait_ge(e["O"], t + 1)
                    act.activation(Osb[:, t * DNH:t * DNH + 4, :], banks4(b), ACT.Copy).then_inc(e["Oe"], 1)
                    act.activation(Osb[:, t * DNH + 4:t * DNH + 6, :], banks4(b + 1)[:, 0:2, :], ACT.Copy).then_inc(e["Oe"], 1)
                act.wait_ge(e["Oe"], 4)
                act.activation(Osq, Osb, ACT.Square).then_inc(e["osq"], 1)
                act.wait_ge(e["oms"], 1)
                link(act.activation(on[:, 1, :], on[:, 1, :], ACT.Ln))
                act.activation(on[:, 1, :], on[:, 1, :], ACT.Exp, scale=-0.5).then_inc(e["ors"], 1)
                cross1.act(act, link, lambda eng: eng.wait_ge(s_toke, NTJ))
                act.wait_ge(e["g8"], 1)
                cross1.act_evacuate(act)
                xa1.act(act)
                op1.act(act)

            @block.gpsimd
            def _(pool):
                pool.wait_ge(e["Dexp"], 2)
                pool.tensor_tensor(DT, DT, upincl[:].unsqueeze(1).to_broadcast([P, NP_, P]), ALU.mult).then_inc(e["DTmask"], 1)
                gv = gate.rearrange("p t (h d) -> p (t h) d", d=P)
                pool.tensor_tensor(gv, gv, ogain.unsqueeze(1).to_broadcast([P, NP_, P]), ALU.mult).then_inc(e["gg"], 1)
                pool.wait_ge(e["vb"], NP_)
                for i in range(1, SOLVE):
                    pool.wait_ge(e["AT"], NQ)
                    if i == 2:
                        pool.wait_ge(e["T0"], 1)
                    if i >= 3:
                        pool.wait_ge(e["W"], NQ * (i - 2))
                    pool.tensor_tensor(CT[(i - 1) % 2], AT, maskT[:, i, :].unsqueeze(1).to_broadcast([P, NP_, P]),
                                       ALU.mult).then_inc(e["CT"], 1)

            @block.vector
            def _(dve):
                link = linker(dve, "dve")

                def th(v):
                    return v.rearrange("p (t h) -> p t h", t=NT)

                dve.tensor_scalar(gcol1[:, 2:3], gcol1[:, 0:1], HD ** -0.5, None, ALU.mult).then_inc(e["g8"], 1)
                dve.tensor_tensor(th(tk[:, 0, :]), last[:, :, 0:DNH], dtb.unsqueeze(1).to_broadcast([P, NT, DNH]), ALU.add).then_inc(e["xa"], 1)
                dve.wait_ge(e["ln"], 1)
                link(dve.scalar_tensor_tensor(out=tk[:, 2, :], in0=tk[:, 0, :], scalar=0.0, in1=tk[:, 1, :], op0=ALU.max, op1=ALU.add))
                dve.wait_ge(e["alog"], 1)
                dve.scalar_tensor_tensor(out=th(tk[:, 2, :]), in0=th(tk[:, 2, :]), scalar=-1.0,
                                         in1=alog.unsqueeze(1).to_broadcast([P, NT, DNH]), op0=ALU.mult, op1=ALU.mult).then_inc(e["g"], 1)
                dve.wait_ge(e["eb"], 1)
                link(dve.tensor_scalar(tk[:, 3, :], tk[:, 3, :], 1.0, None, ALU.add))
                dve.reciprocal(tk[:, 4, :], tk[:, 3, :]).then_inc(e["beta"], 1)
                dve.wait_ge(e["g"], 1)
                for p in range(NP_):
                    dve.tensor_scalar(rg[:, p, :], upincl[:], tk[:, 2, p:p + 1], None, ALU.mult).then_inc(e["rg"], 1)
                dve.wait_ge(e["gc"], 1)
                dve.tensor_copy(tk[:, 5:8:2, :], PS[:, 7, 0:2 * NP_].rearrange("p (a n) -> p a n", a=2)).then_inc(e["gcs"], 1)
                dve.wait_ge(e["gcs"], 1)
                dve.tensor_tensor(tk[:, 8, :], tk[:, 7, :], tk[:, 5, :], ALU.subtract).then_inc(e["kdarg"], 1)
                for p in range(NP_):
                    if p % PQ == 0:
                        dve.wait_ge(e["G"], p // PQ + 1)
                    gp = banks4(p // PQ)[:, p % PQ, :]
                    dve.tensor_scalar(DT[:, p, :], gp, tk[:, 5, p:p + 1], 0.0, ALU.subtract, ALU.min).then_inc(e["Darg"], 1)
                    dve.tensor_scalar(Dm[:, p, :], gp, tk[:, 5, p:p + 1], 0.0, ALU.subtract, ALU.max).then_inc(e["Darg"], 1)
                for h in range(DNH):
                    dve.wait_ge(e["r"], h + 1)
                    dve.scalar_tensor_tensor(out=qkvT[:, h, :], in0=qkvT[:, h, :], scalar=float(P) ** -0.5, in1=sq2[:, h % 2, 0, :],
                                             op0=ALU.mult, op1=ALU.mult).then_inc(e["qn"], 1)
                    kk = qkvT[:, DNH + h, :]
                    dve.tensor_tensor(kk, kk, sq2[:, h % 2, 1, :], ALU.mult).then_inc(e["kn"], 1)
                dve.wait_ge(e["egc"], 1)
                dve.wait_ge(e["beta"], 1)
                dve.scalar_tensor_tensor(out=tk[:, 9, :], in0=tk[:, 6, :], scalar=-1.0, in1=tk[:, 4, :],
                                         op0=ALU.mult, op1=ALU.mult).then_inc(e["nb"], 1)
                dve.wait_ge(e["Dexp"], 2)
                dve.tensor_tensor(Dm, Dm, lowstrict.unsqueeze(1).to_broadcast([P, NP_, P]), ALU.mult).then_inc(e["Dmask"], 1)
                dve.wait_ge(e["egr"], 2)
                dve.wait_ge(e["qn"], DNH)
                dve.tensor_tensor(qd, qd, qkvT[:, 0:DNH, P:S], ALU.mult).then_inc(e["qd"], 1)
                dve.wait_ge(e["kd"], 1)
                dve.wait_ge(e["nb"], 1)
                for q in range(NQ):
                    dve.wait_ge(e["tr"], NQ + q + 1)
                    for i in range(PQ):
                        p = q * PQ + i
                        src = banks4((3, 4, 0)[q])[:, i, :]
                        if p < DNH:
                            dve.tensor_scalar(kdec[:, p, :], src, tk[:, 8, p:p + 1], None, ALU.mult).then_inc(e["kt"], 1)
                        else:
                            dve.tensor_scalar(nkbg[:, p - DNH, :], src, tk[:, 9, p:p + 1], None, ALU.mult).then_inc(e["kt"], 1)
                dve.wait_ge(e["Dmask"], 1)
                for q in range(NQ):
                    dve.wait_ge(e["KK"], q + 1)
                    for i in range(PQ):
                        p = q * PQ + i
                        dve.scalar_tensor_tensor(out=A[:, p, :], in0=banks4(1 + q)[:, i, :], scalar=tk[:, 4, p:p + 1],
                                                 in1=Dm[:, p, :], op0=ALU.mult, op1=ALU.mult).then_inc(e["A"], 1)
                dve.wait_ge(e["DTmask"], 1)
                for q in range(NQ):
                    dve.wait_ge(e["KQ"], q + 1)
                    dve.tensor_tensor(trio(DT, q), trio(DT, q), banks4((4, 0, 1)[q]), ALU.mult).then_inc(e["qk"], 1)
                dve.wait_ge(s_mask, 2 + SOLVE)
                dve.wait_ge(e["A"], NP_)
                idb = ident[:].unsqueeze(1).to_broadcast([P, NP_, P])
                link(dve.tensor_tensor(T, A, mask1.unsqueeze(1).to_broadcast([P, NP_, P]), ALU.mult))
                dve.tensor_tensor(T, idb, T, ALU.subtract).then_inc(e["T0"], 1)
                dve.wait_ge(e["AT"], NQ)
                link(dve.tensor_tensor(TT, AT, maskT[:, 0, :].unsqueeze(1).to_broadcast([P, NP_, P]), ALU.mult))
                dve.tensor_tensor(TT, idb, TT, ALU.subtract).then_inc(e["TT0"], 1)
                dve.wait_ge(e["T0"], 1)
                dve.wait_ge(e["TT0"], 1)
                for j in range((SOLVE - 1) * NQ):
                    q = j % NQ
                    dve.wait_ge(e["PP"], j + 1)
                    if j < (SOLVE - 2) * NQ:
                        dve.tensor_tensor(trio(T, q), trio(T, q), banks4(2 + q), ALU.subtract).then_inc(e["Tn"], 1)
                    dve.tensor_tensor(trio(TT, q), trio(TT, q), banks4(5 + q), ALU.subtract).then_inc(e["TTn"], 1)
                    if q == NQ - 1:
                        dve.wait_ge(e["TTn"], j + 1)
                        if j < (SOLVE - 2) * NQ:
                            dve.wait_ge(e["Tn"], j + 1)
                dve.wait_ge(e["wT"], 1)
                dve.tensor_copy(wT[:, 0:4, :], banks4(2)).then_inc(e["wTe"], 1)
                dve.tensor_copy(wT[:, 4:6, :], banks4(3)[:, 0:2, :]).then_inc(e["wTe"], 1)
                dve.wait_ge(e["osq"], 1)
                link(dve.tensor_reduce(on[:, 0, :], Osq, X_AXIS, ALU.add))
                dve.tensor_scalar(on[:, 1, :], on[:, 0, :], 1.0 / P, EPS, ALU.mult, ALU.add).then_inc(e["oms"], 1)
                dve.wait_ge(e["ors"], 1)
                dve.tensor_tensor(Osb, Osb, on[:, 1, :].unsqueeze(2).to_broadcast([P, NP_, P]), ALU.mult).then_inc(e["o1"], 1)
                dve.wait_ge(e["o1"], 1)
                dve.wait_ge(e["gg"], 1)
                for t in range(NT):
                    dve.tensor_tensor(mix1[:, t, 0:DNW].rearrange("p (h d) -> p h d", d=P), Osb[:, t * DNH:(t + 1) * DNH, :],
                                      gate[:, t, :].rearrange("p (h d) -> p h d", d=P), ALU.mult).then_inc(e["mix"], 1)
                cross1.dve(dve, link, lambda eng: eng.wait_ge(s_toke, NTJ))
                xa1.dve(dve)
                op1.dve(dve)

            @block.tensor
            def _(pe):
                pe.wait_ge(e["g"], 1)
                pe.matmul(PS[:, 7, 0:NP_], upincl[:], tk[:, 2, :], start=True, stop=True)
                pe.matmul(PS[:, 7, NP_:2 * NP_], ones[:], tk[:, 2, :], start=True, stop=True).then_inc(e["gc"], 1)
                for q in range(NQ):
                    pe.wait_ge(e["rg"], PQ * (q + 1))
                    pe.matmul(PS[:, q, :], ones[:], trio(rg, q), start=True, stop=True).then_inc(e["G"], 1)
                for h in range(DNH):
                    pe.wait_ge(e["sq"], h + 1)
                    if h >= 2:
                        pe.wait_ge(e["r"], h - 1)
                    pe.matmul(PS[:, 3 + h % 2, :], ones[:], sq2[:, h % 2], start=True, stop=True).then_inc(e["sum"], 1)
                pe.wait_ge(e["gcs"], 1)
                for q in range(NQ):
                    for i in range(PQ):
                        t, h = divmod(q * PQ + i, DNH)
                        mm = pe.transpose(banks4(5 + q)[:, i, :], qkvT[:, 2 * DNH + h, t * P:(t + 1) * P], ident[:])
                    mm.then_inc(e["tr"], 1)
                pe.wait_ge(e["kn"], DNH)
                pe.wait_ge(e["qn"], DNH)
                pe.wait_ge(e["Darg"], 2 * NP_)
                pe.wait_ge(e["egr"], 2)
                for q in range(NQ):
                    for i in range(PQ):
                        t, h = divmod(q * PQ + i, DNH)
                        mm = pe.transpose(banks4((3, 4, 0)[q])[:, i, :], qkvT[:, DNH + h, t * P:(t + 1) * P], ident[:])
                    mm.then_inc(e["tr"], 1)

                def products(b, other):
                    for i in range(PQ):
                        t, h = divmod(q * PQ + i, DNH)
                        kk = qkvT[:, DNH + h, t * P:(t + 1) * P]
                        mm = pe.matmul(banks4(b)[:, i, :], kk, qkvT[:, other + h, t * P:(t + 1) * P], start=True, stop=True)
                    return mm

                for q in range(NQ):
                    if q == 2:
                        pe.wait_ge(e["kt"], PQ)
                    products(1 + q, DNH).then_inc(e["KK"], 1)
                for q in range(NQ):
                    pe.wait_ge(e["kt"], (2 * PQ, 3 * PQ, 3 * PQ)[q])
                    if q == 2:
                        pe.wait_ge(e["A"], PQ)
                    products((4, 0, 1)[q], 0).then_inc(e["KQ"], 1)
                for q in range(NQ):
                    pe.wait_ge(e["A"], PQ * (q + 1))
                    pe.wait_ge(e["vb"], PQ * (q + 1))
                    for i in range(PQ):
                        mm = pe.transpose(banks4(5 + q)[:, i, :], A[:, q * PQ + i, :], ident[:])
                    mm.then_inc(e["At"], 1)
                pe.wait_ge(e["qk"], NQ)
                pe.wait_ge(e["T0"], 1)
                pe.wait_ge(e["TT0"], 1)

                def first(j):
                    i, q = divmod(j, NQ)
                    pe.wait_ge(e["CT"], i + 1)
                    if i >= 1:
                        pe.wait_ge(e["Tn"], (i - 1) * NQ + q + 1)
                        pe.wait_ge(e["TTn"], (i - 1) * NQ + q + 1)
                    if j >= 2:
                        pe.wait_ge(e["We"], j - 1)
                    for a in range(PQ):
                        p = q * PQ + a
                        mm = pe.matmul(banks4(j % 2)[:, a, :], CT[i % 2][:, p, :], T[:, p, :], start=True, stop=True)
                    mm.then_inc(e["W"], 1)

                def second(j):
                    i, q = divmod(j, NQ)
                    pe.wait_ge(e["We"], j + 1)
                    for a in range(PQ):
                        p = q * PQ + a
                        if i < SOLVE - 2:
                            pe.matmul(banks4(2 + q)[:, a, :], TT[:, p, :], W[:, p, :], start=True, stop=True)
                        mm = pe.matmul(banks4(5 + q)[:, a, :], W[:, p, :], TT[:, p, :], start=True, stop=True)
                    mm.then_inc(e["PP"], 1)

                for i in range(SOLVE - 1):
                    first(i * NQ)
                    first(i * NQ + 1)
                    second(i * NQ)
                    first(i * NQ + 2)
                    second(i * NQ + 1)
                    second(i * NQ + 2)
                pe.wait_ge(e["TTn"], (SOLVE - 1) * NQ)
                pe.wait_ge(e["We"], (SOLVE - 1) * NQ)

                def b2(b, h):
                    return banks4(b + h // PQ)[:, h % PQ, :]

                for h in range(DNH):
                    mm = pe.matmul(b2(0, h), TT[:, h, :], vb[:, h, :], start=True, stop=True)
                mm.then_inc(e["U"], 1)
                for h in range(DNH):
                    mm = pe.matmul(b2(2, h), nkbg[:, h, :], TT[:, DNH + h, :], start=True, stop=True)
                mm.then_inc(e["wT"], 1)
                pe.wait_ge(e["Ue"], 2)
                for h in range(DNH):
                    mm = pe.matmul(b2(4, h), kdec[:, h, :], U0[:, h, :], start=True, stop=True)
                mm.then_inc(e["S"], 1)
                pe.wait_ge(e["Se"], 2)
                for h in range(DNH):
                    mm = pe.matmul(b2(6, h), DT[:, h, :], U0[:, h, :], start=True, stop=True)
                mm.then_inc(e["O"], 1)
                pe.wait_ge(e["wTe"], 2)
                for h in range(DNH):
                    pe.matmul(b2(0, h), TT[:, DNH + h, :], vb[:, DNH + h, :], start=True, stop=False)
                    mm = pe.matmul(b2(0, h), wT[:, h, :], St[:, h, :], start=False, stop=True)
                mm.then_inc(e["V"], 1)
                pe.wait_ge(e["Ve"], 2)
                for h in range(DNH):
                    pe.matmul(b2(2, h), qd[:, h, :], St[:, h, :], start=True, stop=False)
                    mm = pe.matmul(b2(2, h), DT[:, DNH + h, :], V1[:, h, :], start=False, stop=True)
                mm.then_inc(e["O"], 1)
                cross1.pe(pe, lambda eng, j: eng.wait_ge(e["Oe"], 4) if j == 0 else (eng.wait_ge(cross1.s_eva, j - 1) if j >= 2 else None))
                xa1.pe(pe, lambda eng: eng.wait_ge(cross1.s_eva, 4))
                op1.pe(pe, lambda eng: (eng.wait_ge(xa1.s_mix, 2 * XAH), eng.wait_ge(e["mix"], NT)))

            @block.sync
            def _(sp):
                sp.dma_start(gain[:, 0, :], row(ffn_norm[1], D)).then_inc(s_gain_ffn1, 16)

        next_layer()
        norm_f = NormTranspose("nf", [(X[:, t, :], gain[:, 0, :], hT[:, :, t * P:(t + 1) * P], (s_gain_ffn1, 16)) for t in range(NT)])
        router = gain[:, 1, 0:KC * NE].rearrange("p (c e) -> p c e", c=KC)
        slotno = gain[:, 1, 64:64 + NPB * CAP]
        em8 = gain[:, 1, 400:400 + NE]
        rt = hT[:].rearrange("p c t -> p (c t)")[:, 0:16 * 16].rearrange("p (k t e) -> p k t e", k=16, t=NT)
        rs = hT[:].rearrange("p c t -> p (c t)")[:, 256:256 + 16].rearrange("p (k t) -> p k t", t=NT)
        posn = sb("posn", [P, NT, NE + 1])
        wgt = sb("wgt", [P, NT, NE + 1])
        cnt = sb("cnt", [1, NE + 1], I32)
        cntf = sb("cntf", [1, NE + 1])
        sel = sb("sel", [P, NT, CAP])
        selw = sb("selw", [P, NT, CAP])
        hg = gain[:, 1, 416:416 + 2 * NB * CAP].rearrange("p (i b n) -> p i b n", i=2, b=NB)
        hh = sb("hh", [P, 2, NB, CAP])
        hflat = hT[:].rearrange("p c t -> p (c t)")
        xe = hflat[:, 0:KC * CAP].rearrange("p (c n) -> p c n", c=KC)
        ye = hflat[0:CAP, KC * CAP:KC * CAP + D]
        selT = hflat[0:CAP, KC * CAP + D:KC * CAP + D + S]
        r = {n: lsem(f"f_{n}") for n in (
            "router", "iota", "lg", "lgo", "step", "d", "ed", "mask", "pos", "posn", "cnt")}
        m = {n: lsem(f"m_{n}") for n in (
            "sel", "selw", "gather", "xe_act", "xe_dve", "gu", "silu", "h", "down", "selT", "selTo",
            "y_act", "y_dve", "scatter", "x")}

        def moe_load(sp, ex, g):
            load_group(sp, g % SLOTS, moe_w_gate[0][ex], moe_w_up[0][ex], moe_w_down[0][ex], g)

        def dve_select(dve, ex, b):
            for t in range(NT):
                dve.tensor_scalar(sel[:, t, :], slotno[:, b * CAP:(b + 1) * CAP], posn[:, t, bass.ds(ex, 1)], None,
                                  ALU.is_equal).then_inc(m["sel"], 1)

        def pe_gather(pe, k):
            pe.wait_ge(m["sel"], NT * k + NT)
            for c in range(KC):
                for t in range(NT):
                    mm = pe.matmul(PS[:, c // 4, (c % 4) * CAP:(c % 4 + 1) * CAP], xn[:, t, c * P:(c + 1) * P], sel[:, t, :],
                                   start=(t == 0), stop=(t == NT - 1))
                if c % 4 == 3:
                    mm.then_inc(m["gather"], 1)

        def act_gathered(act, k):
            act.wait_ge(m["gather"], 2 * k + 1)
            act.activation(xe[:, 0:4, :], PS[:, 0, 0:4 * CAP].rearrange("p (c n) -> p c n", c=4), ACT.Copy).then_inc(m["xe_act"], 1)

        def dve_gathered(dve, k):
            dve.wait_ge(m["gather"], 2 * k + 2)
            dve.tensor_copy(xe[:, 4:8, :], PS[:, 1, 0:4 * CAP].rearrange("p (c n) -> p c n", c=4)).then_inc(m["xe_dve"], 1)

        def pe_pass(pe, n, k, gather_next):
            def down(g):
                pe.wait_ge(m["h"], NG * n + g + 1)
                vd = slot_views(g % SLOTS)[2]
                for b in range(NB):
                    for half in range(2):
                        mm = pe.matmul(PS[0:CAP, 4 + half, :], hh[:, g % 2, b, :], vd[:, b, half * 512:(half + 1) * 512],
                                       start=(g == 0 and b == 0), stop=(g == NG - 1 and b == NB - 1))
                mm.then_inc(m["down"], 1)

            pe.wait_ge(m["xe_act"], k + 1)
            pe.wait_ge(m["xe_dve"], k + 1)
            for g in range(NG):
                s = g % SLOTS
                vg, vu, _ = slot_views(s)
                pe.wait_ge(s_w[s], 48 * (2 * n + NG // SLOTS + g // SLOTS + 1))
                if g >= 2:
                    pe.wait_ge(m["h"], NG * n + g - 1)
                for b in range(NB):
                    for i, w in enumerate((vg, vu)):
                        at = (i * NB + b) * CAP
                        for c in range(KC):
                            mm = pe.matmul(PS[:, 2 + g % 2, at:at + CAP], w[:, c, b * P:(b + 1) * P], xe[:, c, :],
                                           start=(c == 0), stop=(c == KC - 1))
                mm.then_inc(m["gu"], 1)
                if g == 1:
                    pe.wait_ge(m["selw"], NT * n + NT)
                    for t in range(NT):
                        mm = pe.transpose(PS[0:CAP, 0, t * P:(t + 1) * P], selw[:, t, :], ident[:])
                    mm.then_inc(m["selT"], 1)
                if g >= 1:
                    down(g - 1)
            pe.wait_ge(m["selTo"], n + 1)
            if gather_next:
                pe_gather(pe, k + 1)
            down(NG - 1)
            for t in range(NT):
                for half in range(2):
                    if t == 0:
                        pe.wait_ge(m["y_act"] if half == 0 else m["y_dve"], n + 1)
                    else:
                        pe.wait_ge(m["x"], 4 * n + half + 1)
                    pe.matmul(PS[:, 6 + half, :], selT[:, t * P:(t + 1) * P], ye[:, half * 512:(half + 1) * 512],
                              start=True, stop=True).then_inc(m["scatter"], 1)

        def act_pass(act, n, k, gather_next):
            for g in range(NG):
                act.wait_ge(m["gu"], NG * n + g + 1)
                if g >= 2:
                    act.wait_ge(m["h"], NG * n + g - 1)
                act.activation(hg[:, g % 2], PS[:, 2 + g % 2, 0:NB * CAP].rearrange("p (b n) -> p b n", b=NB),
                               ACT.Silu).then_inc(m["silu"], 1)
            if gather_next:
                act_gathered(act, k + 1)
            act.wait_ge(m["down"], NG * n + NG)
            act.activation(ye[:, 0:512], PS[0:CAP, 4, :], ACT.Copy).then_inc(m["y_act"], 1)

        def dve_pass(dve, n, k, ex, gather_next):
            for t in range(NT):
                dve.wait_ge(m["sel"], NT * k + NT)
                dve.tensor_scalar(selw[:, t, :], sel[:, t, :], wgt[:, t, bass.ds(ex, 1)], None, ALU.mult).then_inc(m["selw"], 1)
            for g in range(NG):
                dve.wait_ge(m["silu"], NG * n + g + 1)
                if g >= 2:
                    dve.wait_ge(m["down"], NG * n + g - 1)
                dve.tensor_tensor(hh[:, g % 2], hg[:, g % 2],
                                  PS[:, 2 + g % 2, NB * CAP:2 * NB * CAP].rearrange("p (b n) -> p b n", b=NB),
                                  ALU.mult).then_inc(m["h"], 1)
                if g == 1:
                    dve.wait_ge(m["selT"], n + 1)
                    dve.tensor_copy(selT, PS[0:CAP, 0, 0:S]).then_inc(m["selTo"], 1)
                if g == 2 and gather_next:
                    dve.wait_ge(m["gather"], 2 * k + 2)
                    dve.wait_ge(m["selw"], NT * n + NT)
                    dve_select(dve, ex + 1, 0)
            if gather_next:
                dve_gathered(dve, k + 1)
            dve.wait_ge(m["down"], NG * n + NG)
            dve.tensor_copy(ye[:, 512:D], PS[0:CAP, 5, :]).then_inc(m["y_dve"], 1)
            for t in range(NT):
                for half in range(2):
                    dve.wait_ge(m["scatter"], 4 * n + 2 * t + half + 1)
                    xv = X[:, t, half * 512:(half + 1) * 512]
                    dve.tensor_tensor(xv, xv, PS[:, 6 + half, :], ALU.add).then_inc(m["x"], 1)

        with nc.Block() as block:
            @block.sync
            def _(sp):
                sp.dma_start(router, k_rows(moe_router[0])).then_inc(r["router"], 16)
                for g in range(SLOTS):
                    moe_load(sp, 0, g)
                with sp.Fori(0, NE - 1) as ex:
                    for g in range(SLOTS, NG):
                        sp.wait_ge(m["down"], NG * ex + g - SLOTS + 1)
                        moe_load(sp, ex, g)
                    for g in range(SLOTS):
                        sp.wait_ge(m["down"], NG * ex + g + SLOTS + 1)
                        moe_load(sp, ex + 1, g)
                for g in range(SLOTS, NG):
                    sp.wait_ge(m["down"], NG * (NE - 1) + g - SLOTS + 1)
                    moe_load(sp, NE - 1, g)

            @block.gpsimd
            def _(pool):
                pool.iota(slotno, [[1, NPB * CAP]], base=0, channel_multiplier=0,
                          allow_small_or_imprecise_dtypes=True).then_inc(r["iota"], 1)
                pool.iota(em8, [[1, NE]], base=-NE, channel_multiplier=0,
                          allow_small_or_imprecise_dtypes=True).then_inc(r["iota"], 1)

            @block.scalar
            def _(act):
                link = linker(act, "act")
                act.preload_act_table_set("natural_log_exp_and_others")
                norm_f.act_squares(act, link)
                norm_f.act_rstd(act, link)
                norm_f.act_evacuate(act)
                act.wait_ge(r["d"], 1)
                act.activation(rs[:, 3, :], rs[:, 2, :], ACT.Exp).then_inc(r["ed"], 1)
                act_gathered(act, 0)
                with act.Fori(0, NE) as ex:
                    act_pass(act, ex, ex, True)

            @block.vector
            def _(dve):
                link = linker(dve, "dve")
                norm_f.dve_rows(dve)
                dve.wait_ge(r["lg"], 1)
                dve.tensor_copy(rt[:, 0], PS[:, 2, 0:NT * NE].rearrange("p (t e) -> p t e", t=NT)).then_inc(r["lgo"], 1)
                dve.wait_ge(r["lgo"], 1)
                dve.wait_ge(r["iota"], 2)
                em8b = em8.unsqueeze(1).to_broadcast([P, NT, NE])

                def bc(v):
                    return v.unsqueeze(2).to_broadcast([P, NT, NE])

                for i in range(2):
                    lg, eq, first, mask = rt[:, 3 * i], rt[:, 1], rs[:, 4 + i, :], rt[:, 4 + i]
                    link(dve.tensor_reduce(rs[:, i, :], lg, X_AXIS, ALU.max))
                    link(dve.tensor_tensor(eq, lg, bc(rs[:, i, :]), ALU.is_equal))
                    link(dve.tensor_tensor(eq, eq, em8b, ALU.mult))
                    link(dve.tensor_reduce(first, eq, X_AXIS, ALU.min))
                    link(dve.tensor_tensor(mask, em8b, bc(first), ALU.is_equal))
                    if i == 0:
                        link(dve.scalar_tensor_tensor(out=rt[:, 3], in0=mask, scalar=NEG, in1=lg, op0=ALU.mult, op1=ALU.add))
                dve.tensor_tensor(rs[:, 2, :], rs[:, 1, :], rs[:, 0, :], ALU.subtract).then_inc(r["d"], 1)
                dve.tensor_tensor(rt[:, 6], rt[:, 4], rt[:, 5], ALU.add).then_inc(r["mask"], 1)
                dve.wait_ge(r["ed"], 1)
                link(dve.tensor_scalar(rs[:, 6, :], rs[:, 3, :], 1.0, None, ALU.add))
                link(dve.reciprocal(rs[:, 6, :], rs[:, 6, :]))
                link(dve.tensor_tensor(rs[:, 7, :], rs[:, 6, :], rs[:, 3, :], ALU.mult))
                link(dve.tensor_tensor(rt[:, 4], rt[:, 4], bc(rs[:, 6, :]), ALU.mult))
                link(dve.tensor_tensor(rt[:, 5], rt[:, 5], bc(rs[:, 7, :]), ALU.mult))
                link(dve.tensor_tensor(wgt[:, :, 0:NE], rt[:, 4], rt[:, 5], ALU.add))
                dve.wait_ge(r["pos"], 1)
                link(dve.memset(posn[:], -1.0))
                link(dve.scalar_tensor_tensor(out=rt[:, 7], in0=PS[:, 3, 0:NT * NE].rearrange("p (t e) -> p t e", t=NT), scalar=1.0,
                                              in1=rt[:, 6], op0=ALU.add, op1=ALU.mult))
                link(dve.tensor_scalar(posn[:, :, 0:NE], rt[:, 7], -1.0, None, ALU.add))
                link(dve.tensor_copy(cntf[:, 0:NE], PS[0:1, 3, 2 * NT * NE:2 * NT * NE + NE]))
                link(dve.tensor_reduce(cntf[:, NE:NE + 1], cntf[:, 0:NE], X_AXIS, ALU.max))
                dve.tensor_copy(cnt[:], cntf[:]).then_inc(r["cnt"], 1)
                dve_select(dve, 0, 0)
                dve_gathered(dve, 0)
                with dve.Fori(0, NE) as ex:
                    dve_pass(dve, ex, ex, ex, True)

            @block.tensor
            def _(pe):
                norm_f.pe(pe)
                norm_f.ready(pe, NT)
                pe.wait_ge(r["router"], 16)
                for t in range(NT):
                    for c in range(KC):
                        mm = pe.matmul(PS[:, 2, t * NE:(t + 1) * NE], hT[:, c, t * P:(t + 1) * P], router[:, c, :],
                                       start=(c == 0), stop=(c == KC - 1))
                mm.then_inc(r["lg"], 1)
                pe.wait_ge(r["mask"], 1)
                pe.matmul(PS[:, 3, 0:NE], upstrict[:], rt[:, 6, 0], start=True, stop=True)
                pe.matmul(PS[:, 3, NE:2 * NE], upstrict[:], rt[:, 6, 1], start=True, stop=False)
                pe.matmul(PS[:, 3, NE:2 * NE], ones[:], rt[:, 6, 0], start=False, stop=True)
                pe.matmul(PS[:, 3, 4 * NE:5 * NE], ones[:], rt[:, 6, 0], start=True, stop=False)
                pe.matmul(PS[:, 3, 4 * NE:5 * NE], ones[:], rt[:, 6, 1], start=False, stop=True).then_inc(r["pos"], 1)
                pe_gather(pe, 0)
                with pe.Fori(0, NE) as ex:
                    pe_pass(pe, ex, ex, True)

        def overflow(eng, one_pass):
            most = eng.value_load(cnt[0:1, NE:NE + 1], min_val=0, max_val=S)
            with eng.If(most > CAP):
                done = eng.alloc_register("passes_done")
                eng.reg_mov(done, NE)
                with eng.Fori(0, NE) as ex:
                    for b in range(1, NPB):
                        tokens = eng.value_load(cnt[0:1, bass.ds(ex, 1)], min_val=0, max_val=S)
                        with eng.If(tokens > b * CAP):
                            n = eng.snap(done, min_val=NE, max_val=2 * S * NT)
                            one_pass(ex, b, n)
                            eng.reg_add(done, done, 1)
                        with eng.Else():
                            eng.nop()
                        eng.nop()
                eng.nop()
            with eng.Else():
                eng.nop()
            eng.nop()

        with nc.Block() as block:
            @block.sync
            def _(sp):
                def one_pass(ex, b, n):
                    for g in range(NG):
                        sp.wait_ge(m["down"], NG * n + (g - SLOTS + 1))
                        moe_load(sp, ex, g)
                overflow(sp, one_pass)

            @block.scalar
            def _(act):
                def one_pass(ex, b, n):
                    act_gathered(act, n + 1)
                    act_pass(act, n, n + 1, False)
                overflow(act, one_pass)

            @block.vector
            def _(dve):
                def one_pass(ex, b, n):
                    dve.wait_ge(m["gather"], 2 * n + 2)
                    dve.wait_ge(m["selw"], NT * n)
                    dve_select(dve, ex, b)
                    dve_gathered(dve, n + 1)
                    dve_pass(dve, n, n + 1, ex, False)
                overflow(dve, one_pass)

            @block.tensor
            def _(pe):
                def one_pass(ex, b, n):
                    pe_gather(pe, n + 1)
                    pe_pass(pe, n, n + 1, False)
                overflow(pe, one_pass)


        with nc.Block() as block:
            @block.sync
            def _(sp):
                sp.dma_start(out[0].rearrange("(t p) d -> p t d", p=P), X[:]).then_inc(s_y, 16)
                sp.wait_ge(s_y, 16)


_INS = ['x', 'mem', 'mix_norm', 'ffn_norm', 'mem_norm', 'w_mem_kv', 'xa_q_norm', 'xa_k_norm', 'w_out',
        'sb_w_in', 'sb_q_norm', 'sb_k_norm', 'dn_w_in', 'dn_conv', 'dn_a_log', 'dn_dt_bias', 'dn_o_norm',
        'ffd_w_gate', 'ffd_w_up', 'ffd_w_down', 'moe_router', 'moe_w_gate', 'moe_w_up', 'moe_w_down']
_OUTS = [((1, S, D), 'float32')]


def kernel(**inputs):
    import numpy as _np
    import concourse.bacc as _bacc
    from concourse import mybir as _mybir
    from concourse.bass_utils import run_bass_kernel_spmd as _run

    nc = _bacc.Bacc("TRN2", target_bir_lowering=False, num_devices=1)
    arrays, args = {}, []
    for name in _INS:
        a = _np.ascontiguousarray(inputs[name])
        arrays[f"in_{name}_dram"] = a
        args.append(nc.dram_tensor(f"in_{name}_dram", a.shape, _mybir.dt.from_np(a.dtype), kind="ExternalInput").ap())
    for i, (shape, dtype) in enumerate(_OUTS):
        dt = _mybir.dt.from_np(_np.dtype(dtype))
        args.append(nc.dram_tensor(f"out_{i}_dram", shape, dt, kind="ExternalOutput").ap())
    hybrid_kernel(nc, *args)
    r = _run(nc, [arrays], core_ids=[0])
    got = tuple(r.results[0][f"out_{i}_dram"] for i in range(len(_OUTS)))
    return got[0]
```

```python
from contextlib import ExitStack

import numpy as np

import concourse.bass as bass
from concourse import mybir

P = 128
D = 1024
S = 256
NT = S // P
KC = D // P
HD = 64
SBH, XAH, DNH = 12, 4, 6
SBW, XAW, DNW = SBH * HD, XAH * HD, DNH * P
SB_IN = 3 * SBW + XAW
DN_IN = 4 * DNW + 2 * DNH + XAW
FF = 3584
NE = 8
GF = 256
NG = FF // GF
PART = KC * GF
STAGES = 7
CAP = 96
NPB = -(-S // CAP)
EPS = 1e-6
ASLOT = KC * 512
ASLOTS = 3
ARENA = 43008
NEG = -1.0e30

F32 = mybir.dt.float32
BF16 = mybir.dt.bfloat16
F32R = mybir.dt.float32r
I32 = mybir.dt.int32
ALU = mybir.AluOpType
ACT = mybir.ActivationFunctionType
X_AXIS = mybir.AxisListType.X


def hybrid_kernel(nc, x, mem, mix_norm, ffn_norm, mem_norm, w_mem_kv, xa_q_norm, xa_k_norm, w_out,
                  sb_w_in, sb_q_norm, sb_k_norm, dn_w_in, dn_conv, dn_a_log, dn_dt_bias, dn_o_norm,
                  ffd_w_gate, ffd_w_up, ffd_w_down, moe_router, moe_w_gate, moe_w_up, moe_w_down, out):
    with ExitStack() as ctx:
        def sb(name, shape, dt=F32):
            return ctx.enter_context(nc.sbuf_tensor(name, shape, dt))

        layer_sems = []

        def sem(name):
            return ctx.enter_context(nc.semaphore(name))

        def lsem(name):
            h = layer_sems[0].enter_context(nc.semaphore(name))
            layer_sems[1].append(h)
            return h

        def next_layer():
            if layer_sems:
                with nc.Block() as block:
                    @block.gpsimd
                    def _(pool):
                        for h in layer_sems[1]:
                            pool.sem_clear(h)
                layer_sems[0].close()
            layer_sems[:] = [ctx.enter_context(ExitStack()), []]

        s_y = sem("s_y")
        next_layer()

        memory = [None]

        def psb(name, shape, dt=F32):
            return memory[0].enter_context(nc.sbuf_tensor(name, shape, dt))

        def next_memory():
            if memory[0] is not None:
                memory[0].close()
            memory[0] = ctx.enter_context(ExitStack())

        next_memory()

        X = sb("X", [P, NT, D])
        xn = sb("xn", [P, NT, D])
        gain = sb("gain", [P, 2, D])
        junk = sb("junk", [P, D], BF16)
        stat = sb("stat", [P, 3, 8])
        epsc = sb("epsc", [P, 1])
        ident = sb("ident", [P, P])
        ones = sb("ones", [P, P])
        upincl = sb("upincl", [P, P])
        upstrict = sb("upstrict", [P, P])
        PS = ctx.enter_context(nc.psum_tensor("PS", [P, 8, 512], F32))

        hT = psb("hT0", [P, KC, S])
        ring = psb("ring0", [P, ARENA])

        class Scratch:
            def __init__(self):
                self.at = ASLOTS * ASLOT

            def tile(self, parts, *shape):
                n = int(np.prod(shape))
                v = ring[0:parts, self.at:self.at + n]
                self.at += n
                assert self.at <= ARENA, (self.at, ARENA)
                names = "abc"[:len(shape)]
                if len(shape) == 1:
                    return v
                return v.rearrange("p (" + " ".join(names) + ") -> p " + " ".join(names),
                                   **{c: k for c, k in zip(names[1:], shape[1:])})

        def aslot(n, cols):
            at = (n % ASLOTS) * ASLOT
            return ring[:, at:at + KC * cols].rearrange("p (c f) -> p c f", c=KC)

        def k_rows(w):
            return w.rearrange("(c p) f -> p c f", p=P)

        s_chain = {}

        def linker(eng, name):
            if name not in s_chain:
                s_chain[name] = [sem(f"s_{name}_chain"), 0]
            c = s_chain[name]

            def link(ins):
                c[1] += 1
                ins.then_inc(c[0], 1)
                eng.wait_ge(c[0], c[1])
            return link

        class NormTranspose:
            def __init__(self, tag, units):
                self.units = units
                self.s_sq, self.s_ms, self.s_rstd, self.s_xn = (lsem(f"{tag}_{n}") for n in ("sq", "ms", "rstd", "xn"))
                self.s_tr, self.s_eva, self.s_evd = (lsem(f"{tag}_{n}") for n in ("tr", "eva", "evd"))

            def act_squares(self, act, link):
                for u, (src, g, dst, ready) in enumerate(self.units):
                    act.wait_ge(*ready)
                    if u >= 1:
                        act.wait_ge(self.s_sq, u)
                    act.activation(junk[:], src, ACT.Square, accum_out=stat[:, 0, u:u + 1]).then_inc(self.s_sq, 1)

            def act_rstd(self, act, link):
                n = len(self.units)
                act.wait_ge(self.s_ms, 1)
                link(act.activation(stat[:, 2, 0:n], stat[:, 1, 0:n], ACT.Ln))
                act.activation(stat[:, 2, 0:n], stat[:, 2, 0:n], ACT.Exp, scale=-0.5).then_inc(self.s_rstd, 1)

            def act_evacuate(self, act):
                for u, (src, g, dst, ready) in enumerate(self.units):
                    act.wait_ge(self.s_tr, 2 * u + 1)
                    act.activation(dst[:, 0:4, :], PS[:, 0, :].rearrange("p (c t) -> p c t", c=4),
                                   ACT.Copy).then_inc(self.s_eva, 1)

            def dve_rows(self, dve):
                n = len(self.units)
                dve.wait_ge(self.s_sq, n)
                dve.tensor_scalar(stat[:, 1, 0:n], stat[:, 0, 0:n], 1.0 / D, EPS, ALU.mult, ALU.add).then_inc(self.s_ms, 1)
                dve.wait_ge(self.s_rstd, 1)
                for u, (src, g, dst, ready) in enumerate(self.units):
                    if u >= NT:
                        self.dve_evacuate_one(dve, u - NT)
                    dve.scalar_tensor_tensor(out=xn[:, u % NT, :], in0=src, scalar=stat[:, 2, u:u + 1], in1=g,
                                             op0=ALU.mult, op1=ALU.mult).then_inc(self.s_xn, 1)
                for u in range(max(0, n - NT), n):
                    self.dve_evacuate_one(dve, u)

            def dve_evacuate_one(self, dve, u):
                dve.wait_ge(self.s_tr, 2 * u + 2)
                dve.tensor_copy(self.units[u][2][:, 4:8, :],
                                PS[:, 1, :].rearrange("p (c t) -> p c t", c=4)).then_inc(self.s_evd, 1)

            def pe(self, pe):
                for u in range(len(self.units)):
                    pe.wait_ge(self.s_xn, u + 1)
                    for half, freed in ((0, self.s_eva), (1, self.s_evd)):
                        if u >= 1:
                            pe.wait_ge(freed, u)
                        for c in range(4):
                            mm = pe.transpose(PS[:, half, c * P:(c + 1) * P],
                                              xn[:, u % NT, (4 * half + c) * P:(4 * half + c + 1) * P], ident[:])
                        mm.then_inc(self.s_tr, 1)

            def ready(self, eng, units):
                eng.wait_ge(self.s_eva, units)
                eng.wait_ge(self.s_evd, units)

        class NormTransposeSplit(NormTranspose):
            def act_evacuate(self, act):
                for u, (src, g, dst, ready) in enumerate(self.units):
                    for half in range(2):
                        act.wait_ge(self.s_tr, 2 * u + half + 1)
                        act.activation(dst[0][:, 4 * half:4 * half + 4, :], PS[:, half, :].rearrange("p (c t) -> p c t", c=4),
                                       ACT.Copy).then_inc(self.s_eva, 1)

            def dve_evacuate_one(self, dve, u):
                dst = self.units[u][2]
                for half in range(2):
                    dve.wait_ge(self.s_eva, 2 * u + half + 1)
                    hs = slice(4 * half, 4 * half + 4)
                    dve.tensor_tensor(dst[1][:, hs, :], PS[:, half, :].rearrange("p (c t) -> p c t", c=4),
                                      dst[0][:, hs, :].bitcast(F32), ALU.subtract).then_inc(self.s_evd, 1)

            def pe(self, pe):
                for u in range(len(self.units)):
                    pe.wait_ge(self.s_xn, u + 1)
                    for half in range(2):
                        if u >= 1:
                            pe.wait_ge(self.s_evd, 2 * u - 1 + half)
                        for c in range(4):
                            mm = pe.transpose(PS[:, half, c * P:(c + 1) * P],
                                              xn[:, u % NT, (4 * half + c) * P:(4 * half + c + 1) * P], ident[:])
                        mm.then_inc(self.s_tr, 1)

            def ready(self, eng, units):
                eng.wait_ge(self.s_evd, 2 * units)

        class CrossPrep:
            def __init__(self, tag, q_tok, kv_tok, qT, kT, sq, st, gq, gk, banks):
                self.q_tok, self.kv_tok, self.qT, self.kT = q_tok, kv_tok, qT, kT
                self.sq, self.st, self.gq, self.gk, self.banks = sq, st, gq, gk, banks
                self.s_sq, self.s_ms, self.s_rstd, self.s_n = (lsem(f"{tag}_{n}") for n in ("sq", "ms", "rstd", "n"))
                self.s_tr, self.s_eva = lsem(f"{tag}_tr"), lsem(f"{tag}_eva")

            def act(self, act, link, ready):
                ready(act)
                act.activation(self.sq[:, :, 0:XAW], self.q_tok, ACT.Square).then_inc(self.s_sq, 1)
                act.activation(self.sq[:, :, XAW:2 * XAW], self.kv_tok[:, :, 0:XAW], ACT.Square).then_inc(self.s_sq, 1)
                act.wait_ge(self.s_ms, 1)
                link(act.activation(self.st[:, 1], self.st[:, 1], ACT.Ln))
                act.activation(self.st[:, 1], self.st[:, 1], ACT.Exp, scale=-0.5).then_inc(self.s_rstd, 1)

            def dve(self, dve, link, ready):
                dve.wait_ge(self.s_sq, 2)
                link(dve.tensor_reduce(self.st[:, 0].rearrange("p (t h) -> p t h", t=NT),
                                       self.sq.rearrange("p t (h d) -> p t h d", d=HD), X_AXIS, ALU.add))
                dve.tensor_scalar(self.st[:, 1], self.st[:, 0], 1.0 / HD, EPS, ALU.mult, ALU.add).then_inc(self.s_ms, 1)
                dve.wait_ge(self.s_rstd, 1)
                ready(dve)
                r = self.st[:, 1].rearrange("p (t h) -> p t h", t=NT)
                for v, h0 in ((self.q_tok, 0), (self.kv_tok[:, :, 0:XAW], XAH)):
                    for t in range(NT):
                        w = v[:, t, :].rearrange("p (h d) -> p h d", d=HD)
                        dve.tensor_tensor(w, w, r[:, t, h0:h0 + XAH].unsqueeze(2).to_broadcast([P, XAH, HD]),
                                          ALU.mult).then_inc(self.s_n, 1)

            def pe(self, pe, freed):
                for j in range(4):
                    pe.wait_ge(self.s_n, 2 * NT)
                    freed(pe, j)
                    src = self.q_tok if j < 2 else self.kv_tok
                    for i in range(2):
                        h = 2 * (j % 2) + i
                        for t in range(NT):
                            mm = pe.transpose(PS[0:HD, self.banks[j], (i * NT + t) * P:(i * NT + t + 1) * P],
                                              src[:, t, h * HD:(h + 1) * HD], ident[:])
                    mm.then_inc(self.s_tr, 1)

            def act_evacuate(self, act):
                for j in range(4):
                    act.wait_ge(self.s_tr, j + 1)
                    dst = (self.qT if j < 2 else self.kT)[:, 2 * (j % 2):2 * (j % 2) + 2, :]
                    act.activation(dst, PS[0:HD, self.banks[j], :].rearrange("p (h t) -> p h t", h=2), ACT.Copy,
                                   scale=(self.gq if j < 2 else self.gk)).then_inc(self.s_eva, 1)

        class Cross:
            def __init__(self, tag, qT, kT, v_tok, mix, c0, tmp):
                self.qT, self.kT, self.v, self.mix, self.c0 = qT, kT, v_tok, mix, c0
                self.prob, self.probT, self.st = tmp
                self.s_s, self.s_max, self.s_p, self.s_pt, self.s_pe, self.s_o, self.s_mix, self.s_rec = (
                    lsem(f"{tag}_{n}") for n in ("scores", "max", "probs", "probsT", "probsT_out", "o", "mix", "rec"))
                self.units = [(h, t) for h in range(XAH) for t in range(NT)]

            def pe(self, pe, begin):
                n = len(self.units)
                begin(pe)
                for i in range(n + 2):
                    if i < n:
                        h, t = self.units[i]
                        if i >= 2:
                            pe.wait_ge(self.s_p, i - 1)
                        pe.matmul(PS[:, i % 2, 0:S], self.qT[:, h, t * P:(t + 1) * P], self.kT[:, h, :],
                                  start=True, stop=True).then_inc(self.s_s, 1)
                    if 1 <= i <= n:
                        j = i - 1
                        pe.wait_ge(self.s_p, j + 1)
                        if j >= 2:
                            pe.wait_ge(self.s_pe, j - 1)
                        for m in range(NT):
                            mm = pe.transpose(PS[:, 2 + j % 2, m * P:(m + 1) * P],
                                              self.prob[:, j % 2, m * P:(m + 1) * P], ident[:])
                        mm.then_inc(self.s_pt, 1)
                    if i >= 2:
                        j = i - 2
                        h, t = self.units[j]
                        pe.wait_ge(self.s_pe, j + 1)
                        if j >= 2:
                            pe.wait_ge(self.s_mix, j - 1)
                        for m in range(NT):
                            mm = pe.matmul(PS[:, 4 + j % 2, 0:HD], self.probT[:, j % 2, m * P:(m + 1) * P],
                                           self.v[:, m, h * HD:(h + 1) * HD], start=(m == 0), stop=(m == NT - 1))
                        mm.then_inc(self.s_o, 1)

            def act(self, act):
                n = len(self.units)
                for i in range(n + 1):
                    if i < n:
                        act.wait_ge(self.s_max, i + 1)
                        if i >= 2:
                            act.wait_ge(self.s_pt, i - 1)
                        act.activation(self.prob[:, i % 2, :], PS[:, i % 2, 0:S], ACT.Exp,
                                       bias=self.st[:, 0, i:i + 1],
                                       accum_out=self.st[:, 1, i:i + 1]).then_inc(self.s_p, 1)
                    if i >= 1:
                        j = i - 1
                        act.wait_ge(self.s_pt, j + 1)
                        if j >= 2:
                            act.wait_ge(self.s_o, j - 1)
                        act.activation(self.probT[:, j % 2, :], PS[:, 2 + j % 2, 0:S], ACT.Copy).then_inc(self.s_pe, 1)

            def dve(self, dve):
                n = len(self.units)
                for i in range(n + 2):
                    if i < n:
                        dve.wait_ge(self.s_s, i + 1)
                        dve.tensor_reduce(self.st[:, 0, i:i + 1], PS[:, i % 2, 0:S], X_AXIS, ALU.max,
                                          negate=True).then_inc(self.s_max, 1)
                    if i >= 2:
                        j = i - 2
                        h, t = self.units[j]
                        dve.wait_ge(self.s_p, j + 1)
                        dve.reciprocal(self.st[:, 2, j:j + 1], self.st[:, 1, j:j + 1]).then_inc(self.s_rec, 1)
                        dve.wait_ge(self.s_rec, j + 1)
                        dve.wait_ge(self.s_o, j + 1)
                        dve.tensor_scalar(self.mix[:, t, self.c0 + h * HD:self.c0 + (h + 1) * HD],
                                          PS[:, 4 + j % 2, 0:HD], self.st[:, 2, j:j + 1], None,
                                          ALU.mult).then_inc(self.s_mix, 1)

        class OutProjection:
            def __init__(self, tag, mix, slots, s_w):
                self.mix, self.slots, self.s_w = mix, slots, s_w
                self.s_tr, self.s_eva, self.s_evd, self.s_y, self.s_x = (
                    lsem(f"{tag}_{n}") for n in ("tr", "eva", "evd", "y", "x"))

            def pe(self, pe, ready):
                ready(pe)
                for t in range(NT):
                    for half, freed in ((0, self.s_eva), (1, self.s_evd)):
                        if t >= 1:
                            pe.wait_ge(freed, t)
                        for c in range(4):
                            k = 4 * half + c
                            mm = pe.transpose(PS[:, 6 + half, c * P:(c + 1) * P], self.mix[:, t, k * P:(k + 1) * P], ident[:])
                        mm.then_inc(self.s_tr, 1)
                for half in range(2):
                    self.s_w(pe, half)
                    for t in range(NT):
                        pe.wait_ge(self.s_eva, t + 1)
                        pe.wait_ge(self.s_evd, t + 1)
                        for k in range(KC):
                            mm = pe.matmul(PS[:, 2 * half + t, :], hT[:, k, t * P:(t + 1) * P], self.slots[half][:, k, :],
                                           start=(k == 0), stop=(k == KC - 1))
                        mm.then_inc(self.s_y, 1)

            def act(self, act):
                for t in range(NT):
                    act.wait_ge(self.s_tr, 2 * t + 1)
                    act.activation(hT[:, 0:4, t * P:(t + 1) * P], PS[:, 6, :].rearrange("p (c t) -> p c t", c=4),
                                   ACT.Copy).then_inc(self.s_eva, 1)

            def dve(self, dve):
                for t in range(NT):
                    dve.wait_ge(self.s_tr, 2 * t + 2)
                    dve.tensor_copy(hT[:, 4:8, t * P:(t + 1) * P],
                                    PS[:, 7, :].rearrange("p (c t) -> p c t", c=4)).then_inc(self.s_evd, 1)
                for half in range(2):
                    for t in range(NT):
                        dve.wait_ge(self.s_y, 2 * half + t + 1)
                        xv = X[:, t, half * 512:(half + 1) * 512]
                        dve.tensor_tensor(xv, xv, PS[:, 2 * half + t, :], ALU.add).then_inc(self.s_x, 1)

        def row(v, n):
            return v.rearrange("(a n) -> a n", a=1).to_broadcast([P, n])

        def col(v):
            return v.rearrange("(p a) -> p a", a=1)

        sc = Scratch()
        memr = sc.tile(P, NT, D)
        memT = sc.tile(P, KC, S)
        proj = sc.tile(P, NT, SB_IN)
        kv_tok = sc.tile(P, NT, 2 * XAW)
        qT = sc.tile(HD, SBH, S)
        kT = sc.tile(HD, SBH, S)
        xqT = sc.tile(HD, XAH, S)
        xkT = sc.tile(HD, XAH, S)
        mix = sc.tile(P, NT, D)
        sqs = sc.tile(P, 2 * SBW)
        sqx = sc.tile(P, NT, 2 * XAW)
        hst = sc.tile(P, NT, 2, 2 * SBH)
        xst = sc.tile(P, 2, NT * 2 * XAH)
        gcol = sc.tile(HD, 8)
        negup = sc.tile(P, P)
        negones = sc.tile(P, P)
        diag0 = sc.tile(P, 3, P)
        diagneg = sc.tile(P, P)
        xtmp = (sc.tile(P, 2, S), sc.tile(P, 2, S), sc.tile(P, 3, 8))
        flat = ring[:, ASLOTS * ASLOT:ASLOTS * ASLOT + 2 * NT * D].rearrange("p (k b n) -> p k b n", k=4, b=2)
        habs, hln, hL, hA = (flat[:, i, :, 0:384] for i in range(4))

        s_x, s_mem, s_gain, s_gcol = lsem("s_x"), lsem("s_mem"), sem("s_gain"), lsem("s_gcol")
        s_gain_ffn0, s_gain_mem1, s_gain_mix1, s_gain_ffn1 = (sem(f"s_gain_{n}") for n in ("ffn0", "mem1", "mix1", "ffn1"))
        s_const, s_const2 = sem("s_const"), sem("s_const2")
        s_aw = [sem(f"s_aw{i}") for i in range(ASLOTS)]
        loads0 = [(w_mem_kv[0], 512)] + [(sb_w_in[0][:, c * 512:(c + 1) * 512], 512) for c in range(SB_IN // 512)] + \
                 [(w_out[0][:, c * 512:(c + 1) * 512], 512) for c in range(2)]
        QK = 384
        loads1 = [(w_mem_kv[1], 512)] + [(dn_w_in[0][:, c * QK:(c + 1) * QK], QK) for c in range(8)] + \
                 [(dn_w_in[0][:, 4 * DNW:DN_IN], DN_IN - 4 * DNW)] + [(w_out[1][:, c * 512:(c + 1) * 512], 512) for c in range(2)]
        loads = loads0 + loads1
        N0 = len(loads0)

        def attention_loads(sp, first, last, phase):
            for n in range(first, last):
                if n - ASLOTS >= phase:
                    sp.wait_ge(*load_read[n - ASLOTS])
                w, cols = loads[n]
                sp.dma_start(aslot(n, cols), k_rows(w)).then_inc(s_aw[n % ASLOTS], 16)

        def weights_in(pe, n):
            pe.wait_ge(s_aw[n % ASLOTS], 16 * (n // ASLOTS + 1))
            return aslot(n, loads[n][1])

        norm_a = NormTranspose("na", [
            (memr[:, 0, :], gain[:, 1, :], memT[:, :, 0:P], (s_mem, 16)),
            (memr[:, 1, :], gain[:, 1, :], memT[:, :, P:S], (s_mem, 16)),
            (X[:, 0, :], gain[:, 0, :], hT[:, :, 0:P], (s_x, 16)),
            (X[:, 1, :], gain[:, 0, :], hT[:, :, P:S], (s_x, 16))])
        s_pj, s_pja, s_pjd = lsem("a_proj"), lsem("a_proj_act"), lsem("a_proj_dve")
        s_hsq, s_hms, s_hrs, s_hn, s_g8 = lsem("a_hsq"), lsem("a_hms"), lsem("a_hrs"), lsem("a_hn"), lsem("a_g8")
        s_ht, s_hta, s_htd = lsem("a_ht"), lsem("a_ht_act"), lsem("a_ht_dve")
        jobs_a = [(memT, 0, t, kv_tok[:, t, :]) for t in range(NT)] + \
                 [(hT, 1 + c, t, proj[:, t, c * 512:(c + 1) * 512]) for c in range(SB_IN // 512) for t in range(NT)]
        NJ = len(jobs_a)
        cross0 = CrossPrep("cp0", proj[:, :, 3 * SBW:SB_IN], kv_tok, xqT, xkT, sqx, xst, gcol[:, 4:5], gcol[:, 3:4], (0, 1, 2, 3))
        NHJ = SBH // 2

        load_read = [(s_pj, NT * (n + 1)) for n in range(N0 - 2)]

        with nc.Block() as block:
            @block.sync
            def _(sp):
                sp.dma_start(memr, mem[0].rearrange("(t p) d -> p t d", p=P)).then_inc(s_mem, 16)
                sp.dma_start(X[:], x[0].rearrange("(t p) d -> p t d", p=P)).then_inc(s_x, 16)
                sp.dma_start(gain[:, 1, :], row(mem_norm[0], D)).then_inc(s_gain, 16)
                sp.dma_start(gain[:, 0, :], row(mix_norm[0], D)).then_inc(s_gain, 16)
                attention_loads(sp, 0, 2, 0)
                for i, g in enumerate((sb_q_norm[0], sb_k_norm[0], xa_q_norm[0], xa_k_norm[0])):
                    sp.dma_start(gcol[:, i:i + 1], col(g)).then_inc(s_gcol, 16)
                attention_loads(sp, 2, N0, 0)

            @block.gpsimd
            def _(pool):
                link = linker(pool, "pool")
                pool.memset(epsc[:], EPS).then_inc(s_const, 1)
                link(pool.memset(ident[:], 0.0))
                pool.affine_select(out=ident[:], in_=ident[:], compare_op=ALU.not_equal, fill=1.0, base=0,
                                   pattern=[[-1, P]], channel_multiplier=1).then_inc(s_const, 1)
                for v, val in ((ones[:], 1.0), (negones, -1.0), (diag0.rearrange("p a b -> p (a b)"), 1.0)):
                    link(pool.memset(v, val))
                pool.affine_select(out=upincl[:], in_=ones[:], compare_op=ALU.is_ge, fill=0.0, base=0,
                                   pattern=[[1, P]], channel_multiplier=-1).then_inc(s_const2, 1)
                link(pool.affine_select(out=upstrict[:], in_=ones[:], compare_op=ALU.is_gt, fill=0.0, base=0,
                                        pattern=[[1, P]], channel_multiplier=-1))
                pool.affine_select(out=negup, in_=negones, compare_op=ALU.is_ge, fill=0.0, base=0,
                                   pattern=[[-1, P]], channel_multiplier=1).then_inc(s_const2, 1)
                link(pool.memset(diagneg, 0.0))
                pool.affine_select(out=diagneg, in_=diagneg, compare_op=ALU.is_gt, fill=NEG, base=0,
                                   pattern=[[1, P]], channel_multiplier=-1).then_inc(s_const2, 1)
                for a in (0, 2):
                    pool.tensor_copy(diag0[:, a, :], upstrict[:]).then_inc(s_const2, 1)

            @block.scalar
            def _(act):
                link = linker(act, "act")
                act.preload_act_table_set("natural_log_exp_and_others")
                norm_a.act_squares(act, link)
                norm_a.act_rstd(act, link)
                norm_a.act_evacuate(act)
                for n in range(0, NJ, 2):
                    act.wait_ge(s_pj, n + 1)
                    act.activation(jobs_a[n][3], PS[:, 2 + n % 6, :], ACT.Copy).then_inc(s_pja, 1)
                cross0.act(act, link, lambda e: (e.wait_ge(s_pja, NJ // 2), e.wait_ge(s_pjd, NJ // 2)))
                for t in range(NT):
                    if t >= 1:
                        act.wait_ge(s_hms, t)
                    act.activation(sqs, proj[:, t, 0:2 * SBW], ACT.Square).then_inc(s_hsq, 1)
                    act.wait_ge(s_hms, t + 1)
                    link(act.activation(hst[:, t, 1, :], hst[:, t, 1, :], ACT.Ln))
                    act.activation(hst[:, t, 1, :], hst[:, t, 1, :], ACT.Exp, scale=-0.5).then_inc(s_hrs, 1)
                act.wait_ge(s_g8, 1)
                cross0.act_evacuate(act)
                for j in range(NHJ):
                    act.wait_ge(s_ht, 2 * j + 1)
                    act.activation(qT[:, 2 * j:2 * j + 2, :], PS[0:HD, 4 + (2 * j) % 4, :].rearrange("p (h t) -> p h t", h=2),
                                   ACT.Copy, scale=gcol[:, 5:6]).then_inc(s_hta, 1)

            @block.vector
            def _(dve):
                link = linker(dve, "dve")
                dve.wait_ge(s_gain, 32)
                norm_a.dve_rows(dve)
                for n in range(1, NJ, 2):
                    dve.wait_ge(s_pj, n + 1)
                    dve.tensor_copy(jobs_a[n][3], PS[:, 2 + n % 6, :]).then_inc(s_pjd, 1)
                dve.wait_ge(s_gcol, 64)
                for src, dst in ((2, 4), (0, 5)):
                    g = dve.tensor_scalar(gcol[:, dst:dst + 1], gcol[:, src:src + 1], HD ** -0.5, None, ALU.mult)
                g.then_inc(s_g8, 1)
                cross0.dve(dve, link, lambda e: e.wait_ge(s_pja, NJ // 2))
                for t in range(NT):
                    dve.wait_ge(s_hsq, t + 1)
                    link(dve.tensor_reduce(hst[:, t, 0, :], sqs.rearrange("p (h d) -> p h d", d=HD), X_AXIS, ALU.add))
                    dve.tensor_scalar(hst[:, t, 1, :], hst[:, t, 0, :], 1.0 / HD, EPS, ALU.mult, ALU.add).then_inc(s_hms, 1)
                    dve.wait_ge(s_hrs, t + 1)
                    w = proj[:, t, 0:2 * SBW].rearrange("p (h d) -> p h d", d=HD)
                    dve.tensor_tensor(w, w, hst[:, t, 1, :].unsqueeze(2).to_broadcast([P, 2 * SBH, HD]),
                                      ALU.mult).then_inc(s_hn, 1)
                for j in range(NHJ):
                    dve.wait_ge(s_ht, 2 * j + 2)
                    dve.tensor_scalar(kT[:, 2 * j:2 * j + 2, :], PS[0:HD, 4 + (2 * j + 1) % 4, :].rearrange("p (h t) -> p h t", h=2),
                                      gcol[:, 1:2], None, ALU.mult).then_inc(s_htd, 1)

            @block.tensor
            def _(pe):
                pe.wait_ge(s_const, 2)
                norm_a.pe(pe)
                for n, (rows, load, t, dst) in enumerate(jobs_a):
                    if rows is memT:
                        norm_a.ready(pe, 2)
                    else:
                        norm_a.ready(pe, 4)
                    w = weights_in(pe, load)
                    if n >= 6:
                        pe.wait_ge(s_pja if n % 2 == 0 else s_pjd, (n - 6) // 2 + 1)
                    for k in range(KC):
                        mm = pe.matmul(PS[:, 2 + n % 6, :], rows[:, k, t * P:(t + 1) * P], w[:, k, :],
                                       start=(k == 0), stop=(k == KC - 1))
                    mm.then_inc(s_pj, 1)
                cross0.pe(pe, lambda e, j: (e.wait_ge(s_pja, NJ // 2), e.wait_ge(s_pjd, NJ // 2)) if j == 0 else None)
                for j in range(2 * NHJ):
                    pe.wait_ge(s_hn, NT)
                    if j >= 4:
                        pe.wait_ge(s_hta if j % 2 == 0 else s_htd, (j - 4) // 2 + 1)
                    base = (j % 2) * SBW
                    for i in range(2):
                        h = 2 * (j // 2) + i
                        for t in range(NT):
                            mm = pe.transpose(PS[0:HD, 4 + j % 4, (i * NT + t) * P:(i * NT + t + 1) * P],
                                              proj[:, t, base + h * HD:base + (h + 1) * HD], ident[:])
                    mm.then_inc(s_ht, 1)

        s_z, s_ab, s_ex, s_ln, s_Lr, s_L, s_cum, s_a, s_o, s_oe = (
            lsem(f"b_{n}") for n in ("z", "abs", "exp", "ln", "Lraw", "L", "cum", "a", "o", "o_out"))
        xa0 = Cross("xa0", xqT, xkT, kv_tok[:, :, XAW:2 * XAW], mix, SBW, xtmp)
        op0 = OutProjection("op0", mix, [aslot(N0 - 2, 512), aslot(N0 - 1, 512)], lambda pe, half: weights_in(pe, N0 - 2 + half))
        v_tok = proj[:, :, 2 * SBW:3 * SBW]

        with nc.Block() as block:
            @block.tensor
            def _(pe):
                pe.wait_ge(s_const2, 5)
                for i in range(SBH + 2):
                    if i < SBH:
                        z = PS[:, i % 3, :]
                        if i >= 3:
                            pe.wait_ge(s_a, i - 2)
                        pe.matmul(z[:, 0:S], kT[:, i, 0:P], qT[:, i, :], start=True, stop=True, skip_group_check=True)
                        pe.matmul(z[:, S:S + P], kT[:, i, P:S], qT[:, i, P:S], start=False, stop=True,
                                  skip_group_check=True).then_inc(s_z, 1)
                    if 1 <= i <= SBH:
                        j = i - 1
                        z, L = PS[:, j % 3, :], hL[:, j % 2, :]
                        pe.wait_ge(s_L, j + 1)
                        for o, w, r in ((z[:, 0:S], negup, L[:, 0:S]), (z[:, P:S], negones, L[:, S:S + P]),
                                        (z[:, S:S + P], negup, L[:, S:S + P]), (z[:, 0:P], ident[:], diagneg),
                                        (z[:, S:S + P], ident[:], diagneg)):
                            mm = pe.matmul(o, w, r, start=False, stop=True, skip_group_check=True)
                        mm.then_inc(s_cum, 1)
                    if i >= 2:
                        j = i - 2
                        pe.wait_ge(s_a, j + 1)
                        if j >= 2:
                            pe.wait_ge(s_oe, j - 1)
                        o, A = PS[:, 3 + j % 2, :], hA[:, j % 2, :]
                        vh = slice(j * HD, (j + 1) * HD)
                        pe.matmul(o[:, 0:HD], A[:, 0:P], v_tok[:, 0, vh], start=True, stop=True)
                        pe.matmul(o[:, HD:2 * HD], A[:, P:S], v_tok[:, 0, vh], start=True, stop=False)
                        pe.matmul(o[:, HD:2 * HD], A[:, S:S + P], v_tok[:, 1, vh], start=False, stop=True).then_inc(s_o, 1)
                xa0.pe(pe, lambda e: (e.wait_ge(s_a, SBH), e.wait_ge(s_oe, SBH)))
                op0.pe(pe, lambda e: (e.wait_ge(xa0.s_mix, 2 * XAH), e.wait_ge(s_oe, SBH)))

            @block.scalar
            def _(act):
                for i in range(SBH + 1):
                    if i < SBH:
                        act.wait_ge(s_z, i + 1)
                        if i >= 2:
                            act.wait_ge(s_Lr, i - 1)
                        act.activation(habs[:, i % 2, :], PS[:, i % 3, 0:384], ACT.Abs).then_inc(s_ab, 1)
                        act.wait_ge(s_ab, i + 1)
                        act.activation(habs[:, i % 2, :], habs[:, i % 2, :], ACT.Exp, scale=-1.0).then_inc(s_ex, 1)
                        act.wait_ge(s_ex, i + 1)
                        act.activation(hln[:, i % 2, :], habs[:, i % 2, :], ACT.Ln, bias=1.0).then_inc(s_ln, 1)
                    if i >= 1:
                        j = i - 1
                        act.wait_ge(s_cum, j + 1)
                        if j >= 2:
                            act.wait_ge(s_o, j - 1)
                        act.activation(hA[:, j % 2, :], PS[:, j % 3, 0:384], ACT.Exp).then_inc(s_a, 1)
                xa0.act(act)
                op0.act(act)

            @block.vector
            def _(dve):
                for i in range(SBH + 2):
                    if i < SBH:
                        dve.wait_ge(s_ln, i + 1)
                        if i >= 2:
                            dve.wait_ge(s_cum, i - 1)
                        dve.scalar_tensor_tensor(out=hL[:, i % 2, :], in0=PS[:, i % 3, 0:384], scalar=0.0, in1=hln[:, i % 2, :],
                                                 op0=ALU.max, op1=ALU.add).then_inc(s_Lr, 1)
                        dve.wait_ge(s_Lr, i + 1)
                        dve.tensor_tensor(hL[:, i % 2, :], hL[:, i % 2, :], diag0.rearrange("p a b -> p (a b)"),
                                          ALU.mult).then_inc(s_L, 1)
                    if i >= 2:
                        j = i - 2
                        dve.wait_ge(s_o, j + 1)
                        dve.tensor_copy(mix[:, :, j * HD:(j + 1) * HD],
                                        PS[:, 3 + j % 2, 0:2 * HD].rearrange("p (t d) -> p t d", t=NT)).then_inc(s_oe, 1)
                xa0.dve(dve)
                op0.dve(dve)

            @block.sync
            def _(sp):
                sp.dma_start(gain[:, 0, :], row(ffn_norm[0], D)).then_inc(s_gain_ffn0, 16)

        s_w = [sem(f"s_w{i}") for i in range(STAGES)]
        NB = GF // P
        GPP = 3 * NG
        GATE, UP, DOWN = range(3)

        def part_no(n, g, kind):
            return GPP * n + 3 * g + (kind if kind != DOWN else 2 + 6)

        def stage_of(g, kind):
            return part_no(0, g, kind) % STAGES

        def landed(eng, n, g, kind):
            at = part_no(0, g, kind)
            uses = at // STAGES + (0 if at % STAGES in (2, 5) else 1)
            eng.wait_ge(s_w[at % STAGES], 16 * (n * (GPP // STAGES) + uses))

        def split_no(g, kind, alone, last):
            if kind == DOWN:
                return 3 * g + 7 if g < NG - 2 or not last else GPP - (NG - 1 - g)
            if g >= 2:
                return 3 * g - 1 + kind
            return (2 * g + kind + 1) if alone else 3 * g - 1 + kind

        def staged(g, kind):
            return stage[:, stage_of(g, kind), :]

        def load_part(eng, w, g, kind):
            if kind == DOWN:
                src = w[DOWN].rearrange("(g b p) d -> g p b d", b=NB, p=P)[g]
                dst = staged(g, kind).rearrange("p (b d) -> p b d", b=NB)
            else:
                src = k_rows(w[kind])[:, :, g * GF:(g + 1) * GF]
                dst = staged(g, kind).rearrange("p (c f) -> p c f", c=KC)
            eng.dma_start(dst, src).then_inc(s_w[stage_of(g, kind)], 16)

        def reload_part(eng, n, w, g, kind, alone, first=False):
            before = part_no(0, g, kind) - STAGES
            if before >= 0 and before not in (2, 5):
                k = before % 3
                bg = before // 3 if k != DOWN else (before - 8) // 3
                eng.wait_ge(s_lo[0], GPP * n + split_no(bg, k, alone, False))
            elif not alone:
                eng.wait_ge(s_lo[0], GPP * n + before - 1)
            elif not first:
                eng.wait_ge(s_lo[0], GPP * n)
            load_part(eng, w, g, kind)

        def split_views(g, kind):
            if kind == DOWN:
                return (staged(g, kind), wdh[:, g % 2, :], wdl[:, g % 2, :])
            return (staged(g, kind).rearrange("p (c f) -> p c f", c=KC), wgh[:, g % 2, :, kind, :], wgl[:, g % 2, :, kind, :])

        def act_high(act, n, g, kind, signal):
            landed(act, n, g, kind)
            src, hi, lo = split_views(g, kind)
            act.activation(hi, src, ACT.Copy).then_inc(signal, 1)

        def dve_rest(dve, g, kind, signal):
            src, hi, lo = split_views(g, kind)
            dve.tensor_tensor(lo, src, hi.bitcast(F32), ALU.subtract).then_inc(signal, 1)

        def three_passes(pe, out, left, right, start, stop):
            pe.matmul(out, left[0], right[0], start=start, stop=False)
            pe.matmul(out, left[0], right[1], start=False, stop=False)
            return pe.matmul(out, left[1], right[0], start=False, stop=stop)

        def feed_forward_memory(tag):
            next_memory()
            return (psb(f"stage{tag}", [P, STAGES, PART]),
                    psb(f"wgh{tag}", [P, 2, KC, 2, GF], F32R), psb(f"wgl{tag}", [P, 2, KC, 2, GF], F32R),
                    psb(f"wdh{tag}", [P, 2, NB * D], F32R), psb(f"wdl{tag}", [P, 2, NB * D], F32R))

        stage, wgh, wgl, wdh, wdl = feed_forward_memory(0)
        hTh, hTl = psb("hTh", [P, KC, S], F32R), psb("hTl", [P, KC, S], F32R)
        hh, hl = psb("hh0", [P, 2, NB, S], F32R), psb("hl0", [P, 2, NB, S], F32R)
        sg = xn[:, 0, :].rearrange("p (i b t) -> p i b t", i=2, b=NB)
        hm = xn[:, 1, :].rearrange("p (i b t) -> p i b t", i=2, b=NB)
        norm_c = NormTransposeSplit("nc", [(X[:, t, :], gain[:, 0, :], (hTh[:, :, t * P:(t + 1) * P], hTl[:, :, t * P:(t + 1) * P]),
                                            (s_gain_ffn0, 16)) for t in range(NT)])
        c_hi, c_lo, c_gu, c_sg, c_hm, c_hh, c_hl, c_dn, c_x = (
            lsem(f"c_{n}") for n in ("hi", "lo", "gu", "silu", "hm", "hh", "hl", "down", "x"))
        s_lo = [c_lo]
        dense_w = (ffd_w_gate[0], ffd_w_up[0], ffd_w_down[0])

        def steps_parts(g):
            return [(g + 2, GATE), (g + 2, UP)] * (g + 2 < NG) + [(g, DOWN)]

        FIRST_PARTS = [(0, GATE), (0, UP), (1, GATE), (1, UP)]

        with nc.Block() as block:
            @block.sync
            def _(sp):
                for g, kind in FIRST_PARTS:
                    load_part(sp, dense_w, g, kind)
                for g in range(NG):
                    for pg, kind in steps_parts(g):
                        reload_part(sp, 0, dense_w, pg, kind, True, first=True)
                sp.dma_start(gain[:, 1, :], row(mem_norm[1], D)).then_inc(s_gain_mem1, 16)

            @block.scalar
            def _(act):
                link = linker(act, "act")
                norm_c.act_squares(act, link)
                norm_c.act_rstd(act, link)
                for g, kind in FIRST_PARTS[:2]:
                    act_high(act, 0, g, kind, c_hi)
                norm_c.act_evacuate(act)
                for g, kind in FIRST_PARTS[2:]:
                    act_high(act, 0, g, kind, c_hi)
                for g in range(NG):
                    act.wait_ge(c_gu, g + 1)
                    if g >= 2:
                        act.wait_ge(c_hm, g - 1)
                    act.activation(sg[:, g % 2], PS[:, 2 * (g % 2):2 * (g % 2) + 2, 0:S], ACT.Silu).then_inc(c_sg, 1)
                    for pg, kind in steps_parts(g):
                        if kind == DOWN:
                            act.wait_ge(c_hm, g + 1)
                            if g >= 2:
                                act.wait_ge(c_dn, g - 1)
                            act.activation(hh[:, g % 2], hm[:, g % 2], ACT.Copy).then_inc(c_hh, 1)
                        act_high(act, 0, pg, kind, c_hi)

            @block.vector
            def _(dve):
                norm_c.dve_rows(dve)
                done = 0
                for g, kind in FIRST_PARTS:
                    done += 1
                    dve.wait_ge(c_hi, done)
                    dve_rest(dve, g, kind, c_lo)
                for g in range(NG):
                    dve.wait_ge(c_sg, g + 1)
                    if g >= 2:
                        dve.wait_ge(c_hl, g - 1)
                    dve.tensor_tensor(hm[:, g % 2], sg[:, g % 2], PS[:, 2 * (g % 2):2 * (g % 2) + 2, S:2 * S], ALU.mult).then_inc(c_hm, 1)
                    for pg, kind in steps_parts(g):
                        if kind == DOWN:
                            dve.wait_ge(c_hh, g + 1)
                            dve.tensor_tensor(hl[:, g % 2], hm[:, g % 2], hh[:, g % 2].bitcast(F32), ALU.subtract).then_inc(c_hl, 1)
                        done += 1
                        dve.wait_ge(c_hi, done)
                        dve_rest(dve, pg, kind, c_lo)
                dve.wait_ge(c_dn, NG)
                for t in range(NT):
                    xv = X[:, t, :].rearrange("p (a n) -> p a n", a=2)
                    dve.tensor_tensor(xv, xv, PS[:, 4 + 2 * t:6 + 2 * t, :], ALU.add).then_inc(c_x, 1)

            @block.tensor
            def _(pe):
                norm_c.pe(pe)
                norm_c.ready(pe, NT)
                for g in range(NG + 1):
                    if g < NG:
                        pe.wait_ge(c_lo, split_no(g, UP, True, True))
                        if g >= 2:
                            pe.wait_ge(c_hm, g - 1)
                        for b in range(NB):
                            bs = slice(b * P, (b + 1) * P)
                            for kind in (GATE, UP):
                                for k in range(KC):
                                    mm = three_passes(pe, PS[:, 2 * (g % 2) + b, kind * S:(kind + 1) * S],
                                                      (wgh[:, g % 2, k, kind, bs], wgl[:, g % 2, k, kind, bs]),
                                                      (hTh[:, k, :], hTl[:, k, :]), k == 0, k == KC - 1)
                        mm.then_inc(c_gu, 1)
                    if g >= 1:
                        j = g - 1
                        pe.wait_ge(c_hl, j + 1)
                        pe.wait_ge(c_lo, split_no(j, DOWN, True, True))
                        for b in range(NB):
                            for t in range(NT):
                                ts = slice(t * P, (t + 1) * P)
                                for half in range(2):
                                    ws = slice(b * D + half * 512, b * D + (half + 1) * 512)
                                    mm = three_passes(pe, PS[:, 4 + 2 * t + half, :], (hh[:, j % 2, b, ts], hl[:, j % 2, b, ts]),
                                                      (wdh[:, j % 2, ws], wdl[:, j % 2, ws]), j == 0 and b == 0, j == NG - 1 and b == NB - 1)
                        mm.then_inc(c_dn, 1)

        next_layer()
        next_memory()
        hT = psb("hT1", [P, KC, S])
        ring = psb("ring1", [P, ARENA])
        NCH = 3 * DNW // P
        CT_ = 4
        NP_ = NT * DNH
        sd = Scratch()
        qkvT = sd.tile(P, NCH, S)
        gate = sd.tile(P, NT, DNW)
        last = sd.tile(P, NT, 2 * DNH + XAW)
        kv1 = sd.tile(P, NT, 2 * XAW)
        xqT1 = sd.tile(HD, XAH, S)
        xkT1 = sd.tile(HD, XAH, S)
        mix1 = sd.tile(P, NT, D)
        convr = sd.tile(CT_ * NCH, P)
        convw = sd.tile(P, CT_ * NCH)
        alog = sd.tile(P, DNH)
        dtb = sd.tile(P, DNH)
        ogain = sd.tile(P, P)
        gcol1 = sd.tile(HD, 4)
        lowstrict = sd.tile(P, P)
        mask1 = sd.tile(P, P)
        SOLVE = 7
        maskT = sd.tile(P, SOLVE, P)
        tk = sd.tile(P, 12, NP_)
        on = sd.tile(P, 3, NP_)
        xtmp1 = (sd.tile(P, 2, S), sd.tile(P, 2, S), sd.tile(P, 3, 8))
        xst1 = sd.tile(P, 2, NT * 2 * XAH)
        e_at = sd.at
        memr1 = sd.tile(P, NT, D)
        memT1 = sd.tile(P, KC, S)
        yconv = sd.tile(P, 2, S)

        norm_d = NormTranspose("nd", [
            (memr1[:, 0, :], gain[:, 1, :], memT1[:, :, 0:P], None),
            (memr1[:, 1, :], gain[:, 1, :], memT1[:, :, P:S], None),
            (X[:, 0, :], gain[:, 0, :], hT[:, :, 0:P], None),
            (X[:, 1, :], gain[:, 0, :], hT[:, :, P:S], None)])
        s_mem1, s_small = lsem("s_mem1"), lsem("s_small")
        norm_d.units = [(a, b, c, (s_mem1, 16)) for i, (a, b, c, _) in enumerate(norm_d.units)]
        s_cwt, s_cw, s_cv, s_y0, s_y1, s_y2, s_yc, s_si, s_tok, s_toke, s_mask = (
            lsem(f"d_{n}") for n in ("cwt", "cw", "cv", "y0", "y1", "y2", "y", "silu", "tok", "tok_out", "mask"))
        jobs_d = [(memT1, N0, t, kv1[:, t, :], 512, ACT.Copy) for t in range(NT)] + \
                 [(hT, N0 + 7 + c, t, gate[:, t, c * QK:(c + 1) * QK], QK, ACT.Silu) for c in range(2) for t in range(NT)] + \
                 [(hT, N0 + 9, t, last[:, t, :], DN_IN - 4 * DNW, ACT.Copy) for t in range(NT)]
        NTJ = len(jobs_d)
        CPL = QK // P
        op1 = OutProjection("op1", mix1, [aslot(len(loads) - 2, 512), aslot(len(loads) - 1, 512)],
                            lambda pe, half: weights_in(pe, len(loads) - 2 + half))
        load_read[N0 - ASLOTS:] = [None] * (N0 - len(load_read[:N0 - ASLOTS]))
        load_read += [(s_tok, NT)] + \
                     [(s_cv, CPL * (i + 1)) for i in range(6)] + [(s_tok, NT * (i + 2)) for i in range(3)]

        with nc.Block() as block:
            @block.sync
            def _(sp):
                sp.dma_start(memr1, mem[0].rearrange("(t p) d -> p t d", p=P)).then_inc(s_mem1, 16)
                sp.dma_start(gain[:, 0, :], row(mix_norm[1], D)).then_inc(s_gain_mix1, 16)
                sp.dma_start(convr, dn_conv[0].rearrange("j (c p) -> (j c) p", p=P)).then_inc(s_small, 16)
                sp.dma_start(alog, row(dn_a_log[0], DNH)).then_inc(s_small, 16)
                sp.dma_start(dtb, row(dn_dt_bias[0], DNH)).then_inc(s_small, 16)
                sp.dma_start(ogain, row(dn_o_norm[0], P)).then_inc(s_small, 16)
                for i, g in enumerate((xa_q_norm[1], xa_k_norm[1])):
                    sp.dma_start(gcol1[:, i:i + 1], col(g)).then_inc(s_small, 16)
                attention_loads(sp, N0, len(loads), N0)

            @block.gpsimd
            def _(pool):
                link = linker(pool, "pool")
                pool.affine_select(out=lowstrict, in_=ones[:], compare_op=ALU.is_gt, fill=0.0, base=0,
                                   pattern=[[-1, P]], channel_multiplier=1).then_inc(s_mask, 1)
                link(pool.memset(maskT.rearrange("p a b -> p (a b)"), 0.0))
                link(pool.memset(mask1, 0.0))
                pool.affine_select(out=mask1.rearrange("p (a h) -> p a h", h=2)[:, :, 0], in_=mask1.rearrange("p (a h) -> p a h", h=2)[:, :, 0],
                                   compare_op=ALU.not_equal, fill=1.0, base=-1, pattern=[[-2, P // 2]],
                                   channel_multiplier=1).then_inc(s_mask, 1)
                for i in range(SOLVE):
                    s = 1 << i
                    v = maskT[:, i, :].rearrange("p (a h b) -> p a h b", h=2, b=s)[:, :, 1, :]
                    link(pool.memset(v, 1.0))
                    link(pool.affine_select(out=v, in_=v, compare_op=ALU.is_ge, fill=0.0, base=0,
                                            pattern=[[-2 * s, P // (2 * s)], [0, s]], channel_multiplier=1))
                    pool.affine_select(out=v, in_=v, compare_op=ALU.is_ge, fill=0.0, base=s - 1,
                                       pattern=[[2 * s, P // (2 * s)], [0, s]], channel_multiplier=-1).then_inc(s_mask, 1)

            @block.scalar
            def _(act):
                link = linker(act, "act")
                act.preload_act_table_set("natural_log_exp_and_others")
                norm_d.act_squares(act, link)
                norm_d.act_rstd(act, link)
                norm_d.act_evacuate(act)

                def token_job(n):
                    rows, load, t, dst, cols, f = jobs_d[n]
                    act.wait_ge(s_tok, n + 1)
                    act.activation(dst, PS[:, 5 + n % 3, 0:cols], f).then_inc(s_toke, 1)

                for n in range(NT):
                    token_job(n)
                for c in range(NCH):
                    act.wait_ge(s_yc, c + 1)
                    act.activation(qkvT[:, c, :], yconv[:, c % 2, :], ACT.Silu).then_inc(s_si, 1)
                for n in range(NT, NTJ):
                    token_job(n)

            @block.vector
            def _(dve):
                dve.wait_ge(s_gain_mem1, 16)
                dve.wait_ge(s_gain_mix1, 16)
                norm_d.dve_rows(dve)
                dve.wait_ge(s_cwt, 1)
                dve.tensor_copy(convw, PS[:, 7, 0:CT_ * NCH]).then_inc(s_cw, 1)
                dve.wait_ge(s_cw, 1)
                for c in range(NCH):
                    dve.wait_ge(s_cv, c + 1)
                    if c >= 2:
                        dve.wait_ge(s_si, c - 1)
                    xp, y = PS[:, 2 + c % 3, 0:S], yconv[:, c % 2, :]

                    def tap(j):
                        return convw[:, j * NCH + c:j * NCH + c + 1]
                    dve.tensor_scalar(y, xp, tap(3), None, ALU.mult).then_inc(s_y0, 1)
                    for back, before, after in ((1, s_y0, s_y1), (2, s_y1, s_y2), (3, s_y2, s_yc)):
                        dve.wait_ge(before, c + 1)
                        dve.scalar_tensor_tensor(out=y[:, back:S], in0=xp[:, 0:S - back], scalar=tap(3 - back),
                                                 in1=y[:, back:S], op0=ALU.mult, op1=ALU.add).then_inc(after, 1)

            @block.tensor
            def _(pe):
                norm_d.pe(pe)
                pe.wait_ge(s_small, 96)
                pe.transpose(PS[:, 7, 0:CT_ * NCH], convr, ident[0:CT_ * NCH, 0:CT_ * NCH]).then_inc(s_cwt, 1)

                def token_job(n):
                    rows, load, t, dst, cols, f = jobs_d[n]
                    w = weights_in(pe, load)
                    if n == 2:
                        pe.wait_ge(s_cw, 1)
                    if n >= 3:
                        pe.wait_ge(s_toke, n - 2)
                    for k in range(KC):
                        mm = pe.matmul(PS[:, 5 + n % 3, 0:cols], rows[:, k, t * P:(t + 1) * P], w[:, k, :],
                                       start=(k == 0), stop=(k == KC - 1))
                    mm.then_inc(s_tok, 1)

                norm_d.ready(pe, 4)
                for n in range(NT):
                    token_job(n)
                for c in range(NCH):
                    w = weights_in(pe, N0 + 1 + c // CPL)
                    if c >= 3:
                        pe.wait_ge(s_yc, c - 2)
                    for k in range(KC):
                        mm = pe.matmul(PS[:, 2 + c % 3, 0:S], w[:, k, (c % CPL) * P:(c % CPL + 1) * P], hT[:, k, :],
                                       start=(k == 0), stop=(k == KC - 1))
                    mm.then_inc(s_cv, 1)
                for n in range(NT, NTJ):
                    token_job(n)

        sd.at = e_at
        vb = sd.tile(P, NP_, P)
        kdec = sd.tile(P, DNH, P)
        nkbg = sd.tile(P, DNH, P)
        qd = sd.tile(P, DNH, P)
        Dm = sd.tile(P, NP_, P)
        DT = sd.tile(P, NP_, P)
        A = sd.tile(P, NP_, P)
        AT = sd.tile(P, NP_, P)
        T = sd.tile(P, NP_, P)
        TT = sd.tile(P, NP_, P)
        W = Dm
        rg = T
        sq2 = TT.rearrange("p a b -> p (a b)")[:, 0:4 * S].rearrange("p (i a b) -> p i a b", i=2, a=2)
        CT = [qkvT[:, 2 * DNH:3 * DNH, :].rearrange("p c (t n) -> p (c t) n", n=P), A]
        U0, St = T[:, 0:DNH, :], T[:, DNH:NP_, :]
        wT, V1, Osb, Osq = W[:, 0:DNH, :], A[:, 0:DNH, :], AT, T
        sqx1 = vb.rearrange("p a b -> p (a b)")[:, 0:NT * 2 * XAW].rearrange("p (t n) -> p t n", t=NT)
        cross1 = CrossPrep("cp1", last[:, :, 2 * DNH:], kv1, xqT1, xkT1, sqx1, xst1, gcol1[:, 2:3], gcol1[:, 1:2], (6, 7, 6, 7))
        xa1 = Cross("xa1", xqT1, xkT1, kv1[:, :, XAW:2 * XAW], mix1, DNW, xtmp1)
        PQ = 4
        NQ = NP_ // PQ
        e = {n: lsem(f"e_{n}") for n in (
            "g8", "xa", "abs", "exp", "ln", "alog", "eb", "g", "beta", "rg", "gc", "gcs", "egc", "kdarg", "kd", "nb",
            "G", "Darg", "Dexp", "egr", "Dmask", "DTmask", "sq", "sum", "lnr", "r", "qn", "kn", "qd",
            "tr", "vb", "kt", "KK", "KQ", "A", "qk", "At", "AT", "T0", "TT0", "CT", "W", "We", "PP", "Tn", "TTn",
            "U", "Ue", "S", "Se", "wT", "wTe", "V", "Ve", "O", "Oe", "osq", "oms", "ors", "gg", "o1", "mix")}

        def banks4(b):
            return PS[:, b, :].rearrange("p (a n) -> p a n", a=PQ)

        def trio(v, q):
            return v[:, q * PQ:(q + 1) * PQ, :]

        with nc.Block() as block:
            @block.scalar
            def _(act):
                link = linker(act, "act")
                act.preload_act_table_set("natural_log_exp_and_others")
                act.wait_ge(e["xa"], 1)
                act.activation(tk[:, 1, :], tk[:, 0, :], ACT.Abs).then_inc(e["abs"], 1)
                act.wait_ge(e["abs"], 1)
                act.activation(tk[:, 1, :], tk[:, 1, :], ACT.Exp, scale=-1.0).then_inc(e["exp"], 1)
                act.wait_ge(e["exp"], 1)
                act.activation(tk[:, 1, :], tk[:, 1, :], ACT.Ln, bias=1.0).then_inc(e["ln"], 1)
                act.activation(alog, alog, ACT.Exp).then_inc(e["alog"], 1)
                act.activation(tk[:, 3, :].rearrange("p (t h) -> p t h", t=NT), last[:, :, DNH:2 * DNH], ACT.Exp,
                               scale=-1.0).then_inc(e["eb"], 1)
                for h in range(DNH):
                    if h >= 2:
                        act.wait_ge(e["kn"], h - 1)
                    act.activation(sq2[:, h % 2], qkvT[:, h:h + DNH + 1:DNH, :], ACT.Square).then_inc(e["sq"], 1)
                    act.wait_ge(e["sum"], h + 1)
                    act.activation(sq2[:, h % 2], PS[:, 3 + h % 2, :].rearrange("p (a b) -> p a b", a=2), ACT.Ln,
                                   bias=epsc[:]).then_inc(e["lnr"], 1)
                    act.wait_ge(e["lnr"], h + 1)
                    act.activation(sq2[:, h % 2], sq2[:, h % 2], ACT.Exp, scale=-0.5).then_inc(e["r"], 1)
                act.wait_ge(e["gcs"], 1)
                act.activation(tk[:, 6, :], tk[:, 5, :], ACT.Exp).then_inc(e["egc"], 1)
                act.wait_ge(e["kdarg"], 1)
                act.activation(tk[:, 8, :], tk[:, 8, :], ACT.Exp).then_inc(e["kd"], 1)
                act.wait_ge(e["Darg"], 2 * NP_)
                act.activation(DT, DT, ACT.Exp).then_inc(e["Dexp"], 1)
                act.activation(Dm, Dm, ACT.Exp, scale=-1.0).then_inc(e["Dexp"], 1)
                act.activation(qd[:, 0:2, :], banks4(1)[:, 2:4, :], ACT.Exp).then_inc(e["egr"], 1)
                act.activation(qd[:, 2:6, :], banks4(2), ACT.Exp).then_inc(e["egr"], 1)
                for q in range(NQ):
                    act.wait_ge(e["tr"], q + 1)
                    if q == 0:
                        act.wait_ge(e["beta"], 1)
                    for i in range(PQ):
                        p = q * PQ + i
                        act.activation(vb[:, p, :], banks4(5 + q)[:, i, :], ACT.Copy, scale=tk[:, 4, p:p + 1]).then_inc(e["vb"], 1)
                for q in range(NQ):
                    act.wait_ge(e["At"], q + 1)
                    act.activation(trio(AT, q), banks4(5 + q), ACT.Copy).then_inc(e["AT"], 1)
                for j in range((SOLVE - 1) * NQ):
                    act.wait_ge(e["W"], j + 1)
                    act.activation(trio(W, j % NQ), banks4(j % 2), ACT.Copy).then_inc(e["We"], 1)
                act.wait_ge(e["U"], 1)
                act.activation(U0[:, 0:4, :], banks4(0), ACT.Copy).then_inc(e["Ue"], 1)
                act.activation(U0[:, 4:6, :], banks4(1)[:, 0:2, :], ACT.Copy).then_inc(e["Ue"], 1)
                act.wait_ge(e["S"], 1)
                act.activation(St[:, 0:4, :], banks4(4), ACT.Copy).then_inc(e["Se"], 1)
                act.activation(St[:, 4:6, :], banks4(5)[:, 0:2, :], ACT.Copy).then_inc(e["Se"], 1)
                act.wait_ge(e["V"], 1)
                act.activation(V1[:, 0:4, :], banks4(0), ACT.Copy).then_inc(e["Ve"], 1)
                act.activation(V1[:, 4:6, :], banks4(1)[:, 0:2, :], ACT.Copy).then_inc(e["Ve"], 1)
                for t, b in ((0, 6), (1, 2)):
                    act.wait_ge(e["O"], t + 1)
                    act.activation(Osb[:, t * DNH:t * DNH + 4, :], banks4(b), ACT.Copy).then_inc(e["Oe"], 1)
                    act.activation(Osb[:, t * DNH + 4:t * DNH + 6, :], banks4(b + 1)[:, 0:2, :], ACT.Copy).then_inc(e["Oe"], 1)
                act.wait_ge(e["Oe"], 4)
                act.activation(Osq, Osb, ACT.Square).then_inc(e["osq"], 1)
                act.wait_ge(e["oms"], 1)
                link(act.activation(on[:, 1, :], on[:, 1, :], ACT.Ln))
                act.activation(on[:, 1, :], on[:, 1, :], ACT.Exp, scale=-0.5).then_inc(e["ors"], 1)
                cross1.act(act, link, lambda eng: eng.wait_ge(s_toke, NTJ))
                act.wait_ge(e["g8"], 1)
                cross1.act_evacuate(act)
                xa1.act(act)
                op1.act(act)

            @block.gpsimd
            def _(pool):
                pool.wait_ge(e["Dexp"], 2)
                pool.tensor_tensor(DT, DT, upincl[:].unsqueeze(1).to_broadcast([P, NP_, P]), ALU.mult).then_inc(e["DTmask"], 1)
                gv = gate.rearrange("p t (h d) -> p (t h) d", d=P)
                pool.tensor_tensor(gv, gv, ogain.unsqueeze(1).to_broadcast([P, NP_, P]), ALU.mult).then_inc(e["gg"], 1)
                pool.wait_ge(e["vb"], NP_)
                for i in range(1, SOLVE):
                    pool.wait_ge(e["AT"], NQ)
                    if i == 2:
                        pool.wait_ge(e["T0"], 1)
                    if i >= 3:
                        pool.wait_ge(e["W"], NQ * (i - 2))
                    pool.tensor_tensor(CT[(i - 1) % 2], AT, maskT[:, i, :].unsqueeze(1).to_broadcast([P, NP_, P]),
                                       ALU.mult).then_inc(e["CT"], 1)

            @block.vector
            def _(dve):
                link = linker(dve, "dve")

                def th(v):
                    return v.rearrange("p (t h) -> p t h", t=NT)

                dve.tensor_scalar(gcol1[:, 2:3], gcol1[:, 0:1], HD ** -0.5, None, ALU.mult).then_inc(e["g8"], 1)
                dve.tensor_tensor(th(tk[:, 0, :]), last[:, :, 0:DNH], dtb.unsqueeze(1).to_broadcast([P, NT, DNH]), ALU.add).then_inc(e["xa"], 1)
                dve.wait_ge(e["ln"], 1)
                link(dve.scalar_tensor_tensor(out=tk[:, 2, :], in0=tk[:, 0, :], scalar=0.0, in1=tk[:, 1, :], op0=ALU.max, op1=ALU.add))
                dve.wait_ge(e["alog"], 1)
                dve.scalar_tensor_tensor(out=th(tk[:, 2, :]), in0=th(tk[:, 2, :]), scalar=-1.0,
                                         in1=alog.unsqueeze(1).to_broadcast([P, NT, DNH]), op0=ALU.mult, op1=ALU.mult).then_inc(e["g"], 1)
                dve.wait_ge(e["eb"], 1)
                link(dve.tensor_scalar(tk[:, 3, :], tk[:, 3, :], 1.0, None, ALU.add))
                dve.reciprocal(tk[:, 4, :], tk[:, 3, :]).then_inc(e["beta"], 1)
                dve.wait_ge(e["g"], 1)
                for p in range(NP_):
                    dve.tensor_scalar(rg[:, p, :], upincl[:], tk[:, 2, p:p + 1], None, ALU.mult).then_inc(e["rg"], 1)
                dve.wait_ge(e["gc"], 1)
                dve.tensor_copy(tk[:, 5:8:2, :], PS[:, 7, 0:2 * NP_].rearrange("p (a n) -> p a n", a=2)).then_inc(e["gcs"], 1)
                dve.wait_ge(e["gcs"], 1)
                dve.tensor_tensor(tk[:, 8, :], tk[:, 7, :], tk[:, 5, :], ALU.subtract).then_inc(e["kdarg"], 1)
                for p in range(NP_):
                    if p % PQ == 0:
                        dve.wait_ge(e["G"], p // PQ + 1)
                    gp = banks4(p // PQ)[:, p % PQ, :]
                    dve.tensor_scalar(DT[:, p, :], gp, tk[:, 5, p:p + 1], 0.0, ALU.subtract, ALU.min).then_inc(e["Darg"], 1)
                    dve.tensor_scalar(Dm[:, p, :], gp, tk[:, 5, p:p + 1], 0.0, ALU.subtract, ALU.max).then_inc(e["Darg"], 1)
                for h in range(DNH):
                    dve.wait_ge(e["r"], h + 1)
                    dve.scalar_tensor_tensor(out=qkvT[:, h, :], in0=qkvT[:, h, :], scalar=float(P) ** -0.5, in1=sq2[:, h % 2, 0, :],
                                             op0=ALU.mult, op1=ALU.mult).then_inc(e["qn"], 1)
                    kk = qkvT[:, DNH + h, :]
                    dve.tensor_tensor(kk, kk, sq2[:, h % 2, 1, :], ALU.mult).then_inc(e["kn"], 1)
                dve.wait_ge(e["egc"], 1)
                dve.wait_ge(e["beta"], 1)
                dve.scalar_tensor_tensor(out=tk[:, 9, :], in0=tk[:, 6, :], scalar=-1.0, in1=tk[:, 4, :],
                                         op0=ALU.mult, op1=ALU.mult).then_inc(e["nb"], 1)
                dve.wait_ge(e["Dexp"], 2)
                dve.tensor_tensor(Dm, Dm, lowstrict.unsqueeze(1).to_broadcast([P, NP_, P]), ALU.mult).then_inc(e["Dmask"], 1)
                dve.wait_ge(e["egr"], 2)
                dve.wait_ge(e["qn"], DNH)
                dve.tensor_tensor(qd, qd, qkvT[:, 0:DNH, P:S], ALU.mult).then_inc(e["qd"], 1)
                dve.wait_ge(e["kd"], 1)
                dve.wait_ge(e["nb"], 1)
                for q in range(NQ):
                    dve.wait_ge(e["tr"], NQ + q + 1)
                    for i in range(PQ):
                        p = q * PQ + i
                        src = banks4((3, 4, 0)[q])[:, i, :]
                        if p < DNH:
                            dve.tensor_scalar(kdec[:, p, :], src, tk[:, 8, p:p + 1], None, ALU.mult).then_inc(e["kt"], 1)
                        else:
                            dve.tensor_scalar(nkbg[:, p - DNH, :], src, tk[:, 9, p:p + 1], None, ALU.mult).then_inc(e["kt"], 1)
                dve.wait_ge(e["Dmask"], 1)
                for q in range(NQ):
                    dve.wait_ge(e["KK"], q + 1)
                    for i in range(PQ):
                        p = q * PQ + i
                        dve.scalar_tensor_tensor(out=A[:, p, :], in0=banks4(1 + q)[:, i, :], scalar=tk[:, 4, p:p + 1],
                                                 in1=Dm[:, p, :], op0=ALU.mult, op1=ALU.mult).then_inc(e["A"], 1)
                dve.wait_ge(e["DTmask"], 1)
                for q in range(NQ):
                    dve.wait_ge(e["KQ"], q + 1)
                    dve.tensor_tensor(trio(DT, q), trio(DT, q), banks4((4, 0, 1)[q]), ALU.mult).then_inc(e["qk"], 1)
                dve.wait_ge(s_mask, 2 + SOLVE)
                dve.wait_ge(e["A"], NP_)
                idb = ident[:].unsqueeze(1).to_broadcast([P, NP_, P])
                link(dve.tensor_tensor(T, A, mask1.unsqueeze(1).to_broadcast([P, NP_, P]), ALU.mult))
                dve.tensor_tensor(T, idb, T, ALU.subtract).then_inc(e["T0"], 1)
                dve.wait_ge(e["AT"], NQ)
                link(dve.tensor_tensor(TT, AT, maskT[:, 0, :].unsqueeze(1).to_broadcast([P, NP_, P]), ALU.mult))
                dve.tensor_tensor(TT, idb, TT, ALU.subtract).then_inc(e["TT0"], 1)
                dve.wait_ge(e["T0"], 1)
                dve.wait_ge(e["TT0"], 1)
                for j in range((SOLVE - 1) * NQ):
                    q = j % NQ
                    dve.wait_ge(e["PP"], j + 1)
                    if j < (SOLVE - 2) * NQ:
                        dve.tensor_tensor(trio(T, q), trio(T, q), banks4(2 + q), ALU.subtract).then_inc(e["Tn"], 1)
                    dve.tensor_tensor(trio(TT, q), trio(TT, q), banks4(5 + q), ALU.subtract).then_inc(e["TTn"], 1)
                    if q == NQ - 1:
                        dve.wait_ge(e["TTn"], j + 1)
                        if j < (SOLVE - 2) * NQ:
                            dve.wait_ge(e["Tn"], j + 1)
                dve.wait_ge(e["wT"], 1)
                dve.tensor_copy(wT[:, 0:4, :], banks4(2)).then_inc(e["wTe"], 1)
                dve.tensor_copy(wT[:, 4:6, :], banks4(3)[:, 0:2, :]).then_inc(e["wTe"], 1)
                dve.wait_ge(e["osq"], 1)
                link(dve.tensor_reduce(on[:, 0, :], Osq, X_AXIS, ALU.add))
                dve.tensor_scalar(on[:, 1, :], on[:, 0, :], 1.0 / P, EPS, ALU.mult, ALU.add).then_inc(e["oms"], 1)
                dve.wait_ge(e["ors"], 1)
                dve.tensor_tensor(Osb, Osb, on[:, 1, :].unsqueeze(2).to_broadcast([P, NP_, P]), ALU.mult).then_inc(e["o1"], 1)
                dve.wait_ge(e["o1"], 1)
                dve.wait_ge(e["gg"], 1)
                for t in range(NT):
                    dve.tensor_tensor(mix1[:, t, 0:DNW].rearrange("p (h d) -> p h d", d=P), Osb[:, t * DNH:(t + 1) * DNH, :],
                                      gate[:, t, :].rearrange("p (h d) -> p h d", d=P), ALU.mult).then_inc(e["mix"], 1)
                cross1.dve(dve, link, lambda eng: eng.wait_ge(s_toke, NTJ))
                xa1.dve(dve)
                op1.dve(dve)

            @block.tensor
            def _(pe):
                pe.wait_ge(e["g"], 1)
                pe.matmul(PS[:, 7, 0:NP_], upincl[:], tk[:, 2, :], start=True, stop=True)
                pe.matmul(PS[:, 7, NP_:2 * NP_], ones[:], tk[:, 2, :], start=True, stop=True).then_inc(e["gc"], 1)
                for q in range(NQ):
                    pe.wait_ge(e["rg"], PQ * (q + 1))
                    pe.matmul(PS[:, q, :], ones[:], trio(rg, q), start=True, stop=True).then_inc(e["G"], 1)
                for h in range(DNH):
                    pe.wait_ge(e["sq"], h + 1)
                    if h >= 2:
                        pe.wait_ge(e["r"], h - 1)
                    pe.matmul(PS[:, 3 + h % 2, :], ones[:], sq2[:, h % 2], start=True, stop=True).then_inc(e["sum"], 1)
                pe.wait_ge(e["gcs"], 1)
                for q in range(NQ):
                    for i in range(PQ):
                        t, h = divmod(q * PQ + i, DNH)
                        mm = pe.transpose(banks4(5 + q)[:, i, :], qkvT[:, 2 * DNH + h, t * P:(t + 1) * P], ident[:])
                    mm.then_inc(e["tr"], 1)
                pe.wait_ge(e["kn"], DNH)
                pe.wait_ge(e["qn"], DNH)
                pe.wait_ge(e["Darg"], 2 * NP_)
                pe.wait_ge(e["egr"], 2)
                for q in range(NQ):
                    for i in range(PQ):
                        t, h = divmod(q * PQ + i, DNH)
                        mm = pe.transpose(banks4((3, 4, 0)[q])[:, i, :], qkvT[:, DNH + h, t * P:(t + 1) * P], ident[:])
                    mm.then_inc(e["tr"], 1)

                def products(b, other):
                    for i in range(PQ):
                        t, h = divmod(q * PQ + i, DNH)
                        kk = qkvT[:, DNH + h, t * P:(t + 1) * P]
                        mm = pe.matmul(banks4(b)[:, i, :], kk, qkvT[:, other + h, t * P:(t + 1) * P], start=True, stop=True)
                    return mm

                for q in range(NQ):
                    if q == 2:
                        pe.wait_ge(e["kt"], PQ)
                    products(1 + q, DNH).then_inc(e["KK"], 1)
                for q in range(NQ):
                    pe.wait_ge(e["kt"], (2 * PQ, 3 * PQ, 3 * PQ)[q])
                    if q == 2:
                        pe.wait_ge(e["A"], PQ)
                    products((4, 0, 1)[q], 0).then_inc(e["KQ"], 1)
                for q in range(NQ):
                    pe.wait_ge(e["A"], PQ * (q + 1))
                    pe.wait_ge(e["vb"], PQ * (q + 1))
                    for i in range(PQ):
                        mm = pe.transpose(banks4(5 + q)[:, i, :], A[:, q * PQ + i, :], ident[:])
                    mm.then_inc(e["At"], 1)
                pe.wait_ge(e["qk"], NQ)
                pe.wait_ge(e["T0"], 1)
                pe.wait_ge(e["TT0"], 1)

                def first(j):
                    i, q = divmod(j, NQ)
                    pe.wait_ge(e["CT"], i + 1)
                    if i >= 1:
                        pe.wait_ge(e["Tn"], (i - 1) * NQ + q + 1)
                        pe.wait_ge(e["TTn"], (i - 1) * NQ + q + 1)
                    if j >= 2:
                        pe.wait_ge(e["We"], j - 1)
                    for a in range(PQ):
                        p = q * PQ + a
                        mm = pe.matmul(banks4(j % 2)[:, a, :], CT[i % 2][:, p, :], T[:, p, :], start=True, stop=True)
                    mm.then_inc(e["W"], 1)

                def second(j):
                    i, q = divmod(j, NQ)
                    pe.wait_ge(e["We"], j + 1)
                    for a in range(PQ):
                        p = q * PQ + a
                        if i < SOLVE - 2:
                            pe.matmul(banks4(2 + q)[:, a, :], TT[:, p, :], W[:, p, :], start=True, stop=True)
                        mm = pe.matmul(banks4(5 + q)[:, a, :], W[:, p, :], TT[:, p, :], start=True, stop=True)
                    mm.then_inc(e["PP"], 1)

                for i in range(SOLVE - 1):
                    first(i * NQ)
                    first(i * NQ + 1)
                    second(i * NQ)
                    first(i * NQ + 2)
                    second(i * NQ + 1)
                    second(i * NQ + 2)
                pe.wait_ge(e["TTn"], (SOLVE - 1) * NQ)
                pe.wait_ge(e["We"], (SOLVE - 1) * NQ)

                def b2(b, h):
                    return banks4(b + h // PQ)[:, h % PQ, :]

                for h in range(DNH):
                    mm = pe.matmul(b2(0, h), TT[:, h, :], vb[:, h, :], start=True, stop=True)
                mm.then_inc(e["U"], 1)
                for h in range(DNH):
                    mm = pe.matmul(b2(2, h), nkbg[:, h, :], TT[:, DNH + h, :], start=True, stop=True)
                mm.then_inc(e["wT"], 1)
                pe.wait_ge(e["Ue"], 2)
                for h in range(DNH):
                    mm = pe.matmul(b2(4, h), kdec[:, h, :], U0[:, h, :], start=True, stop=True)
                mm.then_inc(e["S"], 1)
                pe.wait_ge(e["Se"], 2)
                for h in range(DNH):
                    mm = pe.matmul(b2(6, h), DT[:, h, :], U0[:, h, :], start=True, stop=True)
                mm.then_inc(e["O"], 1)
                pe.wait_ge(e["wTe"], 2)
                for h in range(DNH):
                    pe.matmul(b2(0, h), TT[:, DNH + h, :], vb[:, DNH + h, :], start=True, stop=False)
                    mm = pe.matmul(b2(0, h), wT[:, h, :], St[:, h, :], start=False, stop=True)
                mm.then_inc(e["V"], 1)
                pe.wait_ge(e["Ve"], 2)
                for h in range(DNH):
                    pe.matmul(b2(2, h), qd[:, h, :], St[:, h, :], start=True, stop=False)
                    mm = pe.matmul(b2(2, h), DT[:, DNH + h, :], V1[:, h, :], start=False, stop=True)
                mm.then_inc(e["O"], 1)
                cross1.pe(pe, lambda eng, j: eng.wait_ge(e["Oe"], 4) if j == 0 else (eng.wait_ge(cross1.s_eva, j - 1) if j >= 2 else None))
                xa1.pe(pe, lambda eng: eng.wait_ge(cross1.s_eva, 4))
                op1.pe(pe, lambda eng: (eng.wait_ge(xa1.s_mix, 2 * XAH), eng.wait_ge(e["mix"], NT)))

            @block.sync
            def _(sp):
                sp.dma_start(gain[:, 0, :], row(ffn_norm[1], D)).then_inc(s_gain_ffn1, 16)

        next_layer()
        stage, wgh, wgl, wdh, wdl = feed_forward_memory(1)
        hT = psb("hT2", [P, KC, S])
        norm_f = NormTranspose("nf", [(X[:, t, :], gain[:, 0, :], hT[:, :, t * P:(t + 1) * P], (s_gain_ffn1, 16)) for t in range(NT)])
        router = gain[:, 1, 0:KC * NE].rearrange("p (c e) -> p c e", c=KC)
        slotno = gain[:, 1, 64:64 + NPB * CAP]
        em8 = gain[:, 1, 400:400 + NE]
        rt = hT[:].rearrange("p c t -> p (c t)")[:, 0:16 * 16].rearrange("p (k t e) -> p k t e", k=16, t=NT)
        rs = hT[:].rearrange("p c t -> p (c t)")[:, 256:256 + 16].rearrange("p (k t) -> p k t", t=NT)
        posn = psb("posn", [P, NT, NE + 1])
        wgt = psb("wgt", [P, NT, NE + 1])
        cnt = psb("cnt", [1, NE + 1], I32)
        cntf = psb("cntf", [1, NE + 1])
        sel = psb("sel", [P, NT, CAP])
        selw = psb("selw", [P, NT, CAP])
        selT = psb("selT", [CAP, S])
        xeh, xel = psb("xeh", [P, KC, CAP], F32R), psb("xel", [P, KC, CAP], F32R)
        hh, hl = psb("hh1", [P, 2, NB, CAP], F32R), psb("hl1", [P, 2, NB, CAP], F32R)
        hflat = hT[:].rearrange("p c t -> p (c t)")
        ye = hflat[0:CAP, 0:D]
        sg = hflat[0:CAP, D:D + 2 * GF].rearrange("p (i f) -> p i f", i=2)
        hm = hflat[0:CAP, D + 2 * GF:D + 4 * GF].rearrange("p (i f) -> p i f", i=2)
        r = {n: lsem(f"f_{n}") for n in (
            "router", "iota", "lg", "lgo", "step", "d", "ed", "mask", "pos", "posn", "cnt")}
        m = {n: lsem(f"m_{n}") for n in (
            "sel", "selw", "gather", "xeh", "xel", "hi", "lo", "gu", "silu", "hm", "tr", "hh", "hl", "down",
            "selT", "selTo", "y_act", "y_dve", "scatter", "x")}
        s_lo[0] = m["lo"]

        def expert(ex):
            return (moe_w_gate[0][ex], moe_w_up[0][ex], moe_w_down[0][ex])

        def after(eng, name, n, per, count):
            if isinstance(n, int) and per * n + count <= 0:
                return
            eng.wait_ge(m[name], per * n + count)

        def step_parts(g, has_next):
            if g + 2 < NG:
                first = [(0, g + 2, kind) for kind in (GATE, UP)]
            elif has_next:
                first = [(1, g + 2 - NG, kind) for kind in (GATE, UP)]
            else:
                first = []
            return first + [(0, g, DOWN)]

        def sp_start(sp, n, ex):
            if not isinstance(n, int) or n > 0:
                sp.wait_ge(m["lo"], GPP * n)
            for g, kind in FIRST_PARTS:
                load_part(sp, expert(ex), g, kind)

        def sp_pass(sp, n, ex, alone, has_next):
            for g in range(NG):
                parts = step_parts(g, has_next)
                for ahead, pg, kind in parts[::-1] if g == 0 else parts:
                    reload_part(sp, n + ahead, expert(ex + ahead), pg, kind, alone and not ahead,
                                first=isinstance(n, int) and n == 0)

        def dve_select(dve, ex, b):
            for t in range(NT):
                dve.tensor_scalar(sel[:, t, :], slotno[:, b * CAP:(b + 1) * CAP], posn[:, t, bass.ds(ex, 1)], None,
                                  ALU.is_equal).then_inc(m["sel"], 1)

        def pe_gather(pe, n):
            after(pe, "sel", n, NT, NT)
            for c in range(KC):
                for t in range(NT):
                    mm = pe.matmul(PS[:, c // 4, (c % 4) * CAP:(c % 4 + 1) * CAP], xn[:, t, c * P:(c + 1) * P], sel[:, t, :],
                                   start=(t == 0), stop=(t == NT - 1))
            mm.then_inc(m["gather"], 1)

        def gathered(half):
            return PS[:, half, 0:4 * CAP].rearrange("p (c n) -> p c n", c=4)

        def act_gathered(act, n):
            after(act, "gather", n, 1, 1)
            for half in range(2):
                act.activation(xeh[:, 4 * half:4 * half + 4, :], gathered(half), ACT.Copy).then_inc(m["xeh"], 1)

        def dve_gathered(dve, n):
            for half in range(2):
                after(dve, "xeh", n, 2, half + 1)
                hs = slice(4 * half, 4 * half + 4)
                dve.tensor_tensor(xel[:, hs, :], gathered(half), xeh[:, hs, :].bitcast(F32), ALU.subtract).then_inc(m["xel"], 1)

        def pe_transpose(pe, n, g):
            after(pe, "hm", n, NG, g + 1)
            after(pe, "hl", n, NG, g - 1)
            for b in range(NB):
                mm = pe.transpose(PS[:, 6 + g % 2, b * CAP:(b + 1) * CAP], hm[:, g % 2, b * P:(b + 1) * P], ident[0:CAP, 0:CAP])
            mm.then_inc(m["tr"], 1)

        def pe_down(pe, n, g, last):
            after(pe, "hl", n, NG, g + 1)
            after(pe, "lo", n, GPP, split_no(g, DOWN, False, last))
            if g == 0:
                after(pe, "y_act", n, 1, 0)
                after(pe, "y_dve", n, 1, 0)
            for b in range(NB):
                for half in range(2):
                    ws = slice(b * D + half * 512, b * D + (half + 1) * 512)
                    mm = three_passes(pe, PS[0:CAP, 4 + half, :], (hh[:, g % 2, b, :], hl[:, g % 2, b, :]),
                                      (wdh[:, g % 2, ws], wdl[:, g % 2, ws]), g == 0 and b == 0, g == NG - 1 and b == NB - 1)
            mm.then_inc(m["down"], 1)

        def pe_scatter(pe, n):
            after(pe, "selTo", n, 1, 1)
            for t in range(NT):
                for half in range(2):
                    if t == 0:
                        after(pe, "y_act" if half == 0 else "y_dve", n, 1, 1)
                    else:
                        after(pe, "x", n, 4, half + 1)
                    pe.matmul(PS[:, half, :], selT[:, t * P:(t + 1) * P], ye[:, half * 512:(half + 1) * 512],
                              start=True, stop=True).then_inc(m["scatter"], 1)

        def pe_pass(pe, n, alone, has_next):
            for g in range(NG):
                if g == 0:
                    after(pe, "xel", n, 2, 2)
                after(pe, "lo", n, GPP, split_no(g, UP, alone, not has_next))
                after(pe, "hm", n, NG, g - 1)
                for c in range(KC):
                    mm = three_passes(pe, PS[0:CAP, 2 + g % 2, :], (xeh[:, c, :], xel[:, c, :]),
                                      (wgh[:, g % 2, c].rearrange("p a f -> p (a f)"), wgl[:, g % 2, c].rearrange("p a f -> p (a f)")),
                                      c == 0, c == KC - 1)
                mm.then_inc(m["gu"], 1)
                if g >= 1:
                    pe_transpose(pe, n, g - 1)
                elif not alone:
                    pe_transpose(pe, n - 1, NG - 1)
                if g >= 2:
                    pe_down(pe, n, g - 2, not has_next)
                elif not alone:
                    pe_down(pe, n - 1, NG + g - 2, False)
                if g == 3 and not alone:
                    pe_scatter(pe, n - 1)
                if g == 6:
                    after(pe, "selw", n, NT, NT)
                    after(pe, "x", n, 4, 0)
                    for t in range(NT):
                        mm = pe.transpose(PS[0:CAP, 0, t * P:(t + 1) * P], selw[:, t, :], ident[:])
                    mm.then_inc(m["selT"], 1)
                if g == NG - 2 and has_next:
                    after(pe, "selTo", n, 1, 1)
                    pe_gather(pe, n + 1)

        def pe_finish(pe, n):
            pe_transpose(pe, n, NG - 1)
            for g in (NG - 2, NG - 1):
                pe_down(pe, n, g, True)
            pe_scatter(pe, n)

        def act_hidden(act, n, g):
            after(act, "tr", n, NG, g + 1)
            after(act, "down", n, NG, g - 1)
            act.activation(hh[:, g % 2].rearrange("p b n -> p (b n)"), PS[:, 6 + g % 2, 0:NB * CAP], ACT.Copy).then_inc(m["hh"], 1)

        def act_results(act, n):
            after(act, "down", n, NG, NG)
            act.activation(ye[:, 0:512], PS[0:CAP, 4, :], ACT.Copy).then_inc(m["y_act"], 1)

        def act_start(act, n):
            for g, kind in FIRST_PARTS:
                act_high(act, n + 1, g, kind, m["hi"])

        def act_pass(act, n, ex, alone, has_next):
            for g in range(NG):
                after(act, "gu", n, NG, g + 1)
                after(act, "hm", n, NG, g - 1)
                act.activation(sg[:, g % 2, :], PS[0:CAP, 2 + g % 2, 0:GF], ACT.Silu).then_inc(m["silu"], 1)
                if g == NG - 1 and has_next:
                    act_gathered(act, n + 1)
                if g >= 1:
                    act_hidden(act, n, g - 1)
                elif not alone:
                    act_hidden(act, n - 1, NG - 1)
                for ahead, pg, kind in step_parts(g, has_next):
                    if kind == DOWN:
                        after(act, "down", n, NG, g - 1)
                    act_high(act, n + 1 + ahead, pg, kind, m["hi"])
                if g == 1 and not alone:
                    act_results(act, n - 1)

        def act_finish(act, n):
            act_hidden(act, n, NG - 1)
            act_results(act, n)

        def dve_hidden(dve, n, g):
            after(dve, "hh", n, NG, g + 1)
            dve.tensor_tensor(hl[:, g % 2].rearrange("p b n -> p (b n)"), PS[:, 6 + g % 2, 0:NB * CAP],
                              hh[:, g % 2].rearrange("p b n -> p (b n)").bitcast(F32), ALU.subtract).then_inc(m["hl"], 1)

        def dve_results(dve, n):
            after(dve, "down", n, NG, NG)
            dve.tensor_copy(ye[:, 512:D], PS[0:CAP, 5, :]).then_inc(m["y_dve"], 1)

        def dve_sums(dve, n):
            for t in range(NT):
                for half in range(2):
                    after(dve, "scatter", n, 4, 2 * t + half + 1)
                    xv = X[:, t, half * 512:(half + 1) * 512]
                    dve.tensor_tensor(xv, xv, PS[:, half, :], ALU.add).then_inc(m["x"], 1)

        def dve_start(dve, n):
            for i, (g, kind) in enumerate(FIRST_PARTS):
                after(dve, "hi", n, GPP, i + 1)
                dve_rest(dve, g, kind, m["lo"])

        def dve_pass(dve, n, ex, alone, has_next):
            for g in range(NG):
                after(dve, "silu", n, NG, g + 1)
                after(dve, "tr", n, NG, g - 1)
                dve.tensor_tensor(hm[:, g % 2, :], sg[:, g % 2, :], PS[0:CAP, 2 + g % 2, GF:2 * GF], ALU.mult).then_inc(m["hm"], 1)
                if g == NG - 1 and has_next:
                    dve_gathered(dve, n + 1)
                if g >= 1:
                    dve_hidden(dve, n, g - 1)
                elif not alone:
                    dve_hidden(dve, n - 1, NG - 1)
                for ahead, pg, kind in step_parts(g, has_next):
                    after(dve, "hi", n + ahead, GPP, split_no(pg, kind, alone and not ahead, not has_next))
                    dve_rest(dve, pg, kind, m["lo"])
                if g == 1 and not alone:
                    dve_results(dve, n - 1)
                if g == 3 and not alone:
                    dve_sums(dve, n - 1)
                if g == 4:
                    for t in range(NT):
                        after(dve, "sel", n, NT, NT)
                        after(dve, "selT", n, 1, 0)
                        dve.tensor_scalar(selw[:, t, :], sel[:, t, :], wgt[:, t, bass.ds(ex, 1)], None, ALU.mult).then_inc(m["selw"], 1)
                if g == 7:
                    after(dve, "selT", n, 1, 1)
                    dve.tensor_copy(selT[:], PS[0:CAP, 0, 0:S]).then_inc(m["selTo"], 1)
                if g == 8 and has_next:
                    after(dve, "gather", n, 1, 1)
                    after(dve, "selw", n, NT, NT)
                    dve_select(dve, ex + 1, 0)

        def dve_finish(dve, n):
            dve_hidden(dve, n, NG - 1)
            dve_results(dve, n)
            dve_sums(dve, n)

        with nc.Block() as block:
            @block.sync
            def _(sp):
                sp.dma_start(router, k_rows(moe_router[0])).then_inc(r["router"], 16)
                sp_start(sp, 0, 0)
                sp_pass(sp, 0, 0, True, True)
                with sp.Fori(1, NE - 1) as ex:
                    sp_pass(sp, ex, ex, False, True)
                sp_pass(sp, NE - 1, NE - 1, False, False)

            @block.gpsimd
            def _(pool):
                pool.iota(slotno, [[1, NPB * CAP]], base=0, channel_multiplier=0,
                          allow_small_or_imprecise_dtypes=True).then_inc(r["iota"], 1)
                pool.iota(em8, [[1, NE]], base=-NE, channel_multiplier=0,
                          allow_small_or_imprecise_dtypes=True).then_inc(r["iota"], 1)

            @block.scalar
            def _(act):
                link = linker(act, "act")
                act.preload_act_table_set("natural_log_exp_and_others")
                norm_f.act_squares(act, link)
                norm_f.act_rstd(act, link)
                norm_f.act_evacuate(act)
                act.wait_ge(r["d"], 1)
                act.activation(rs[:, 3, :], rs[:, 2, :], ACT.Exp).then_inc(r["ed"], 1)
                act_start(act, 0)
                act_gathered(act, 0)
                act_pass(act, 0, 0, True, True)
                with act.Fori(1, NE - 1) as ex:
                    act_pass(act, ex, ex, False, True)
                act_pass(act, NE - 1, NE - 1, False, False)
                act_finish(act, NE - 1)

            @block.vector
            def _(dve):
                link = linker(dve, "dve")
                norm_f.dve_rows(dve)
                dve.wait_ge(r["lg"], 1)
                dve.tensor_copy(rt[:, 0], PS[:, 2, 0:NT * NE].rearrange("p (t e) -> p t e", t=NT)).then_inc(r["lgo"], 1)
                dve.wait_ge(r["lgo"], 1)
                dve.wait_ge(r["iota"], 2)
                em8b = em8.unsqueeze(1).to_broadcast([P, NT, NE])

                def bc(v):
                    return v.unsqueeze(2).to_broadcast([P, NT, NE])

                for i in range(2):
                    lg, eq, first, mask = rt[:, 3 * i], rt[:, 1], rs[:, 4 + i, :], rt[:, 4 + i]
                    link(dve.tensor_reduce(rs[:, i, :], lg, X_AXIS, ALU.max))
                    link(dve.tensor_tensor(eq, lg, bc(rs[:, i, :]), ALU.is_equal))
                    link(dve.tensor_tensor(eq, eq, em8b, ALU.mult))
                    link(dve.tensor_reduce(first, eq, X_AXIS, ALU.min))
                    link(dve.tensor_tensor(mask, em8b, bc(first), ALU.is_equal))
                    if i == 0:
                        link(dve.scalar_tensor_tensor(out=rt[:, 3], in0=mask, scalar=NEG, in1=lg, op0=ALU.mult, op1=ALU.add))
                dve.tensor_tensor(rs[:, 2, :], rs[:, 1, :], rs[:, 0, :], ALU.subtract).then_inc(r["d"], 1)
                dve.tensor_tensor(rt[:, 6], rt[:, 4], rt[:, 5], ALU.add).then_inc(r["mask"], 1)
                dve.wait_ge(r["ed"], 1)
                link(dve.tensor_scalar(rs[:, 6, :], rs[:, 3, :], 1.0, None, ALU.add))
                link(dve.reciprocal(rs[:, 6, :], rs[:, 6, :]))
                link(dve.tensor_tensor(rs[:, 7, :], rs[:, 6, :], rs[:, 3, :], ALU.mult))
                link(dve.tensor_tensor(rt[:, 4], rt[:, 4], bc(rs[:, 6, :]), ALU.mult))
                link(dve.tensor_tensor(rt[:, 5], rt[:, 5], bc(rs[:, 7, :]), ALU.mult))
                link(dve.tensor_tensor(wgt[:, :, 0:NE], rt[:, 4], rt[:, 5], ALU.add))
                dve.wait_ge(r["pos"], 1)
                link(dve.memset(posn[:], -1.0))
                link(dve.scalar_tensor_tensor(out=rt[:, 7], in0=PS[:, 3, 0:NT * NE].rearrange("p (t e) -> p t e", t=NT), scalar=1.0,
                                              in1=rt[:, 6], op0=ALU.add, op1=ALU.mult))
                link(dve.tensor_scalar(posn[:, :, 0:NE], rt[:, 7], -1.0, None, ALU.add))
                link(dve.tensor_copy(cntf[:, 0:NE], PS[0:1, 3, 2 * NT * NE:2 * NT * NE + NE]))
                link(dve.tensor_reduce(cntf[:, NE:NE + 1], cntf[:, 0:NE], X_AXIS, ALU.max))
                dve.tensor_copy(cnt[:], cntf[:]).then_inc(r["cnt"], 1)
                dve_select(dve, 0, 0)
                dve_start(dve, 0)
                dve_gathered(dve, 0)
                dve_pass(dve, 0, 0, True, True)
                with dve.Fori(1, NE - 1) as ex:
                    dve_pass(dve, ex, ex, False, True)
                dve_pass(dve, NE - 1, NE - 1, False, False)
                dve_finish(dve, NE - 1)

            @block.tensor
            def _(pe):
                norm_f.pe(pe)
                norm_f.ready(pe, NT)
                pe.wait_ge(r["router"], 16)
                for t in range(NT):
                    for c in range(KC):
                        mm = pe.matmul(PS[:, 2, t * NE:(t + 1) * NE], hT[:, c, t * P:(t + 1) * P], router[:, c, :],
                                       start=(c == 0), stop=(c == KC - 1))
                mm.then_inc(r["lg"], 1)
                pe.wait_ge(r["mask"], 1)
                pe.matmul(PS[:, 3, 0:NE], upstrict[:], rt[:, 6, 0], start=True, stop=True)
                pe.matmul(PS[:, 3, NE:2 * NE], upstrict[:], rt[:, 6, 1], start=True, stop=False)
                pe.matmul(PS[:, 3, NE:2 * NE], ones[:], rt[:, 6, 0], start=False, stop=True)
                pe.matmul(PS[:, 3, 4 * NE:5 * NE], ones[:], rt[:, 6, 0], start=True, stop=False)
                pe.matmul(PS[:, 3, 4 * NE:5 * NE], ones[:], rt[:, 6, 1], start=False, stop=True).then_inc(r["pos"], 1)
                pe_gather(pe, 0)
                pe_pass(pe, 0, True, True)
                with pe.Fori(1, NE - 1) as ex:
                    pe_pass(pe, ex, False, True)
                pe_pass(pe, NE - 1, False, False)
                pe_finish(pe, NE - 1)

        def overflow(eng, one_pass):
            most = eng.value_load(cnt[0:1, NE:NE + 1], min_val=0, max_val=S)
            with eng.If(most > CAP):
                done = eng.alloc_register("passes_done")
                eng.reg_mov(done, NE)
                with eng.Fori(0, NE) as ex:
                    for b in range(1, NPB):
                        tokens = eng.value_load(cnt[0:1, bass.ds(ex, 1)], min_val=0, max_val=S)
                        with eng.If(tokens > b * CAP):
                            n = eng.snap(done, min_val=NE, max_val=2 * S * NT)
                            one_pass(ex, b, n)
                            eng.reg_add(done, done, 1)
                        with eng.Else():
                            eng.nop()
                        eng.nop()
                eng.nop()
            with eng.Else():
                eng.nop()
            eng.nop()

        with nc.Block() as block:
            @block.sync
            def _(sp):
                def one_pass(ex, b, n):
                    sp_start(sp, n, ex)
                    sp_pass(sp, n, ex, True, False)
                overflow(sp, one_pass)

            @block.scalar
            def _(act):
                def one_pass(ex, b, n):
                    act_start(act, n)
                    act_gathered(act, n)
                    act_pass(act, n, ex, True, False)
                    act_finish(act, n)
                overflow(act, one_pass)

            @block.vector
            def _(dve):
                def one_pass(ex, b, n):
                    after(dve, "gather", n, 1, 0)
                    after(dve, "selw", n, NT, 0)
                    dve_select(dve, ex, b)
                    dve_start(dve, n)
                    dve_gathered(dve, n)
                    dve_pass(dve, n, ex, True, False)
                    dve_finish(dve, n)
                overflow(dve, one_pass)

            @block.tensor
            def _(pe):
                def one_pass(ex, b, n):
                    after(pe, "x", n, 4, 0)
                    pe_gather(pe, n)
                    pe_pass(pe, n, True, False)
                    pe_finish(pe, n)
                overflow(pe, one_pass)


        with nc.Block() as block:
            @block.sync
            def _(sp):
                sp.dma_start(out[0].rearrange("(t p) d -> p t d", p=P), X[:]).then_inc(s_y, 16)
                sp.wait_ge(s_y, 16)


_INS = ['x', 'mem', 'mix_norm', 'ffn_norm', 'mem_norm', 'w_mem_kv', 'xa_q_norm', 'xa_k_norm', 'w_out',
        'sb_w_in', 'sb_q_norm', 'sb_k_norm', 'dn_w_in', 'dn_conv', 'dn_a_log', 'dn_dt_bias', 'dn_o_norm',
        'ffd_w_gate', 'ffd_w_up', 'ffd_w_down', 'moe_router', 'moe_w_gate', 'moe_w_up', 'moe_w_down']
_OUTS = [((1, S, D), 'float32')]


def kernel(**inputs):
    import numpy as _np
    import concourse.bacc as _bacc
    from concourse import mybir as _mybir
    from concourse.bass_utils import run_bass_kernel_spmd as _run

    nc = _bacc.Bacc("TRN2", target_bir_lowering=False, num_devices=1)
    arrays, args = {}, []
    for name in _INS:
        a = _np.ascontiguousarray(inputs[name])
        arrays[f"in_{name}_dram"] = a
        args.append(nc.dram_tensor(f"in_{name}_dram", a.shape, _mybir.dt.from_np(a.dtype), kind="ExternalInput").ap())
    for i, (shape, dtype) in enumerate(_OUTS):
        dt = _mybir.dt.from_np(_np.dtype(dtype))
        args.append(nc.dram_tensor(f"out_{i}_dram", shape, dt, kind="ExternalOutput").ap())
    hybrid_kernel(nc, *args)
    r = _run(nc, [arrays], core_ids=[0])
    got = tuple(r.results[0][f"out_{i}_dram"] for i in range(len(_OUTS)))
    return got[0]
```

```python
from contextlib import ExitStack

import numpy as np

import concourse.bass as bass
from concourse import mybir

P = 128
D = 1024
S = 256
NT = S // P
KC = D // P
HD = 64
SBH, XAH, DNH = 12, 4, 6
SBW, XAW, DNW = SBH * HD, XAH * HD, DNH * P
SB_IN = 3 * SBW + XAW
DN_IN = 4 * DNW + 2 * DNH + XAW
FF = 3584
NE = 8
GF = 256
NG = FF // GF
PART = KC * GF
STAGES = 7
CAP = 96
NPB = -(-S // CAP)
EPS = 1e-6
ASLOT = KC * 512
ASLOTS = 3
ARENA = 42880
NEG = -1.0e30

F32 = mybir.dt.float32
BF16 = mybir.dt.bfloat16
F32R = mybir.dt.float32r
I32 = mybir.dt.int32
ALU = mybir.AluOpType
ACT = mybir.ActivationFunctionType
X_AXIS = mybir.AxisListType.X


def hybrid_kernel(nc, x, mem, mix_norm, ffn_norm, mem_norm, w_mem_kv, xa_q_norm, xa_k_norm, w_out,
                  sb_w_in, sb_q_norm, sb_k_norm, dn_w_in, dn_conv, dn_a_log, dn_dt_bias, dn_o_norm,
                  ffd_w_gate, ffd_w_up, ffd_w_down, moe_router, moe_w_gate, moe_w_up, moe_w_down, out):
    with ExitStack() as ctx:
        def sb(name, shape, dt=F32):
            return ctx.enter_context(nc.sbuf_tensor(name, shape, dt))

        layer_sems = []

        def sem(name):
            return ctx.enter_context(nc.semaphore(name))

        def lsem(name):
            h = layer_sems[0].enter_context(nc.semaphore(name))
            layer_sems[1].append(h)
            return h

        def next_layer():
            if layer_sems:
                def clear(eng, i):
                    for h in layer_sems[1][i::5]:
                        eng.sem_clear(h)

                with nc.Block() as block:
                    @block.gpsimd
                    def _(pool):
                        clear(pool, 0)

                    @block.scalar
                    def _(act):
                        act.preload_act_table_set("natural_log_exp_and_others")
                        clear(act, 1)

                    @block.vector
                    def _(dve):
                        clear(dve, 2)

                    @block.tensor
                    def _(pe):
                        clear(pe, 3)

                    @block.sync
                    def _(sp):
                        clear(sp, 4)
                layer_sems[0].close()
            layer_sems[:] = [ctx.enter_context(ExitStack()), []]

        s_y = sem("s_y")
        next_layer()

        memory = [None]

        def psb(name, shape, dt=F32):
            return memory[0].enter_context(nc.sbuf_tensor(name, shape, dt))

        def next_memory():
            if memory[0] is not None:
                memory[0].close()
            memory[0] = ctx.enter_context(ExitStack())

        X = sb("X", [P, NT, D])
        kv1 = sb("kv1", [P, NT, 2 * XAW])
        xn = sb("xn", [P, NT, D])
        gain = sb("gain", [P, 2, D])
        stat = sb("stat", [P, 3, 8])
        epsc = sb("epsc", [P, 1])
        ident = sb("ident", [P, P])
        ones = sb("ones", [P, P])
        upincl = sb("upincl", [P, P])
        upstrict = sb("upstrict", [P, P])
        PS = ctx.enter_context(nc.psum_tensor("PS", [P, 8, 512], F32))

        next_memory()
        hT = psb("hT0", [P, KC, S])
        ring = psb("ring0", [P, ARENA])

        class Scratch:
            def __init__(self):
                self.at = ASLOTS * ASLOT

            def tile(self, parts, *shape):
                n = int(np.prod(shape))
                v = ring[0:parts, self.at:self.at + n]
                self.at += n
                assert self.at <= ARENA, (self.at, ARENA)
                names = "abc"[:len(shape)]
                if len(shape) == 1:
                    return v
                return v.rearrange("p (" + " ".join(names) + ") -> p " + " ".join(names),
                                   **{c: k for c, k in zip(names[1:], shape[1:])})

        def aslot(n, cols):
            at = (n % ASLOTS) * ASLOT
            return ring[:, at:at + KC * cols].rearrange("p (c f) -> p c f", c=KC)

        def k_rows(w):
            return w.rearrange("(c p) f -> p c f", p=P)

        s_chain = {}

        def linker(eng, name):
            if name not in s_chain:
                s_chain[name] = [sem(f"s_{name}_chain"), 0]
            c = s_chain[name]

            def link(ins):
                c[1] += 1
                ins.then_inc(c[0], 1)
                eng.wait_ge(c[0], c[1])
            return link

        class NormTranspose:
            def __init__(self, tag, units, at=0, squares=None):
                self.units = units
                self.stat = stat[:, :, at:at + len(units)]
                self.squares = xn[:, 0, :] if squares is None else squares
                self.s_sq, self.s_ms, self.s_rstd, self.s_xn = (lsem(f"{tag}_{n}") for n in ("sq", "ms", "rstd", "xn"))
                self.s_tr, self.s_eva, self.s_evd = (lsem(f"{tag}_{n}") for n in ("tr", "eva", "evd"))

            def act_squares(self, act, link):
                for u, (src, g, dst, ready) in enumerate(self.units):
                    act.wait_ge(*ready)
                    if u >= 1:
                        act.wait_ge(self.s_sq, u)
                    act.activation(self.squares, src, ACT.Square, accum_out=self.stat[:, 0, u:u + 1]).then_inc(self.s_sq, 1)

            def act_row_squares(self, act, s_x):
                for t in range(NT):
                    act.wait_ge(s_x, 2 * t + 2)
                    if t >= 1:
                        act.wait_ge(self.s_sq, t)
                    act.activation(self.squares, X[:, t, :], ACT.Square, accum_out=self.stat[:, 0, t:t + 1]).then_inc(self.s_sq, 1)

            def act_rstd(self, act, link):
                act.wait_ge(self.s_ms, 1)
                link(act.activation(self.stat[:, 2, :], self.stat[:, 1, :], ACT.Ln))
                act.activation(self.stat[:, 2, :], self.stat[:, 2, :], ACT.Exp, scale=-0.5).then_inc(self.s_rstd, 1)

            def act_evacuate(self, act):
                for u, (src, g, dst, ready) in enumerate(self.units):
                    act.wait_ge(self.s_tr, 2 * u + 1)
                    act.activation(dst[:, 0:4, :], PS[:, 0, :].rearrange("p (c t) -> p c t", c=4),
                                   ACT.Copy).then_inc(self.s_eva, 1)

            def dve_rows(self, dve):
                n = len(self.units)
                dve.wait_ge(self.s_sq, n)
                dve.tensor_scalar(self.stat[:, 1, :], self.stat[:, 0, :], 1.0 / D, EPS, ALU.mult, ALU.add).then_inc(self.s_ms, 1)
                dve.wait_ge(self.s_rstd, 1)
                for u, (src, g, dst, ready) in enumerate(self.units):
                    if u >= NT:
                        self.dve_evacuate_one(dve, u - NT)
                    if g is None:
                        dve.tensor_scalar(xn[:, u % NT, :], src, self.stat[:, 2, u:u + 1], None, ALU.mult).then_inc(self.s_xn, 1)
                    else:
                        dve.scalar_tensor_tensor(out=xn[:, u % NT, :], in0=src, scalar=self.stat[:, 2, u:u + 1], in1=g,
                                                 op0=ALU.mult, op1=ALU.mult).then_inc(self.s_xn, 1)
                for u in range(max(0, n - NT), n):
                    self.dve_evacuate_one(dve, u)

            def dve_evacuate_one(self, dve, u):
                dve.wait_ge(self.s_tr, 2 * u + 2)
                dve.tensor_copy(self.units[u][2][:, 4:8, :],
                                PS[:, 1, :].rearrange("p (c t) -> p c t", c=4)).then_inc(self.s_evd, 1)

            def pe(self, pe):
                for u in range(len(self.units)):
                    pe.wait_ge(self.s_xn, u + 1)
                    for half, freed in ((0, self.s_eva), (1, self.s_evd)):
                        if u >= 1:
                            pe.wait_ge(freed, u)
                        for c in range(4):
                            mm = pe.transpose(PS[:, half, c * P:(c + 1) * P],
                                              xn[:, u % NT, (4 * half + c) * P:(4 * half + c + 1) * P], ident[:])
                        mm.then_inc(self.s_tr, 1)

            def ready(self, eng, units):
                eng.wait_ge(self.s_eva, units)
                eng.wait_ge(self.s_evd, units)

        class NormTransposeSplit(NormTranspose):
            def act_evacuate(self, act):
                for u in range(len(self.units)):
                    dst = self.units[u][2]
                    for half in range(2):
                        act.wait_ge(self.s_tr, 2 * u + half + 1)
                        act.activation(dst[0][:, 4 * half:4 * half + 4, :], PS[:, 2 * u + half, :].rearrange("p (c t) -> p c t", c=4),
                                       ACT.Copy).then_inc(self.s_eva, 1)

            def dve_evacuate_one(self, dve, u):
                dst = self.units[u][2]
                for half in range(2):
                    dve.wait_ge(self.s_eva, 2 * u + half + 1)
                    hs = slice(4 * half, 4 * half + 4)
                    dve.tensor_tensor(dst[1][:, hs, :], PS[:, 2 * u + half, :].rearrange("p (c t) -> p c t", c=4),
                                      dst[0][:, hs, :].bitcast(F32), ALU.subtract).then_inc(self.s_evd, 1)

            def pe(self, pe):
                for u in range(len(self.units)):
                    pe.wait_ge(self.s_xn, u + 1)
                    for half in range(2):
                        for c in range(4):
                            mm = pe.transpose(PS[:, 2 * u + half, c * P:(c + 1) * P],
                                              xn[:, u % NT, (4 * half + c) * P:(4 * half + c + 1) * P], ident[:])
                        mm.then_inc(self.s_tr, 1)

            def ready(self, eng, units):
                eng.wait_ge(self.s_evd, 2 * units)

        class CrossPrep:
            def __init__(self, tag, q_tok, kv_tok, qT, kT, sq, st, gq, gk, banks):
                self.q_tok, self.kv_tok, self.qT, self.kT = q_tok, kv_tok, qT, kT
                self.sq, self.st, self.gq, self.gk, self.banks = sq, st, gq, gk, banks
                self.s_sq, self.s_ms, self.s_rstd, self.s_n = (lsem(f"{tag}_{n}") for n in ("sq", "ms", "rstd", "n"))
                self.s_tr, self.s_eva = lsem(f"{tag}_tr"), lsem(f"{tag}_eva")

            def act(self, act, link, ready):
                ready(act)
                act.activation(self.sq[:, :, 0:XAW], self.q_tok, ACT.Square).then_inc(self.s_sq, 1)
                act.activation(self.sq[:, :, XAW:2 * XAW], self.kv_tok[:, :, 0:XAW], ACT.Square).then_inc(self.s_sq, 1)
                act.wait_ge(self.s_ms, 1)
                link(act.activation(self.st[:, 1], self.st[:, 1], ACT.Ln))
                act.activation(self.st[:, 1], self.st[:, 1], ACT.Exp, scale=-0.5).then_inc(self.s_rstd, 1)

            def dve(self, dve, link, ready):
                dve.wait_ge(self.s_sq, 2)
                link(dve.tensor_reduce(self.st[:, 0].rearrange("p (t h) -> p t h", t=NT),
                                       self.sq.rearrange("p t (h d) -> p t h d", d=HD), X_AXIS, ALU.add))
                dve.tensor_scalar(self.st[:, 1], self.st[:, 0], 1.0 / HD, EPS, ALU.mult, ALU.add).then_inc(self.s_ms, 1)
                dve.wait_ge(self.s_rstd, 1)
                ready(dve)
                r = self.st[:, 1].rearrange("p (t h) -> p t h", t=NT)
                for v, h0 in ((self.q_tok, 0), (self.kv_tok[:, :, 0:XAW], XAH)):
                    for t in range(NT):
                        w = v[:, t, :].rearrange("p (h d) -> p h d", d=HD)
                        dve.tensor_tensor(w, w, r[:, t, h0:h0 + XAH].unsqueeze(2).to_broadcast([P, XAH, HD]),
                                          ALU.mult).then_inc(self.s_n, 1)

            def pe(self, pe, freed):
                for j in range(4):
                    pe.wait_ge(self.s_n, 2 * NT)
                    freed(pe, j)
                    src = self.q_tok if j < 2 else self.kv_tok
                    for i in range(2):
                        h = 2 * (j % 2) + i
                        for t in range(NT):
                            mm = pe.transpose(PS[0:HD, self.banks[j], (i * NT + t) * P:(i * NT + t + 1) * P],
                                              src[:, t, h * HD:(h + 1) * HD], ident[:])
                    mm.then_inc(self.s_tr, 1)

            def act_evacuate(self, act):
                for j in range(4):
                    act.wait_ge(self.s_tr, j + 1)
                    dst = (self.qT if j < 2 else self.kT)[:, 2 * (j % 2):2 * (j % 2) + 2, :]
                    act.activation(dst, PS[0:HD, self.banks[j], :].rearrange("p (h t) -> p h t", h=2), ACT.Copy,
                                   scale=(self.gq if j < 2 else self.gk)).then_inc(self.s_eva, 1)

        class Cross:
            def __init__(self, tag, qT, kT, v_tok, mix, c0, tmp):
                self.qT, self.kT, self.v, self.mix, self.c0 = qT, kT, v_tok, mix, c0
                self.prob, self.probT, self.st = tmp
                self.s_s, self.s_max, self.s_p, self.s_pt, self.s_pe, self.s_o, self.s_mix, self.s_rec = (
                    lsem(f"{tag}_{n}") for n in ("scores", "max", "probs", "probsT", "probsT_out", "o", "mix", "rec"))
                self.units = [(h, t) for h in range(XAH) for t in range(NT)]

            def steps(self):
                return len(self.units) + 2

            def pe_step(self, pe, i):
                n = len(self.units)
                if i < n:
                    h, t = self.units[i]
                    if i >= 2:
                        pe.wait_ge(self.s_p, i - 1)
                    pe.matmul(PS[:, i % 2, 0:S], self.qT[:, h, t * P:(t + 1) * P], self.kT[:, h, :],
                              start=True, stop=True).then_inc(self.s_s, 1)
                if 1 <= i <= n:
                    j = i - 1
                    pe.wait_ge(self.s_p, j + 1)
                    if j >= 2:
                        pe.wait_ge(self.s_pe, j - 1)
                    for m in range(NT):
                        mm = pe.transpose(PS[:, 2 + j % 2, m * P:(m + 1) * P],
                                          self.prob[:, j % 2, m * P:(m + 1) * P], ident[:])
                    mm.then_inc(self.s_pt, 1)
                if i >= 2:
                    j = i - 2
                    h, t = self.units[j]
                    pe.wait_ge(self.s_pe, j + 1)
                    if j >= 2:
                        pe.wait_ge(self.s_mix, j - 1)
                    for m in range(NT):
                        mm = pe.matmul(PS[:, 4 + j % 2, 0:HD], self.probT[:, j % 2, m * P:(m + 1) * P],
                                       self.v[:, m, h * HD:(h + 1) * HD], start=(m == 0), stop=(m == NT - 1))
                    mm.then_inc(self.s_o, 1)

            def act_step(self, act, i):
                n = len(self.units)
                if i < n:
                    act.wait_ge(self.s_max, i + 1)
                    if i >= 2:
                        act.wait_ge(self.s_pt, i - 1)
                    act.activation(self.prob[:, i % 2, :], PS[:, i % 2, 0:S], ACT.Exp,
                                   bias=self.st[:, 0, i:i + 1],
                                   accum_out=self.st[:, 1, i:i + 1]).then_inc(self.s_p, 1)
                if 1 <= i <= n:
                    j = i - 1
                    act.wait_ge(self.s_pt, j + 1)
                    if j >= 2:
                        act.wait_ge(self.s_o, j - 1)
                    act.activation(self.probT[:, j % 2, :], PS[:, 2 + j % 2, 0:S], ACT.Copy).then_inc(self.s_pe, 1)

            def dve_step(self, dve, i):
                n = len(self.units)
                if i < n:
                    dve.wait_ge(self.s_s, i + 1)
                    dve.tensor_reduce(self.st[:, 0, i:i + 1], PS[:, i % 2, 0:S], X_AXIS, ALU.max,
                                      negate=True).then_inc(self.s_max, 1)
                if i >= 2:
                    j = i - 2
                    h, t = self.units[j]
                    dve.wait_ge(self.s_p, j + 1)
                    dve.reciprocal(self.st[:, 2, j:j + 1], self.st[:, 1, j:j + 1]).then_inc(self.s_rec, 1)
                    dve.wait_ge(self.s_rec, j + 1)
                    dve.wait_ge(self.s_o, j + 1)
                    dve.tensor_scalar(self.mix[:, t, self.c0 + h * HD:self.c0 + (h + 1) * HD],
                                      PS[:, 4 + j % 2, 0:HD], self.st[:, 2, j:j + 1], None,
                                      ALU.mult).then_inc(self.s_mix, 1)

        class OutProjection:
            def __init__(self, tag, mix, slots, s_w):
                self.mix, self.slots, self.s_w = mix, slots, s_w
                self.s_tr, self.s_eva, self.s_evd, self.s_y, self.s_x = (
                    lsem(f"{tag}_{n}") for n in ("tr", "eva", "evd", "y", "x"))

            def bank(self, t, half):
                return (4 + half) if t == 0 else half

            def pe(self, pe, ready):
                for t in range(NT):
                    ready(pe, t)
                    for half, freed in ((0, self.s_eva), (1, self.s_evd)):
                        if t >= 1:
                            pe.wait_ge(freed, t)
                        for c in range(4):
                            k = 4 * half + c
                            mm = pe.transpose(PS[:, 6 + half, c * P:(c + 1) * P], self.mix[:, t, k * P:(k + 1) * P], ident[:])
                        mm.then_inc(self.s_tr, 1)
                    pe.wait_ge(self.s_eva, t + 1)
                    pe.wait_ge(self.s_evd, t + 1)
                    for half in range(2):
                        self.s_w(pe, half)
                        for k in range(KC):
                            mm = pe.matmul(PS[:, self.bank(t, half), :], hT[:, k, t * P:(t + 1) * P], self.slots[half][:, k, :],
                                           start=(k == 0), stop=(k == KC - 1))
                        mm.then_inc(self.s_y, 1)

            def act_evacuate(self, act, t):
                act.wait_ge(self.s_tr, 2 * t + 1)
                act.activation(hT[:, 0:4, t * P:(t + 1) * P], PS[:, 6, :].rearrange("p (c t) -> p c t", c=4),
                               ACT.Copy).then_inc(self.s_eva, 1)

            def dve_evacuate(self, dve, t):
                dve.wait_ge(self.s_tr, 2 * t + 2)
                dve.tensor_copy(hT[:, 4:8, t * P:(t + 1) * P],
                                PS[:, 7, :].rearrange("p (c t) -> p c t", c=4)).then_inc(self.s_evd, 1)

            def dve_sums(self, dve):
                for t in range(NT):
                    for half in range(2):
                        dve.wait_ge(self.s_y, 2 * t + half + 1)
                        xv = X[:, t, half * 512:(half + 1) * 512]
                        dve.tensor_tensor(xv, xv, PS[:, self.bank(t, half), :], ALU.add).then_inc(self.s_x, 1)

        def row(v, n):
            return v.rearrange("(a n) -> a n", a=1).to_broadcast([P, n])

        def col(v):
            return v.rearrange("(p a) -> p a", a=1)

        sc = Scratch()
        memr = sc.tile(P, NT, D)
        memT = sc.tile(P, KC, S)
        memT1 = sc.tile(P, KC, S)
        memU = sc.tile(P, KC, S)
        gmem_rows = sc.tile(2 * KC, P)
        gmem = sc.tile(P, 2, KC)
        proj = sc.tile(P, NT, SB_IN)
        kv_tok = sc.tile(P, NT, 2 * XAW)
        qT = sc.tile(HD, SBH, S)
        kT = sc.tile(HD, SBH, S)
        xqT = sc.tile(HD, XAH, S)
        xkT = sc.tile(HD, XAH, S)
        mix = sc.tile(P, NT, D)
        sqs = sc.tile(P, 2 * SBW)
        sqx = sc.tile(P, NT, 2 * XAW)
        hst = sc.tile(P, NT, 2, 2 * SBH)
        xst = sc.tile(P, 2, NT * 2 * XAH)
        gcol = sc.tile(HD, 8)
        negup = sc.tile(P, P)
        negones = sc.tile(P, P)
        diag0 = sc.tile(P, 3, P)
        diagneg = sc.tile(P, P)
        xtmp = (sc.tile(P, 2, S), sc.tile(P, 2, S), sc.tile(P, 3, 8))
        flat = ring[:, ASLOTS * ASLOT:ASLOTS * ASLOT + 2 * NT * D].rearrange("p (k b n) -> p k b n", k=4, b=2)
        habs, hln, hL, hA = (flat[:, i, :, 0:384] for i in range(4))

        s_x, s_mem, s_gain, s_gcol = lsem("s_x"), lsem("s_mem"), sem("s_gain"), lsem("s_gcol")
        s_gain_ffn0, s_gain_mix1, s_gain_ffn1 = (sem(f"s_gain_{n}") for n in ("ffn0", "mix1", "ffn1"))
        identb, diagnegb = psb("identb", [P, P], BF16), psb("diagnegb", [P, P], BF16)
        s_const, s_const2 = sem("s_const"), sem("s_const2")
        s_aw = [sem(f"s_aw{i}") for i in range(ASLOTS)]
        NSB = SB_IN // 512
        sb_blocks = [NSB - 1] + list(range(NSB - 1))
        loads0 = [(sb_w_in[0][:, c * 512:(c + 1) * 512], 512) for c in sb_blocks[:1]] + [(w_mem_kv[0], 512)] + \
                 [(sb_w_in[0][:, c * 512:(c + 1) * 512], 512) for c in sb_blocks[1:]] + [(w_mem_kv[1], 512)] + \
                 [(w_out[0][:, c * 512:(c + 1) * 512], 512) for c in range(2)]
        QK = 384
        loads1 = [(dn_w_in[0][:, 4 * DNW:DN_IN], DN_IN - 4 * DNW)] + \
                 [(dn_w_in[0][:, c * QK:(c + 1) * QK], QK) for c in range(8)] + [(w_out[1][:, c * 512:(c + 1) * 512], 512) for c in range(2)]
        loads = loads0 + loads1
        N0 = len(loads0)

        def attention_loads(sp, first, last, phase):
            for n in range(first, last):
                if n - ASLOTS >= phase:
                    sp.wait_ge(*load_read[n - ASLOTS])
                w, cols = loads[n]
                sp.dma_start(aslot(n, cols), k_rows(w)).then_inc(s_aw[n % ASLOTS], 16)

        def weights_in(pe, n):
            pe.wait_ge(s_aw[n % ASLOTS], 16 * (n // ASLOTS + 1))
            return aslot(n, loads[n][1])

        norm_x = NormTranspose("nx", [(X[:, t, :], gain[:, 0, :], hT[:, :, t * P:(t + 1) * P], (s_x, 16)) for t in range(NT)])
        norm_m = NormTranspose("nm", [(memr[:, t, :], None, memU[:, :, t * P:(t + 1) * P], (s_mem, 16)) for t in range(NT)],
                               at=NT, squares=mix[:, 0, :])
        s_pj, s_pja, s_pjd = lsem("a_proj"), lsem("a_proj_act"), lsem("a_proj_dve")
        s_hsq, s_hms, s_hrs, s_hn, s_g8 = lsem("a_hsq"), lsem("a_hms"), lsem("a_hrs"), lsem("a_hn"), lsem("a_g8")
        s_ht, s_hta, s_htd = lsem("a_ht"), lsem("a_ht_act"), lsem("a_ht_dve")
        s_gmem, s_gmt, s_gmo, s_memg = (lsem(f"a_{n}") for n in ("gmem", "gmemT", "gmem_out", "mem_gained"))
        jobs_a = [(hT, load, t, proj[:, t, c * 512:(c + 1) * 512]) for load, c in [(0, NSB - 1)] for t in range(NT)] + \
                 [(memT, 1, t, kv_tok[:, t, :]) for t in range(NT)] + \
                 [(hT, 2 + c, t, proj[:, t, c * 512:(c + 1) * 512]) for c in range(NSB - 1) for t in range(NT)] + \
                 [(memT1, NSB + 1, t, kv1[:, t, :]) for t in range(NT)]
        XJ = 5
        QKJ = 4 + 3 * NT
        cross0 = CrossPrep("cp0", proj[:, :, 3 * SBW:SB_IN], kv_tok, xqT, xkT, sqx, xst, gcol[:, 4:5], gcol[:, 3:4], (0, 1, 2, 3))
        NHJ = SBH // 2
        xa0 = Cross("xa0", xqT, xkT, kv_tok[:, :, XAW:2 * XAW], mix, SBW, xtmp)

        load_read = [(s_pj, NT * (n + 1)) for n in range(N0 - 2)]

        with nc.Block() as block:
            @block.sync
            def _(sp):
                sp.dma_start(X[:], x[0].rearrange("(t p) d -> p t d", p=P)).then_inc(s_x, 16)
                sp.dma_start(gain[:, 0, :], row(mix_norm[0], D)).then_inc(s_gain, 16)
                sp.dma_start(gmem_rows, mem_norm.rearrange("l (c p) -> (l c) p", p=P)).then_inc(s_gmem, 16)
                attention_loads(sp, 0, 1, 0)
                sp.dma_start(memr, mem[0].rearrange("(t p) d -> p t d", p=P)).then_inc(s_mem, 16)
                attention_loads(sp, 1, 2, 0)
                for i, g in enumerate((sb_q_norm[0], sb_k_norm[0], xa_q_norm[0], xa_k_norm[0])):
                    sp.dma_start(gcol[:, i:i + 1], col(g)).then_inc(s_gcol, 16)
                attention_loads(sp, 2, N0, 0)

            @block.gpsimd
            def _(pool):
                link = linker(pool, "pool")
                pool.memset(epsc[:], EPS).then_inc(s_const, 1)
                link(pool.memset(ident[:], 0.0))
                pool.affine_select(out=ident[:], in_=ident[:], compare_op=ALU.not_equal, fill=1.0, base=0,
                                   pattern=[[-1, P]], channel_multiplier=1).then_inc(s_const, 1)
                for v, val in ((ones[:], 1.0), (negones, -1.0), (diag0.rearrange("p a b -> p (a b)"), 1.0)):
                    link(pool.memset(v, val))
                pool.affine_select(out=upincl[:], in_=ones[:], compare_op=ALU.is_ge, fill=0.0, base=0,
                                   pattern=[[1, P]], channel_multiplier=-1).then_inc(s_const2, 1)
                link(pool.affine_select(out=upstrict[:], in_=ones[:], compare_op=ALU.is_gt, fill=0.0, base=0,
                                        pattern=[[1, P]], channel_multiplier=-1))
                pool.affine_select(out=negup, in_=negones, compare_op=ALU.is_ge, fill=0.0, base=0,
                                   pattern=[[-1, P]], channel_multiplier=1).then_inc(s_const2, 1)
                link(pool.memset(diagneg, 0.0))
                link(pool.affine_select(out=diagneg, in_=diagneg, compare_op=ALU.is_gt, fill=NEG, base=0,
                                        pattern=[[1, P]], channel_multiplier=-1))
                pool.tensor_copy(diagnegb[:], diagneg).then_inc(s_const2, 1)
                pool.wait_ge(s_const, 2)
                pool.tensor_copy(identb[:], ident[:]).then_inc(s_const2, 1)
                for a in (0, 2):
                    pool.tensor_copy(diag0[:, a, :], upstrict[:]).then_inc(s_const2, 1)
                norm_m.ready(pool, 2)
                pool.wait_ge(s_gmo, 1)
                for i, dst in enumerate((memT, memT1)):
                    pool.tensor_tensor(dst, memU, gmem[:, i, :].unsqueeze(2).to_broadcast([P, KC, S]), ALU.mult).then_inc(s_memg, 1)

            @block.scalar
            def _(act):
                link = linker(act, "act")
                act.preload_act_table_set("natural_log_exp_and_others")
                for norm in (norm_x, norm_m):
                    norm.act_squares(act, link)
                    norm.act_rstd(act, link)
                    norm.act_evacuate(act)

                def evacuate(n):
                    act.wait_ge(s_pj, n + 1)
                    act.activation(jobs_a[n][3], PS[:, 6, :], ACT.Copy).then_inc(s_pja, 1)

                evacuate(0)
                evacuate(2)
                cross0.act(act, link, lambda e: (e.wait_ge(s_pja, 2), e.wait_ge(s_pjd, 2)))
                act.wait_ge(s_g8, 1)
                cross0.act_evacuate(act)
                evacuate(4)
                for i in range(xa0.steps()):
                    xa0.act_step(act, i)
                    if (XJ + i // 2) % 2 == 0 and i % 2 == 1:
                        evacuate(XJ + i // 2)
                for t in range(NT):
                    if t == 0:
                        act.wait_ge(s_pja, QKJ // 2)
                    else:
                        act.wait_ge(s_pjd, QKJ // 2)
                        act.wait_ge(s_hms, t)
                    act.activation(sqs, proj[:, t, 0:2 * SBW], ACT.Square).then_inc(s_hsq, 1)
                    act.wait_ge(s_hms, t + 1)
                    link(act.activation(hst[:, t, 1, :], hst[:, t, 1, :], ACT.Ln))
                    act.activation(hst[:, t, 1, :], hst[:, t, 1, :], ACT.Exp, scale=-0.5).then_inc(s_hrs, 1)
                evacuate(QKJ)
                for j in range(NHJ):
                    act.wait_ge(s_ht, 2 * j + 1)
                    act.activation(qT[:, 2 * j:2 * j + 2, :], PS[0:HD, (2 * j) % 6, :].rearrange("p (h t) -> p h t", h=2),
                                   ACT.Copy, scale=gcol[:, 5:6]).then_inc(s_hta, 1)
                evacuate(QKJ + 2)

            @block.vector
            def _(dve):
                link = linker(dve, "dve")
                dve.wait_ge(s_gain, 16)
                norm_x.dve_rows(dve)
                dve.wait_ge(s_gmt, 1)
                dve.tensor_copy(gmem.rearrange("p l c -> p (l c)"), PS[:, 7, 0:2 * KC]).then_inc(s_gmo, 1)
                norm_m.dve_rows(dve)

                def evacuate(n):
                    dve.wait_ge(s_pj, n + 1)
                    dve.tensor_copy(jobs_a[n][3], PS[:, 7, :]).then_inc(s_pjd, 1)

                evacuate(1)
                dve.wait_ge(s_gcol, 64)
                for src, dst in ((2, 4), (0, 5)):
                    g = dve.tensor_scalar(gcol[:, dst:dst + 1], gcol[:, src:src + 1], HD ** -0.5, None, ALU.mult)
                g.then_inc(s_g8, 1)
                evacuate(3)
                cross0.dve(dve, link, lambda e: e.wait_ge(s_pja, 2))
                for i in range(xa0.steps()):
                    xa0.dve_step(dve, i)
                    if (XJ + i // 2) % 2 == 1 and i % 2 == 1:
                        evacuate(XJ + i // 2)
                for t in range(NT):
                    dve.wait_ge(s_hsq, t + 1)
                    link(dve.tensor_reduce(hst[:, t, 0, :], sqs.rearrange("p (h d) -> p h d", d=HD), X_AXIS, ALU.add))
                    dve.tensor_scalar(hst[:, t, 1, :], hst[:, t, 0, :], 1.0 / HD, EPS, ALU.mult, ALU.add).then_inc(s_hms, 1)
                    dve.wait_ge(s_hrs, t + 1)
                    w = proj[:, t, 0:2 * SBW].rearrange("p (h d) -> p h d", d=HD)
                    dve.tensor_tensor(w, w, hst[:, t, 1, :].unsqueeze(2).to_broadcast([P, 2 * SBH, HD]),
                                      ALU.mult).then_inc(s_hn, 1)
                evacuate(QKJ + 1)
                for j in range(NHJ):
                    dve.wait_ge(s_ht, 2 * j + 2)
                    dve.tensor_scalar(kT[:, 2 * j:2 * j + 2, :], PS[0:HD, (2 * j + 1) % 6, :].rearrange("p (h t) -> p h t", h=2),
                                      gcol[:, 1:2], None, ALU.mult).then_inc(s_htd, 1)
                evacuate(QKJ + 3)

            @block.tensor
            def _(pe):
                pe.wait_ge(s_const, 2)
                norm_x.pe(pe)
                pe.wait_ge(s_gmem, 16)
                pe.transpose(PS[:, 7, 0:2 * KC], gmem_rows, ident[0:2 * KC, 0:2 * KC]).then_inc(s_gmt, 1)
                norm_x.ready(pe, NT)
                for n, (rows, load, t, dst) in enumerate(jobs_a):
                    if rows is memT or rows is memT1:
                        pe.wait_ge(s_memg, 1 if rows is memT else 2)
                    w = weights_in(pe, load)
                    if n == 1:
                        pe.wait_ge(s_gmo, 1)
                    if n >= 2:
                        pe.wait_ge(s_pja if n % 2 == 0 else s_pjd, n // 2)
                    if n == QKJ + 2:
                        for j in range(2 * NHJ):
                            pe.wait_ge(s_hn, NT)
                            if j == 0:
                                pe.wait_ge(xa0.s_mix, 2 * XAH)
                            if j >= 6:
                                pe.wait_ge(s_hta if j % 2 == 0 else s_htd, (j - 6) // 2 + 1)
                            base = (j % 2) * SBW
                            for i in range(2):
                                h = 2 * (j // 2) + i
                                for tt in range(NT):
                                    mm = pe.transpose(PS[0:HD, j % 6, (i * NT + tt) * P:(i * NT + tt + 1) * P],
                                                      proj[:, tt, base + h * HD:base + (h + 1) * HD], ident[:])
                            mm.then_inc(s_ht, 1)
                    for k in range(KC):
                        mm = pe.matmul(PS[:, 6 + n % 2, :], rows[:, k, t * P:(t + 1) * P], w[:, k, :],
                                       start=(k == 0), stop=(k == KC - 1))
                        if k == 3 and XJ <= n < XJ + 5:
                            if n == XJ:
                                pe.wait_ge(cross0.s_eva, 4)
                            xa0.pe_step(pe, 2 * (n - XJ))
                    mm.then_inc(s_pj, 1)
                    if n == 0:
                        norm_m.pe(pe)
                    if n == XJ - 1:
                        cross0.pe(pe, lambda e, j: None)
                    if XJ <= n < XJ + 5:
                        xa0.pe_step(pe, 2 * (n - XJ) + 1)

        s_z, s_ab, s_ex, s_ln, s_Lr, s_L, s_cum, s_a, s_o, s_oe = (
            lsem(f"b_{n}") for n in ("z", "abs", "exp", "ln", "Lraw", "L", "cum", "a", "o", "o_out"))
        norm_c = NormTransposeSplit("nc", [None] * NT)
        op0 = OutProjection("op0", mix, [aslot(N0 - 2, 512), aslot(N0 - 1, 512)], lambda pe, half: weights_in(pe, N0 - 2 + half))
        v_tok = proj[:, :, 2 * SBW:3 * SBW]

        with nc.Block() as block:
            @block.tensor
            def _(pe):
                pe.wait_ge(s_const2, 6)
                for i in range(SBH + 2):
                    if i < SBH:
                        z = PS[:, i % 3, :]
                        if i >= 3:
                            pe.wait_ge(s_a, i - 2)
                        pe.matmul(z[:, 0:S], kT[:, i, 0:P], qT[:, i, :], start=True, stop=True, skip_group_check=True)
                        pe.matmul(z[:, S:S + P], kT[:, i, P:S], qT[:, i, P:S], start=False, stop=True,
                                  skip_group_check=True).then_inc(s_z, 1)
                    if 1 <= i <= SBH:
                        j = i - 1
                        z, L = PS[:, j % 3, :], hL[:, j % 2, :]
                        pe.wait_ge(s_L, j + 1)
                        for o, w, r in ((z[:, 0:S], negup, L[:, 0:S]), (z[:, P:S], negones, L[:, S:S + P]),
                                        (z[:, S:S + P], negup, L[:, S:S + P]),
                                        (z[:, 0:384].rearrange("p (a n) -> p a n", n=P)[:, 0:3:2, :], identb[:],
                                         diagnegb[:].unsqueeze(1).to_broadcast([P, 2, P]))):
                            mm = pe.matmul(o, w, r, start=False, stop=True, skip_group_check=True)
                        mm.then_inc(s_cum, 1)
                    if i >= 2:
                        j = i - 2
                        pe.wait_ge(s_a, j + 1)
                        if j >= 2:
                            pe.wait_ge(s_oe, j - 1)
                        o, A = PS[:, 3 + j % 2, :], hA[:, j % 2, :]
                        vh = slice(j * HD, (j + 1) * HD)
                        pe.matmul(o[:, 0:HD], A[:, 0:P], v_tok[:, 0, vh], start=True, stop=True)
                        pe.matmul(o[:, HD:2 * HD], A[:, P:S], v_tok[:, 0, vh], start=True, stop=False)
                        pe.matmul(o[:, HD:2 * HD], A[:, S:S + P], v_tok[:, 1, vh], start=False, stop=True).then_inc(s_o, 1)
                op0.pe(pe, lambda e, t: (e.wait_ge(s_a, SBH), e.wait_ge(s_oe, SBH)))

            @block.scalar
            def _(act):
                for i in range(SBH + 1):
                    if i < SBH:
                        act.wait_ge(s_z, i + 1)
                        if i >= 2:
                            act.wait_ge(s_Lr, i - 1)
                        act.activation(habs[:, i % 2, :], PS[:, i % 3, 0:384], ACT.Abs).then_inc(s_ab, 1)
                        act.wait_ge(s_ab, i + 1)
                        act.activation(habs[:, i % 2, :], habs[:, i % 2, :], ACT.Exp, scale=-1.0).then_inc(s_ex, 1)
                        act.wait_ge(s_ex, i + 1)
                        act.activation(hln[:, i % 2, :], habs[:, i % 2, :], ACT.Ln, bias=1.0).then_inc(s_ln, 1)
                    if i >= 1:
                        j = i - 1
                        act.wait_ge(s_cum, j + 1)
                        if j >= 2:
                            act.wait_ge(s_o, j - 1)
                        act.activation(hA[:, j % 2, :], PS[:, j % 3, 0:384], ACT.Exp).then_inc(s_a, 1)
                for t in range(NT):
                    op0.act_evacuate(act, t)
                norm_c.act_row_squares(act, op0.s_x)

            @block.vector
            def _(dve):
                for i in range(SBH + 2):
                    if i < SBH:
                        dve.wait_ge(s_ln, i + 1)
                        if i >= 2:
                            dve.wait_ge(s_cum, i - 1)
                        dve.scalar_tensor_tensor(out=hL[:, i % 2, :], in0=PS[:, i % 3, 0:384], scalar=0.0, in1=hln[:, i % 2, :],
                                                 op0=ALU.max, op1=ALU.add).then_inc(s_Lr, 1)
                        dve.wait_ge(s_Lr, i + 1)
                        dve.tensor_tensor(hL[:, i % 2, :], hL[:, i % 2, :], diag0.rearrange("p a b -> p (a b)"),
                                          ALU.mult).then_inc(s_L, 1)
                    if i >= 2:
                        j = i - 2
                        dve.wait_ge(s_o, j + 1)
                        dve.tensor_copy(mix[:, :, j * HD:(j + 1) * HD],
                                        PS[:, 3 + j % 2, 0:2 * HD].rearrange("p (t d) -> p t d", t=NT)).then_inc(s_oe, 1)
                for t in range(NT):
                    op0.dve_evacuate(dve, t)
                op0.dve_sums(dve)

            @block.sync
            def _(sp):
                sp.dma_start(gain[:, 0, :], row(ffn_norm[0], D)).then_inc(s_gain_ffn0, 16)

        s_w = [sem(f"s_w{i}") for i in range(STAGES)]
        NB = GF // P
        GPP = 3 * NG
        GATE, UP, DOWN = range(3)

        def part_no(n, g, kind):
            return GPP * n + 3 * g + (kind if kind != DOWN else 2 + 6)

        def stage_of(g, kind):
            return part_no(0, g, kind) % STAGES

        def landed(eng, n, g, kind):
            at = part_no(0, g, kind)
            uses = at // STAGES + (0 if at % STAGES in (2, 5) else 1)
            eng.wait_ge(s_w[at % STAGES], 16 * (n * (GPP // STAGES) + uses))

        def split_no(g, kind, alone, last):
            if kind == DOWN:
                return 3 * g + 7 if g < NG - 2 or not last else GPP - (NG - 1 - g)
            if g >= 2:
                return 3 * g - 1 + kind
            return (2 * g + kind + 1) if alone else 3 * g - 1 + kind

        def staged(g, kind):
            return stage[:, stage_of(g, kind), :]

        def load_part(eng, w, g, kind):
            if kind == DOWN:
                src = w[DOWN].rearrange("(g b p) d -> g p b d", b=NB, p=P)[g]
                dst = staged(g, kind).rearrange("p (b d) -> p b d", b=NB)
            else:
                src = k_rows(w[kind])[:, :, g * GF:(g + 1) * GF]
                dst = staged(g, kind).rearrange("p (c f) -> p c f", c=KC)
            eng.dma_start(dst, src).then_inc(s_w[stage_of(g, kind)], 16)

        def reload_part(eng, n, w, g, kind, alone, first=False):
            before = part_no(0, g, kind) - STAGES
            if before >= 0 and before not in (2, 5):
                k = before % 3
                bg = before // 3 if k != DOWN else (before - 8) // 3
                eng.wait_ge(s_lo[0], GPP * n + split_no(bg, k, alone, False))
            elif not alone:
                eng.wait_ge(s_lo[0], GPP * n + before - 1)
            elif not first:
                eng.wait_ge(s_lo[0], GPP * n)
            load_part(eng, w, g, kind)

        def split_views(g, kind):
            if kind == DOWN:
                return (staged(g, kind), wdh[:, g % 2, :], wdl[:, g % 2, :])
            return (staged(g, kind).rearrange("p (c f) -> p c f", c=KC), wgh[:, g % 2, :, kind, :], wgl[:, g % 2, :, kind, :])

        def act_high(act, n, g, kind, signal):
            landed(act, n, g, kind)
            src, hi, lo = split_views(g, kind)
            act.activation(hi, src, ACT.Copy).then_inc(signal, 1)

        def dve_rest(dve, g, kind, signal):
            src, hi, lo = split_views(g, kind)
            dve.tensor_tensor(lo, src, hi.bitcast(F32), ALU.subtract).then_inc(signal, 1)

        def three_passes(pe, out, left, right, start, stop):
            pe.matmul(out, left[0], right[0], start=start, stop=False)
            pe.matmul(out, left[0], right[1], start=False, stop=False)
            return pe.matmul(out, left[1], right[0], start=False, stop=stop)

        def feed_forward_memory(tag):
            next_memory()
            return (psb(f"stage{tag}", [P, STAGES, PART]),
                    psb(f"wgh{tag}", [P, 2, KC, 2, GF], F32R), psb(f"wgl{tag}", [P, 2, KC, 2, GF], F32R),
                    psb(f"wdh{tag}", [P, 2, NB * D], F32R), psb(f"wdl{tag}", [P, 2, NB * D], F32R))

        stage, wgh, wgl, wdh, wdl = feed_forward_memory(0)
        hTh, hTl = psb("hTh", [P, KC, S], F32R), psb("hTl", [P, KC, S], F32R)
        hh, hl = psb("hh0", [P, 2, NB, S], F32R), psb("hl0", [P, 2, NB, S], F32R)
        sg = xn[:, 0, :].rearrange("p (i b t) -> p i b t", i=2, b=NB)
        hm = xn[:, 1, :].rearrange("p (i b t) -> p i b t", i=2, b=NB)
        norm_c.units = [(X[:, t, :], gain[:, 0, :], (hTh[:, :, t * P:(t + 1) * P], hTl[:, :, t * P:(t + 1) * P]),
                         (s_gain_ffn0, 16)) for t in range(NT)]
        c_hi, c_lo, c_gu, c_sg, c_hm, c_hh, c_hl, c_dn, c_x = (
            lsem(f"c_{n}") for n in ("hi", "lo", "gu", "silu", "hm", "hh", "hl", "down", "x"))
        s_lo = [c_lo]
        dense_w = (ffd_w_gate[0], ffd_w_up[0], ffd_w_down[0])

        def steps_parts(g):
            return [(g + 2, GATE), (g + 2, UP)] * (g + 2 < NG) + [(g, DOWN)]

        FIRST_PARTS = [(0, GATE), (0, UP), (1, GATE), (1, UP)]

        with nc.Block() as block:
            @block.sync
            def _(sp):
                for g, kind in FIRST_PARTS:
                    load_part(sp, dense_w, g, kind)
                for g in range(NG):
                    for pg, kind in steps_parts(g):
                        reload_part(sp, 0, dense_w, pg, kind, True, first=True)
                sp.dma_start(gain[:, 1, :], row(mix_norm[1], D)).then_inc(s_gain_mix1, 16)

            @block.scalar
            def _(act):
                link = linker(act, "act")
                norm_c.act_rstd(act, link)
                norm_c.act_evacuate(act)
                for g, kind in FIRST_PARTS:
                    act_high(act, 0, g, kind, c_hi)
                for g in range(NG):
                    act.wait_ge(c_gu, g + 1)
                    if g >= 2:
                        act.wait_ge(c_hm, g - 1)
                    act.activation(sg[:, g % 2], PS[:, 2 * (g % 2):2 * (g % 2) + 2, 0:S], ACT.Silu).then_inc(c_sg, 1)
                    for pg, kind in steps_parts(g):
                        if kind == DOWN:
                            act.wait_ge(c_hm, g + 1)
                            if g >= 2:
                                act.wait_ge(c_dn, g - 1)
                            act.activation(hh[:, g % 2], hm[:, g % 2], ACT.Copy).then_inc(c_hh, 1)
                        act_high(act, 0, pg, kind, c_hi)

            @block.vector
            def _(dve):
                dve.wait_ge(s_gain_ffn0, 16)
                norm_c.dve_rows(dve)
                done = 0
                for g, kind in FIRST_PARTS:
                    done += 1
                    dve.wait_ge(c_hi, done)
                    dve_rest(dve, g, kind, c_lo)
                for g in range(NG):
                    dve.wait_ge(c_sg, g + 1)
                    if g >= 2:
                        dve.wait_ge(c_hl, g - 1)
                    dve.tensor_tensor(hm[:, g % 2], sg[:, g % 2], PS[:, 2 * (g % 2):2 * (g % 2) + 2, S:2 * S], ALU.mult).then_inc(c_hm, 1)
                    for pg, kind in steps_parts(g):
                        if kind == DOWN:
                            dve.wait_ge(c_hh, g + 1)
                            dve.tensor_tensor(hl[:, g % 2], hm[:, g % 2], hh[:, g % 2].bitcast(F32), ALU.subtract).then_inc(c_hl, 1)
                        done += 1
                        dve.wait_ge(c_hi, done)
                        dve_rest(dve, pg, kind, c_lo)
                dve.wait_ge(c_dn, NG)
                for t in range(NT):
                    xv = X[:, t, :].rearrange("p (a n) -> p a n", a=2)
                    dve.tensor_tensor(xv, xv, PS[:, 4 + 2 * t:6 + 2 * t, :], ALU.add).then_inc(c_x, 1)

            @block.tensor
            def _(pe):
                norm_c.pe(pe)
                norm_c.ready(pe, NT)
                for g in range(NG + 1):
                    if g < NG:
                        if g >= 2:
                            pe.wait_ge(c_hm, g - 1)
                        for kind in (GATE, UP):
                            pe.wait_ge(c_lo, split_no(g, kind, True, True))
                            for b in range(NB):
                                bs = slice(b * P, (b + 1) * P)
                                for k in range(KC):
                                    mm = three_passes(pe, PS[:, 2 * (g % 2) + b, kind * S:(kind + 1) * S],
                                                      (wgh[:, g % 2, k, kind, bs], wgl[:, g % 2, k, kind, bs]),
                                                      (hTh[:, k, :], hTl[:, k, :]), k == 0, k == KC - 1)
                        mm.then_inc(c_gu, 1)
                    if g >= 1:
                        j = g - 1
                        pe.wait_ge(c_hl, j + 1)
                        pe.wait_ge(c_lo, split_no(j, DOWN, True, True))
                        for b in range(NB):
                            for t in range(NT):
                                ts = slice(t * P, (t + 1) * P)
                                for half in range(2):
                                    ws = slice(b * D + half * 512, b * D + (half + 1) * 512)
                                    mm = three_passes(pe, PS[:, 4 + 2 * t + half, :], (hh[:, j % 2, b, ts], hl[:, j % 2, b, ts]),
                                                      (wdh[:, j % 2, ws], wdl[:, j % 2, ws]), j == 0 and b == 0, j == NG - 1 and b == NB - 1)
                        mm.then_inc(c_dn, 1)

        next_layer()
        next_memory()
        hT = psb("hT1", [P, KC, S])
        ring = psb("ring1", [P, ARENA])
        NCH = 3 * DNW // P
        CT_ = 4
        NP_ = NT * DNH
        sd = Scratch()
        qkvT = sd.tile(P, NCH, S)
        gate = sd.tile(P, NT, DNW)
        last = sd.tile(P, NT, 2 * DNH + XAW)
        xqT1 = sd.tile(HD, XAH, S)
        xkT1 = sd.tile(HD, XAH, S)
        mix1 = sd.tile(P, NT, D)
        convr = sd.tile(CT_ * NCH, P)
        convw = sd.tile(P, CT_ * NCH)
        alog = sd.tile(P, DNH)
        dtb = sd.tile(P, DNH)
        ogain = sd.tile(P, P)
        gcol1 = sd.tile(HD, 4)
        lowstrict = sd.tile(P, P)
        mask1 = sd.tile(P, P)
        SOLVE = 7
        maskT = sd.tile(P, SOLVE, P)
        tk = sd.tile(P, 12, NP_)
        on = sd.tile(P, 3, NP_)
        xtmp1 = (sd.tile(P, 2, S), sd.tile(P, 2, S), sd.tile(P, 3, 8))
        xst1 = sd.tile(P, 2, NT * 2 * XAH)
        norm_d = NormTranspose("nd", [(X[:, t, :], gain[:, 1, :], hT[:, :, t * P:(t + 1) * P], (s_gain_mix1, 16)) for t in range(NT)])
        s_small = lsem("s_small")
        s_cwt, s_cw, s_cv, s_y0, s_y1, s_y2, s_yc, s_si, s_tok, s_toke, s_mask = (
            lsem(f"d_{n}") for n in ("cwt", "cw", "cv", "y0", "y1", "y2", "y", "silu", "tok", "tok_out", "mask"))
        jobs_d = [(N0, t, last[:, t, :], DN_IN - 4 * DNW, ACT.Copy, 6 + t) for t in range(NT)] + \
                 [(N0 + 7 + c, t, gate[:, t, c * QK:(c + 1) * QK], QK, ACT.Silu, (0, 1, 2, 5)[NT * c + t]) for c in range(2) for t in range(NT)]
        NTJ = len(jobs_d)
        CPL = QK // P
        norm_f = NormTranspose("nf", [None] * NT)
        op1 = OutProjection("op1", mix1, [aslot(len(loads) - 2, 512), aslot(len(loads) - 1, 512)],
                            lambda pe, half: weights_in(pe, len(loads) - 2 + half))
        load_read[N0 - ASLOTS:] = [None] * (N0 - len(load_read[:N0 - ASLOTS]))
        load_read += [(s_tok, NT)] + [(s_cv, CPL * (i + 1)) for i in range(6)] + [(s_tok, NT * (i + 2)) for i in range(2)]
        QKC = 2 * DNH
        XC = 4
        LC = XC + 2 * XAH + 3

        vb = sd.tile(P, NP_, P)
        kdec = sd.tile(P, DNH, P)
        nkbg = sd.tile(P, DNH, P)
        qd = sd.tile(P, DNH, P)
        Dm = sd.tile(P, NP_, P)
        DT = sd.tile(P, NP_, P)
        A = sd.tile(P, NP_, P)
        AT = sd.tile(P, NP_, P)
        T = sd.tile(P, NP_, P)
        TT = sd.tile(P, NP_, P)
        W = Dm
        rg = T
        sq2 = TT.rearrange("p a b -> p (a b)")[:, 0:4 * S].rearrange("p (i a b) -> p i a b", i=2, a=2)
        CT = [qkvT[:, 2 * DNH:3 * DNH, :].rearrange("p c (t n) -> p (c t) n", n=P), A]
        U0, St = T[:, 0:DNH, :], T[:, DNH:NP_, :]
        wT, V1, Osb, Osq = W[:, 0:DNH, :], A[:, 0:DNH, :], AT, T
        sqx1 = vb.rearrange("p a b -> p (a b)")[:, 0:NT * 2 * XAW].rearrange("p (t n) -> p t n", t=NT)
        cross1 = CrossPrep("cp1", last[:, :, 2 * DNH:], kv1, xqT1, xkT1, sqx1, xst1, gcol1[:, 2:3], gcol1[:, 1:2], (4, 5, 4, 5))
        xa1 = Cross("xa1", xqT1, xkT1, kv1[:, :, XAW:2 * XAW], mix1, DNW, xtmp1)
        PQ = 4
        NQ = NP_ // PQ
        e = {n: lsem(f"e_{n}") for n in (
            "g8", "xa", "abs", "exp", "ln", "alog", "eb", "g", "beta", "rg", "gc", "gcs", "egc", "kdarg", "kd", "nb",
            "G", "Darg", "Dexp", "egr", "Dmask", "DTmask", "sq", "sum", "lnr", "r", "qn", "kn", "qd",
            "tr", "vb", "kt", "KK", "KQ", "A", "qk", "At", "AT", "T0", "TT0", "CT", "W", "We", "PP", "Tn", "TTn",
            "U", "Ue", "S", "Se", "wT", "wTe", "V", "Ve", "O", "Oe", "osq", "oms", "ors", "gg", "o1", "mix")}

        def banks4(b):
            return PS[:, b, :].rearrange("p (a n) -> p a n", a=PQ)

        def trio(v, q):
            return v[:, q * PQ:(q + 1) * PQ, :]

        with nc.Block() as block:
            @block.sync
            def _(sp):
                sp.dma_start(convr, dn_conv[0].rearrange("j (c p) -> (j c) p", p=P)).then_inc(s_small, 16)
                sp.dma_start(alog, row(dn_a_log[0], DNH)).then_inc(s_small, 16)
                sp.dma_start(dtb, row(dn_dt_bias[0], DNH)).then_inc(s_small, 16)
                sp.dma_start(ogain, row(dn_o_norm[0], P)).then_inc(s_small, 16)
                for i, g in enumerate((xa_q_norm[1], xa_k_norm[1])):
                    sp.dma_start(gcol1[:, i:i + 1], col(g)).then_inc(s_small, 16)
                attention_loads(sp, N0, N0 + 4, N0)
                sp.dma_start(gain[:, 0, :], row(ffn_norm[1], D)).then_inc(s_gain_ffn1, 16)
                attention_loads(sp, N0 + 4, len(loads), N0)

            @block.gpsimd
            def _(pool):
                link = linker(pool, "pool")
                pool.affine_select(out=lowstrict, in_=ones[:], compare_op=ALU.is_gt, fill=0.0, base=0,
                                   pattern=[[-1, P]], channel_multiplier=1).then_inc(s_mask, 1)
                link(pool.memset(maskT.rearrange("p a b -> p (a b)"), 0.0))
                link(pool.memset(mask1, 0.0))
                pool.affine_select(out=mask1.rearrange("p (a h) -> p a h", h=2)[:, :, 0], in_=mask1.rearrange("p (a h) -> p a h", h=2)[:, :, 0],
                                   compare_op=ALU.not_equal, fill=1.0, base=-1, pattern=[[-2, P // 2]],
                                   channel_multiplier=1).then_inc(s_mask, 1)
                for i in range(SOLVE):
                    s = 1 << i
                    v = maskT[:, i, :].rearrange("p (a h b) -> p a h b", h=2, b=s)[:, :, 1, :]
                    link(pool.memset(v, 1.0))
                    link(pool.affine_select(out=v, in_=v, compare_op=ALU.is_ge, fill=0.0, base=0,
                                            pattern=[[-2 * s, P // (2 * s)], [0, s]], channel_multiplier=1))
                    pool.affine_select(out=v, in_=v, compare_op=ALU.is_ge, fill=0.0, base=s - 1,
                                       pattern=[[2 * s, P // (2 * s)], [0, s]], channel_multiplier=-1).then_inc(s_mask, 1)
                pool.wait_ge(s_mask, 1)
                pool.wait_ge(e["Dexp"], 2)
                pool.tensor_tensor(DT, DT, upincl[:].unsqueeze(1).to_broadcast([P, NP_, P]), ALU.mult).then_inc(e["DTmask"], 1)
                pool.tensor_tensor(Dm, Dm, lowstrict.unsqueeze(1).to_broadcast([P, NP_, P]), ALU.mult).then_inc(e["Dmask"], 1)

            @block.scalar
            def _(act):
                link = linker(act, "act")
                norm_d.act_squares(act, link)
                norm_d.act_rstd(act, link)
                norm_d.act_evacuate(act)

                def evacuate(n):
                    load, t, dst, cols, f, bank = jobs_d[n]
                    act.wait_ge(s_tok, n + 1)
                    act.activation(dst, PS[:, bank, 0:cols], f).then_inc(s_toke, 1)

                for n in range(NT):
                    evacuate(n)
                act.wait_ge(e["xa"], 1)
                act.activation(tk[:, 1, :], tk[:, 0, :], ACT.Abs).then_inc(e["abs"], 1)
                act.wait_ge(e["abs"], 1)
                act.activation(tk[:, 1, :], tk[:, 1, :], ACT.Exp, scale=-1.0).then_inc(e["exp"], 1)
                act.wait_ge(e["exp"], 1)
                act.activation(tk[:, 1, :], tk[:, 1, :], ACT.Ln, bias=1.0).then_inc(e["ln"], 1)
                act.activation(alog, alog, ACT.Exp).then_inc(e["alog"], 1)
                act.activation(tk[:, 3, :].rearrange("p (t h) -> p t h", t=NT), last[:, :, DNH:2 * DNH], ACT.Exp,
                               scale=-1.0).then_inc(e["eb"], 1)
                cross1.act(act, link, lambda eng: eng.wait_ge(s_toke, NT))
                act.wait_ge(e["g8"], 1)
                cross1.act_evacuate(act)
                act.wait_ge(e["gcs"], 1)
                act.activation(tk[:, 6, :], tk[:, 5, :], ACT.Exp).then_inc(e["egc"], 1)
                act.wait_ge(e["kdarg"], 1)
                act.activation(tk[:, 8, :], tk[:, 8, :], ACT.Exp).then_inc(e["kd"], 1)
                act.wait_ge(e["Darg"], 2 * NP_)
                act.activation(DT, DT, ACT.Exp).then_inc(e["Dexp"], 1)
                act.activation(Dm, Dm, ACT.Exp, scale=-1.0).then_inc(e["Dexp"], 1)
                act.activation(qd[:, 0:2, :], banks4(1)[:, 2:4, :], ACT.Exp).then_inc(e["egr"], 1)
                act.activation(qd[:, 2:6, :], banks4(2), ACT.Exp).then_inc(e["egr"], 1)
                for i in range(xa1.steps()):
                    xa1.act_step(act, i)
                act.wait_ge(s_yc, QKC)
                act.activation(qkvT[:, 0:QKC, :], qkvT[:, 0:QKC, :], ACT.Silu).then_inc(s_si, 1)
                act.wait_ge(s_si, 1)
                for h in range(DNH):
                    if h >= 2:
                        act.wait_ge(e["kn"], h - 1)
                    act.activation(sq2[:, h % 2], qkvT[:, h:h + DNH + 1:DNH, :], ACT.Square).then_inc(e["sq"], 1)
                    act.wait_ge(e["sum"], h + 1)
                    act.activation(sq2[:, h % 2], PS[:, 3 + h % 2, :].rearrange("p (a b) -> p a b", a=2), ACT.Ln,
                                   bias=epsc[:]).then_inc(e["lnr"], 1)
                    act.wait_ge(e["lnr"], h + 1)
                    act.activation(sq2[:, h % 2], sq2[:, h % 2], ACT.Exp, scale=-0.5).then_inc(e["r"], 1)
                act.wait_ge(s_yc, NCH)
                act.activation(qkvT[:, QKC:NCH, :], qkvT[:, QKC:NCH, :], ACT.Silu).then_inc(s_si, 1)
                for n in range(NT, NTJ):
                    evacuate(n)

            @block.vector
            def _(dve):
                link = linker(dve, "dve")

                def convolve(c):
                    dve.wait_ge(s_cv, c + 1)
                    xp, y = PS[:, 6 + c % 2, 0:S], qkvT[:, c, :]

                    def tap(j):
                        return convw[:, j * NCH + c:j * NCH + c + 1]
                    dve.tensor_scalar(y, xp, tap(3), None, ALU.mult).then_inc(s_y0, 1)
                    for back, before, after in ((1, s_y0, s_y1), (2, s_y1, s_y2), (3, s_y2, s_yc)):
                        dve.wait_ge(before, c + 1)
                        dve.scalar_tensor_tensor(out=y[:, back:S], in0=xp[:, 0:S - back], scalar=tap(3 - back),
                                                 in1=y[:, back:S], op0=ALU.mult, op1=ALU.add).then_inc(after, 1)

                def th(v):
                    return v.rearrange("p (t h) -> p t h", t=NT)

                norm_d.dve_rows(dve)
                dve.wait_ge(s_small, 96)
                dve.tensor_scalar(gcol1[:, 2:3], gcol1[:, 0:1], HD ** -0.5, None, ALU.mult).then_inc(e["g8"], 1)
                dve.wait_ge(s_cwt, 1)
                dve.tensor_copy(convw, PS[:, 5, 0:CT_ * NCH]).then_inc(s_cw, 1)
                dve.wait_ge(s_cw, 1)
                dve.wait_ge(s_toke, NT)
                dve.tensor_tensor(th(tk[:, 0, :]), last[:, :, 0:DNH], dtb.unsqueeze(1).to_broadcast([P, NT, DNH]), ALU.add).then_inc(e["xa"], 1)
                convolve(0)
                dve.wait_ge(e["ln"], 1)
                link(dve.scalar_tensor_tensor(out=tk[:, 2, :], in0=tk[:, 0, :], scalar=0.0, in1=tk[:, 1, :], op0=ALU.max, op1=ALU.add))
                dve.wait_ge(e["alog"], 1)
                dve.scalar_tensor_tensor(out=th(tk[:, 2, :]), in0=th(tk[:, 2, :]), scalar=-1.0,
                                         in1=alog.unsqueeze(1).to_broadcast([P, NT, DNH]), op0=ALU.mult, op1=ALU.mult).then_inc(e["g"], 1)
                dve.wait_ge(e["eb"], 1)
                link(dve.tensor_scalar(tk[:, 3, :], tk[:, 3, :], 1.0, None, ALU.add))
                dve.reciprocal(tk[:, 4, :], tk[:, 3, :]).then_inc(e["beta"], 1)
                dve.wait_ge(e["g"], 1)
                for p in range(NP_):
                    dve.tensor_scalar(rg[:, p, :], upincl[:], tk[:, 2, p:p + 1], None, ALU.mult).then_inc(e["rg"], 1)
                convolve(1)
                cross1.dve(dve, link, lambda eng: eng.wait_ge(s_toke, NT))
                dve.wait_ge(e["gc"], 1)
                dve.tensor_copy(tk[:, 5:8:2, :], PS[:, 3, 0:2 * NP_].rearrange("p (a n) -> p a n", a=2)).then_inc(e["gcs"], 1)
                dve.wait_ge(e["gcs"], 1)
                dve.tensor_tensor(tk[:, 8, :], tk[:, 7, :], tk[:, 5, :], ALU.subtract).then_inc(e["kdarg"], 1)
                convolve(2)
                for p in range(NP_):
                    if p % PQ == 0:
                        dve.wait_ge(e["G"], p // PQ + 1)
                    gp = banks4(p // PQ)[:, p % PQ, :]
                    dve.tensor_scalar(DT[:, p, :], gp, tk[:, 5, p:p + 1], 0.0, ALU.subtract, ALU.min).then_inc(e["Darg"], 1)
                    dve.tensor_scalar(Dm[:, p, :], gp, tk[:, 5, p:p + 1], 0.0, ALU.subtract, ALU.max).then_inc(e["Darg"], 1)
                convolve(3)
                dve.wait_ge(e["egc"], 1)
                dve.wait_ge(e["beta"], 1)
                dve.scalar_tensor_tensor(out=tk[:, 9, :], in0=tk[:, 6, :], scalar=-1.0, in1=tk[:, 4, :],
                                         op0=ALU.mult, op1=ALU.mult).then_inc(e["nb"], 1)

                def l2_scale(h):
                    dve.wait_ge(e["r"], h + 1)
                    dve.scalar_tensor_tensor(out=qkvT[:, h, :], in0=qkvT[:, h, :], scalar=float(P) ** -0.5, in1=sq2[:, h % 2, 0, :],
                                             op0=ALU.mult, op1=ALU.mult).then_inc(e["qn"], 1)
                    kk = qkvT[:, DNH + h, :]
                    dve.tensor_tensor(kk, kk, sq2[:, h % 2, 1, :], ALU.mult).then_inc(e["kn"], 1)

                for c in range(4, NCH):
                    convolve(c)
                    if XC <= c < XC + xa1.steps():
                        xa1.dve_step(dve, c - XC)
                    if c > LC:
                        l2_scale(c - LC - 1)
                for h in range(NCH - LC - 1, DNH):
                    l2_scale(h)
                dve.wait_ge(e["egr"], 2)
                dve.wait_ge(e["qn"], DNH)
                dve.tensor_tensor(qd, qd, qkvT[:, 0:DNH, P:S], ALU.mult).then_inc(e["qd"], 1)

            @block.tensor
            def _(pe):
                norm_d.pe(pe)
                pe.wait_ge(s_small, 96)
                pe.transpose(PS[:, 5, 0:CT_ * NCH], convr, ident[0:CT_ * NCH, 0:CT_ * NCH]).then_inc(s_cwt, 1)

                def token_job(n):
                    load, t, dst, cols, f, bank = jobs_d[n]
                    w = weights_in(pe, load)
                    for k in range(KC):
                        mm = pe.matmul(PS[:, bank, 0:cols], hT[:, k, t * P:(t + 1) * P], w[:, k, :],
                                       start=(k == 0), stop=(k == KC - 1))
                    mm.then_inc(s_tok, 1)

                def squares(h):
                    if h == 0:
                        pe.wait_ge(xa1.s_mix, 2 * XAH)
                    pe.wait_ge(e["sq"], h + 1)
                    if h >= 2:
                        pe.wait_ge(e["r"], h - 1)
                    pe.matmul(PS[:, 3 + h % 2, :], ones[:], sq2[:, h % 2], start=True, stop=True).then_inc(e["sum"], 1)

                norm_d.ready(pe, NT)
                for n in range(NT):
                    token_job(n)
                for c in range(NCH):
                    w = weights_in(pe, N0 + 1 + c // CPL)
                    if c < 2:
                        pe.wait_ge(s_toke, c + 1)
                    else:
                        pe.wait_ge(s_yc, c - 1)
                    for k in range(KC):
                        mm = pe.matmul(PS[:, 6 + c % 2, 0:S], w[:, k, (c % CPL) * P:(c % CPL + 1) * P], hT[:, k, :],
                                       start=(k == 0), stop=(k == KC - 1))
                    mm.then_inc(s_cv, 1)
                    if c == 1:
                        pe.wait_ge(e["g"], 1)
                        pe.matmul(PS[:, 3, 0:NP_], upincl[:], tk[:, 2, :], start=True, stop=True)
                        pe.matmul(PS[:, 3, NP_:2 * NP_], ones[:], tk[:, 2, :], start=True, stop=True).then_inc(e["gc"], 1)
                        for q in range(NQ):
                            pe.wait_ge(e["rg"], PQ * (q + 1))
                            pe.matmul(PS[:, q, :], ones[:], trio(rg, q), start=True, stop=True).then_inc(e["G"], 1)
                    if c == 2:
                        pe.wait_ge(s_cw, 1)
                        cross1.pe(pe, lambda eng, j: eng.wait_ge(cross1.s_eva, j - 1) if j >= 2 else None)
                    if XC <= c < XC + xa1.steps():
                        if c == XC:
                            pe.wait_ge(cross1.s_eva, 4)
                            pe.wait_ge(e["gcs"], 1)
                            pe.wait_ge(e["Darg"], 2 * NP_)
                            pe.wait_ge(e["egr"], 2)
                        xa1.pe_step(pe, c - XC)
                    if c >= LC:
                        squares(c - LC)
                for n in range(NT, NTJ):
                    token_job(n)
                    if NCH - LC + n - NT < DNH:
                        squares(NCH - LC + n - NT)

        with nc.Block() as block:
            @block.scalar
            def _(act):
                link = linker(act, "act")
                for q in range(NQ):
                    act.wait_ge(e["tr"], q + 1)
                    for i in range(PQ):
                        p = q * PQ + i
                        act.activation(vb[:, p, :], banks4(5 + q)[:, i, :], ACT.Copy, scale=tk[:, 4, p:p + 1]).then_inc(e["vb"], 1)
                for q in range(NQ):
                    act.wait_ge(e["At"], q + 1)
                    act.activation(trio(AT, q), banks4(5 + q), ACT.Copy).then_inc(e["AT"], 1)
                for j in range((SOLVE - 1) * NQ):
                    act.wait_ge(e["W"], j + 1)
                    act.activation(trio(W, j % NQ), banks4(j % 2), ACT.Copy).then_inc(e["We"], 1)
                act.wait_ge(e["U"], 1)
                act.activation(U0[:, 0:4, :], banks4(0), ACT.Copy).then_inc(e["Ue"], 1)
                act.activation(U0[:, 4:6, :], banks4(1)[:, 0:2, :], ACT.Copy).then_inc(e["Ue"], 1)
                act.wait_ge(e["S"], 1)
                act.activation(St[:, 0:4, :], banks4(4), ACT.Copy).then_inc(e["Se"], 1)
                act.activation(St[:, 4:6, :], banks4(5)[:, 0:2, :], ACT.Copy).then_inc(e["Se"], 1)
                def outputs(t, b):
                    act.wait_ge(e["O"], t + 1)
                    act.activation(Osb[:, t * DNH:t * DNH + 4, :], banks4(b), ACT.Copy).then_inc(e["Oe"], 1)
                    act.activation(Osb[:, t * DNH + 4:t * DNH + 6, :], banks4(b + 1)[:, 0:2, :], ACT.Copy).then_inc(e["Oe"], 1)

                def squares(t):
                    act.wait_ge(e["Oe"], 2 * t + 2)
                    act.activation(Osq[:, t * DNH:(t + 1) * DNH, :], Osb[:, t * DNH:(t + 1) * DNH, :], ACT.Square).then_inc(e["osq"], 1)

                def root(t):
                    v = on[:, 1, t * DNH:(t + 1) * DNH]
                    act.wait_ge(e["oms"], t + 1)
                    link(act.activation(v, v, ACT.Ln))
                    act.activation(v, v, ACT.Exp, scale=-0.5).then_inc(e["ors"], 1)

                outputs(0, 6)
                act.wait_ge(e["V"], 1)
                act.activation(V1[:, 0:4, :], banks4(0), ACT.Copy).then_inc(e["Ve"], 1)
                act.activation(V1[:, 4:6, :], banks4(1)[:, 0:2, :], ACT.Copy).then_inc(e["Ve"], 1)
                squares(0)
                root(0)
                outputs(1, 2)
                squares(1)
                op1.act_evacuate(act, 0)
                root(1)
                op1.act_evacuate(act, 1)
                act.preload_act_table_set("natural_log_exp_and_others")
                norm_f.act_row_squares(act, op1.s_x)

            @block.gpsimd
            def _(pool):
                gv = gate.rearrange("p t (h d) -> p (t h) d", d=P)
                pool.tensor_tensor(gv, gv, ogain.unsqueeze(1).to_broadcast([P, NP_, P]), ALU.mult).then_inc(e["gg"], 1)
                pool.wait_ge(e["vb"], NP_)
                for i in range(1, SOLVE):
                    pool.wait_ge(e["AT"], NQ)
                    if i == 2:
                        pool.wait_ge(e["T0"], 1)
                    if i >= 3:
                        pool.wait_ge(e["W"], NQ * (i - 2))
                    pool.tensor_tensor(CT[(i - 1) % 2], AT, maskT[:, i, :].unsqueeze(1).to_broadcast([P, NP_, P]),
                                       ALU.mult).then_inc(e["CT"], 1)

            @block.vector
            def _(dve):
                link = linker(dve, "dve")

                for q in range(NQ):
                    dve.wait_ge(e["tr"], NQ + q + 1)
                    for i in range(PQ):
                        p = q * PQ + i
                        src = banks4((3, 4, 0)[q])[:, i, :]
                        if p < DNH:
                            dve.tensor_scalar(kdec[:, p, :], src, tk[:, 8, p:p + 1], None, ALU.mult).then_inc(e["kt"], 1)
                        else:
                            dve.tensor_scalar(nkbg[:, p - DNH, :], src, tk[:, 9, p:p + 1], None, ALU.mult).then_inc(e["kt"], 1)
                for q in range(NQ):
                    dve.wait_ge(e["KK"], q + 1)
                    for i in range(PQ):
                        p = q * PQ + i
                        dve.scalar_tensor_tensor(out=A[:, p, :], in0=banks4(1 + q)[:, i, :], scalar=tk[:, 4, p:p + 1],
                                                 in1=Dm[:, p, :], op0=ALU.mult, op1=ALU.mult).then_inc(e["A"], 1)
                dve.wait_ge(e["A"], NP_)
                idb = ident[:].unsqueeze(1).to_broadcast([P, NP_, P])
                link(dve.tensor_tensor(T, A, mask1.unsqueeze(1).to_broadcast([P, NP_, P]), ALU.mult))
                dve.tensor_tensor(T, idb, T, ALU.subtract).then_inc(e["T0"], 1)
                for q in range(NQ):
                    dve.wait_ge(e["KQ"], q + 1)
                    dve.tensor_tensor(trio(DT, q), trio(DT, q), banks4((4, 0, 1)[q]), ALU.mult).then_inc(e["qk"], 1)
                dve.wait_ge(e["AT"], NQ)
                link(dve.tensor_tensor(TT, AT, maskT[:, 0, :].unsqueeze(1).to_broadcast([P, NP_, P]), ALU.mult))
                dve.tensor_tensor(TT, idb, TT, ALU.subtract).then_inc(e["TT0"], 1)
                dve.wait_ge(e["T0"], 1)
                dve.wait_ge(e["TT0"], 1)
                for j in range((SOLVE - 1) * NQ):
                    q = j % NQ
                    dve.wait_ge(e["PP"], j + 1)
                    if j < (SOLVE - 2) * NQ:
                        dve.tensor_tensor(trio(T, q), trio(T, q), banks4(2 + q), ALU.subtract).then_inc(e["Tn"], 1)
                    dve.tensor_tensor(trio(TT, q), trio(TT, q), banks4(5 + q), ALU.subtract).then_inc(e["TTn"], 1)
                    if q == NQ - 1:
                        dve.wait_ge(e["TTn"], j + 1)
                        if j < (SOLVE - 2) * NQ:
                            dve.wait_ge(e["Tn"], j + 1)
                dve.wait_ge(e["wT"], 1)
                dve.tensor_copy(wT[:, 0:4, :], banks4(2)).then_inc(e["wTe"], 1)
                dve.tensor_copy(wT[:, 4:6, :], banks4(3)[:, 0:2, :]).then_inc(e["wTe"], 1)
                def mean(t):
                    ts = slice(t * DNH, (t + 1) * DNH)
                    dve.wait_ge(e["osq"], t + 1)
                    link(dve.tensor_reduce(on[:, 0, ts], Osq[:, ts, :], X_AXIS, ALU.add))
                    dve.tensor_scalar(on[:, 1, ts], on[:, 0, ts], 1.0 / P, EPS, ALU.mult, ALU.add).then_inc(e["oms"], 1)

                def gated(t):
                    o = Osb[:, t * DNH:(t + 1) * DNH, :]
                    dve.wait_ge(e["ors"], t + 1)
                    dve.tensor_tensor(o, o, on[:, 1, t * DNH:(t + 1) * DNH].unsqueeze(2).to_broadcast([P, DNH, P]), ALU.mult).then_inc(e["o1"], 1)
                    dve.wait_ge(e["o1"], t + 1)
                    dve.wait_ge(e["gg"], 1)
                    dve.tensor_tensor(mix1[:, t, 0:DNW].rearrange("p (h d) -> p h d", d=P), o,
                                      gate[:, t, :].rearrange("p (h d) -> p h d", d=P), ALU.mult).then_inc(e["mix"], 1)

                mean(0)
                gated(0)
                mean(1)
                op1.dve_evacuate(dve, 0)
                gated(1)
                op1.dve_evacuate(dve, 1)
                op1.dve_sums(dve)

            @block.tensor
            def _(pe):
                for q in range(NQ):
                    for i in range(PQ):
                        t, h = divmod(q * PQ + i, DNH)
                        mm = pe.transpose(banks4(5 + q)[:, i, :], qkvT[:, 2 * DNH + h, t * P:(t + 1) * P], ident[:])
                    mm.then_inc(e["tr"], 1)
                for q in range(NQ):
                    for i in range(PQ):
                        t, h = divmod(q * PQ + i, DNH)
                        mm = pe.transpose(banks4((3, 4, 0)[q])[:, i, :], qkvT[:, DNH + h, t * P:(t + 1) * P], ident[:])
                    mm.then_inc(e["tr"], 1)

                def products(b, other):
                    for i in range(PQ):
                        t, h = divmod(q * PQ + i, DNH)
                        kk = qkvT[:, DNH + h, t * P:(t + 1) * P]
                        mm = pe.matmul(banks4(b)[:, i, :], kk, qkvT[:, other + h, t * P:(t + 1) * P], start=True, stop=True)
                    return mm

                for q in range(NQ):
                    if q == 2:
                        pe.wait_ge(e["kt"], PQ)
                    products(1 + q, DNH).then_inc(e["KK"], 1)
                for q in range(NQ):
                    pe.wait_ge(e["kt"], (2 * PQ, 3 * PQ, 3 * PQ)[q])
                    if q == 2:
                        pe.wait_ge(e["A"], PQ)
                    products((4, 0, 1)[q], 0).then_inc(e["KQ"], 1)
                for q in range(NQ):
                    pe.wait_ge(e["A"], PQ * (q + 1))
                    pe.wait_ge(e["vb"], PQ * (q + 1))
                    for i in range(PQ):
                        mm = pe.transpose(banks4(5 + q)[:, i, :], A[:, q * PQ + i, :], ident[:])
                    mm.then_inc(e["At"], 1)
                pe.wait_ge(e["T0"], 1)
                pe.wait_ge(e["qk"], NQ)

                def first(j):
                    i, q = divmod(j, NQ)
                    pe.wait_ge(e["CT"], i + 1)
                    if i >= 1:
                        pe.wait_ge(e["Tn"], (i - 1) * NQ + q + 1)
                        pe.wait_ge(e["TTn"], (i - 1) * NQ + q + 1)
                    if j >= 2:
                        pe.wait_ge(e["We"], j - 1)
                    for a in range(PQ):
                        p = q * PQ + a
                        mm = pe.matmul(banks4(j % 2)[:, a, :], CT[i % 2][:, p, :], T[:, p, :], start=True, stop=True)
                    mm.then_inc(e["W"], 1)

                def second(j):
                    i, q = divmod(j, NQ)
                    if j == 0:
                        pe.wait_ge(e["TT0"], 1)
                    pe.wait_ge(e["We"], j + 1)
                    for a in range(PQ):
                        p = q * PQ + a
                        if i < SOLVE - 2:
                            pe.matmul(banks4(2 + q)[:, a, :], TT[:, p, :], W[:, p, :], start=True, stop=True)
                        mm = pe.matmul(banks4(5 + q)[:, a, :], W[:, p, :], TT[:, p, :], start=True, stop=True)
                    mm.then_inc(e["PP"], 1)

                for i in range(SOLVE - 1):
                    first(i * NQ)
                    first(i * NQ + 1)
                    second(i * NQ)
                    first(i * NQ + 2)
                    second(i * NQ + 1)
                    second(i * NQ + 2)
                pe.wait_ge(e["TTn"], (SOLVE - 1) * NQ)
                pe.wait_ge(e["We"], (SOLVE - 1) * NQ)

                def b2(b, h):
                    return banks4(b + h // PQ)[:, h % PQ, :]

                for h in range(DNH):
                    mm = pe.matmul(b2(0, h), TT[:, h, :], vb[:, h, :], start=True, stop=True)
                mm.then_inc(e["U"], 1)
                for h in range(DNH):
                    mm = pe.matmul(b2(2, h), nkbg[:, h, :], TT[:, DNH + h, :], start=True, stop=True)
                mm.then_inc(e["wT"], 1)
                pe.wait_ge(e["Ue"], 2)
                for h in range(DNH):
                    mm = pe.matmul(b2(4, h), kdec[:, h, :], U0[:, h, :], start=True, stop=True)
                mm.then_inc(e["S"], 1)
                pe.wait_ge(e["Se"], 2)
                for h in range(DNH):
                    mm = pe.matmul(b2(6, h), DT[:, h, :], U0[:, h, :], start=True, stop=True)
                mm.then_inc(e["O"], 1)
                pe.wait_ge(e["wTe"], 2)
                for h in range(DNH):
                    pe.matmul(b2(0, h), TT[:, DNH + h, :], vb[:, DNH + h, :], start=True, stop=False)
                    mm = pe.matmul(b2(0, h), wT[:, h, :], St[:, h, :], start=False, stop=True)
                mm.then_inc(e["V"], 1)
                pe.wait_ge(e["Ve"], 2)
                for h in range(DNH):
                    pe.matmul(b2(2, h), qd[:, h, :], St[:, h, :], start=True, stop=False)
                    mm = pe.matmul(b2(2, h), DT[:, DNH + h, :], V1[:, h, :], start=False, stop=True)
                mm.then_inc(e["O"], 1)
                pe.wait_ge(e["Oe"], 2)
                op1.pe(pe, lambda eng, t: eng.wait_ge(e["mix"], t + 1))

        stage, wgh, wgl, wdh, wdl = feed_forward_memory(1)
        hT = psb("hT2", [P, KC, S])
        norm_f.units = [(X[:, t, :], gain[:, 0, :], hT[:, :, t * P:(t + 1) * P], (s_gain_ffn1, 16)) for t in range(NT)]
        router = gain[:, 1, 0:KC * NE].rearrange("p (c e) -> p c e", c=KC)
        slotno = gain[:, 1, 64:64 + NPB * CAP]
        em8 = gain[:, 1, 400:400 + NE]
        rt = hT[:].rearrange("p c t -> p (c t)")[:, 0:16 * 16].rearrange("p (k t e) -> p k t e", k=16, t=NT)
        rs = hT[:].rearrange("p c t -> p (c t)")[:, 256:256 + 16].rearrange("p (k t) -> p k t", t=NT)
        posn = psb("posn", [P, NT, NE + 1])
        wgt = psb("wgt", [P, NT, NE + 1])
        cnt = psb("cnt", [1, NE + 1], I32)
        cntf = psb("cntf", [1, NE + 1])
        sel = psb("sel", [P, NT, CAP])
        selw = psb("selw", [P, NT, CAP])
        selT = psb("selT", [CAP, S])
        xeh, xel = psb("xeh", [P, KC, CAP], F32R), psb("xel", [P, KC, CAP], F32R)
        hh, hl = psb("hh1", [P, 2, NB, CAP], F32R), psb("hl1", [P, 2, NB, CAP], F32R)
        hflat = hT[:].rearrange("p c t -> p (c t)")
        ye = hflat[0:CAP, 0:D]
        sg = hflat[0:CAP, D:D + 2 * GF].rearrange("p (i f) -> p i f", i=2)
        hm = hflat[0:CAP, D + 2 * GF:D + 4 * GF].rearrange("p (i f) -> p i f", i=2)
        r = {n: lsem(f"f_{n}") for n in (
            "router", "iota", "lg", "lgo", "step", "d", "ed", "mask", "pos", "posn", "cnt")}
        m = {n: lsem(f"m_{n}") for n in (
            "sel", "selw", "gather", "xeh", "xel", "hi", "lo", "gu", "silu", "hm", "tr", "hh", "hl", "down",
            "selT", "selTo", "y", "scatter", "x")}
        s_lo[0] = m["lo"]

        def expert(ex):
            return (moe_w_gate[0][ex], moe_w_up[0][ex], moe_w_down[0][ex])

        def after(eng, name, n, per, count):
            if isinstance(n, int) and per * n + count <= 0:
                return
            eng.wait_ge(m[name], per * n + count)

        def step_parts(g, has_next):
            if g + 2 < NG:
                first = [(0, g + 2, kind) for kind in (GATE, UP)]
            elif has_next:
                first = [(1, g + 2 - NG, kind) for kind in (GATE, UP)]
            else:
                first = []
            return first + [(0, g, DOWN)]

        def sp_start(sp, n, ex):
            if not isinstance(n, int) or n > 0:
                sp.wait_ge(m["lo"], GPP * n)
            for g, kind in FIRST_PARTS:
                load_part(sp, expert(ex), g, kind)

        def sp_pass(sp, n, ex, alone, has_next):
            for g in range(NG):
                parts = step_parts(g, has_next)
                for ahead, pg, kind in parts[::-1] if g == 0 else parts:
                    reload_part(sp, n + ahead, expert(ex + ahead), pg, kind, alone and not ahead,
                                first=isinstance(n, int) and n == 0)

        def dve_select(dve, ex, b):
            for t in range(NT):
                dve.tensor_scalar(sel[:, t, :], slotno[:, b * CAP:(b + 1) * CAP], posn[:, t, bass.ds(ex, 1)], None,
                                  ALU.is_equal).then_inc(m["sel"], 1)

        def pe_gather(pe, n):
            after(pe, "sel", n, NT, NT)
            for c in range(KC):
                for t in range(NT):
                    mm = pe.matmul(PS[:, c // 4, (c % 4) * CAP:(c % 4 + 1) * CAP], xn[:, t, c * P:(c + 1) * P], sel[:, t, :],
                                   start=(t == 0), stop=(t == NT - 1))
            mm.then_inc(m["gather"], 1)

        def gathered(half):
            return PS[:, half, 0:4 * CAP].rearrange("p (c n) -> p c n", c=4)

        def act_gathered(act, n):
            after(act, "gather", n, 1, 1)
            for half in range(2):
                act.activation(xeh[:, 4 * half:4 * half + 4, :], gathered(half), ACT.Copy).then_inc(m["xeh"], 1)

        def dve_gathered(dve, n):
            for half in range(2):
                after(dve, "xeh", n, 2, half + 1)
                hs = slice(4 * half, 4 * half + 4)
                dve.tensor_tensor(xel[:, hs, :], gathered(half), xeh[:, hs, :].bitcast(F32), ALU.subtract).then_inc(m["xel"], 1)

        def pe_transpose(pe, n, g):
            after(pe, "hm", n, NG, g + 1)
            after(pe, "hl", n, NG, g - 1)
            for b in range(NB):
                mm = pe.transpose(PS[:, 6 + g % 2, b * CAP:(b + 1) * CAP], hm[:, g % 2, b * P:(b + 1) * P], ident[0:CAP, 0:CAP])
            mm.then_inc(m["tr"], 1)

        def pe_down(pe, n, g, last):
            after(pe, "hl", n, NG, g + 1)
            after(pe, "lo", n, GPP, split_no(g, DOWN, False, last))
            if g == 0:
                after(pe, "y", n, 2, 0)
            for b in range(NB):
                for half in range(2):
                    ws = slice(b * D + half * 512, b * D + (half + 1) * 512)
                    mm = three_passes(pe, PS[0:CAP, 4 + half, :], (hh[:, g % 2, b, :], hl[:, g % 2, b, :]),
                                      (wdh[:, g % 2, ws], wdl[:, g % 2, ws]), g == 0 and b == 0, g == NG - 1 and b == NB - 1)
            mm.then_inc(m["down"], 1)

        def pe_scatter(pe, n, t):
            if t == 0:
                after(pe, "selTo", n, 1, 1)
            for half in range(2):
                if t == 0:
                    after(pe, "y", n, 2, half + 1)
                else:
                    after(pe, "x", n, 4, half + 1)
                pe.matmul(PS[:, half, :], selT[:, t * P:(t + 1) * P], ye[:, half * 512:(half + 1) * 512],
                          start=True, stop=True).then_inc(m["scatter"], 1)

        def pe_pass(pe, n, alone, has_next):
            for g in range(NG):
                if g == 0:
                    after(pe, "xel", n, 2, 2)
                after(pe, "lo", n, GPP, split_no(g, UP, alone, not has_next))
                after(pe, "hm", n, NG, g - 1)
                for c in range(KC):
                    mm = three_passes(pe, PS[0:CAP, 2 + g % 2, :], (xeh[:, c, :], xel[:, c, :]),
                                      (wgh[:, g % 2, c].rearrange("p a f -> p (a f)"), wgl[:, g % 2, c].rearrange("p a f -> p (a f)")),
                                      c == 0, c == KC - 1)
                mm.then_inc(m["gu"], 1)
                if g >= 1:
                    pe_transpose(pe, n, g - 1)
                elif not alone:
                    pe_transpose(pe, n - 1, NG - 1)
                if g >= 2:
                    pe_down(pe, n, g - 2, not has_next)
                elif not alone:
                    pe_down(pe, n - 1, NG + g - 2, False)
                if g in (3, 5) and not alone:
                    pe_scatter(pe, n - 1, (g - 3) // 2)
                if g == 8:
                    after(pe, "selw", n, NT, NT)
                    after(pe, "x", n, 4, 0)
                    for t in range(NT):
                        mm = pe.transpose(PS[0:CAP, 0, t * P:(t + 1) * P], selw[:, t, :], ident[:])
                    mm.then_inc(m["selT"], 1)
                if g == NG - 2 and has_next:
                    after(pe, "selTo", n, 1, 1)
                    pe_gather(pe, n + 1)

        def pe_finish(pe, n):
            pe_transpose(pe, n, NG - 1)
            for g in (NG - 2, NG - 1):
                pe_down(pe, n, g, True)
            for t in range(NT):
                pe_scatter(pe, n, t)

        def act_hidden(act, n, g):
            after(act, "tr", n, NG, g + 1)
            after(act, "down", n, NG, g - 1)
            act.activation(hh[:, g % 2].rearrange("p b n -> p (b n)"), PS[:, 6 + g % 2, 0:NB * CAP], ACT.Copy).then_inc(m["hh"], 1)

        def act_results(act, n):
            after(act, "down", n, NG, NG)
            for half in range(2):
                act.activation(ye[:, half * 512:(half + 1) * 512], PS[0:CAP, 4 + half, :], ACT.Copy).then_inc(m["y"], 1)

        def act_start(act, n):
            for g, kind in FIRST_PARTS:
                act_high(act, n + 1, g, kind, m["hi"])

        def act_pass(act, n, ex, alone, has_next):
            for g in range(NG):
                after(act, "gu", n, NG, g + 1)
                if g == NG - 1 and has_next:
                    act_gathered(act, n + 1)
                after(act, "hm", n, NG, g - 1)
                act.activation(sg[:, g % 2, :], PS[0:CAP, 2 + g % 2, 0:GF], ACT.Silu).then_inc(m["silu"], 1)
                if g >= 1:
                    act_hidden(act, n, g - 1)
                elif not alone:
                    act_hidden(act, n - 1, NG - 1)
                for ahead, pg, kind in step_parts(g, has_next):
                    if kind == DOWN:
                        after(act, "down", n, NG, g - 1)
                    act_high(act, n + 1 + ahead, pg, kind, m["hi"])
                if g == 1 and not alone:
                    act_results(act, n - 1)

        def act_finish(act, n):
            act_hidden(act, n, NG - 1)
            act_results(act, n)

        def dve_hidden(dve, n, g):
            after(dve, "hh", n, NG, g + 1)
            dve.tensor_tensor(hl[:, g % 2].rearrange("p b n -> p (b n)"), PS[:, 6 + g % 2, 0:NB * CAP],
                              hh[:, g % 2].rearrange("p b n -> p (b n)").bitcast(F32), ALU.subtract).then_inc(m["hl"], 1)

        def dve_sums(dve, n, t):
            for half in range(2):
                after(dve, "scatter", n, 4, 2 * t + half + 1)
                xv = X[:, t, half * 512:(half + 1) * 512]
                dve.tensor_tensor(xv, xv, PS[:, half, :], ALU.add).then_inc(m["x"], 1)

        def dve_start(dve, n, first=0, end=len(FIRST_PARTS)):
            for i in range(first, end):
                g, kind = FIRST_PARTS[i]
                after(dve, "hi", n, GPP, i + 1)
                dve_rest(dve, g, kind, m["lo"])

        def dve_pass(dve, n, ex, alone, has_next):
            for g in range(NG):
                if g == NG - 1 and has_next:
                    dve_gathered(dve, n + 1)
                after(dve, "silu", n, NG, g + 1)
                after(dve, "tr", n, NG, g - 1)
                dve.tensor_tensor(hm[:, g % 2, :], sg[:, g % 2, :], PS[0:CAP, 2 + g % 2, GF:2 * GF], ALU.mult).then_inc(m["hm"], 1)
                if g >= 1:
                    dve_hidden(dve, n, g - 1)
                elif not alone:
                    dve_hidden(dve, n - 1, NG - 1)
                if g in (4, 6) and not alone:
                    dve_sums(dve, n - 1, (g - 4) // 2)
                for ahead, pg, kind in step_parts(g, has_next):
                    after(dve, "hi", n + ahead, GPP, split_no(pg, kind, alone and not ahead, not has_next))
                    dve_rest(dve, pg, kind, m["lo"])
                if g == 4:
                    for t in range(NT):
                        after(dve, "sel", n, NT, NT)
                        after(dve, "selT", n, 1, 0)
                        dve.tensor_scalar(selw[:, t, :], sel[:, t, :], wgt[:, t, bass.ds(ex, 1)], None, ALU.mult).then_inc(m["selw"], 1)
                if g == 9:
                    after(dve, "selT", n, 1, 1)
                    dve.tensor_copy(selT[:], PS[0:CAP, 0, 0:S]).then_inc(m["selTo"], 1)
                if g == 8 and has_next:
                    after(dve, "gather", n, 1, 1)
                    after(dve, "selw", n, NT, NT)
                    dve_select(dve, ex + 1, 0)

        def dve_finish(dve, n):
            dve_hidden(dve, n, NG - 1)
            for t in range(NT):
                dve_sums(dve, n, t)

        with nc.Block() as block:
            @block.sync
            def _(sp):
                load_part(sp, expert(0), *FIRST_PARTS[0])
                sp.dma_start(router, k_rows(moe_router[0])).then_inc(r["router"], 16)
                for g, kind in FIRST_PARTS[1:]:
                    load_part(sp, expert(0), g, kind)
                sp_pass(sp, 0, 0, True, True)
                with sp.Fori(1, NE - 1) as ex:
                    sp_pass(sp, ex, ex, False, True)
                sp_pass(sp, NE - 1, NE - 1, False, False)

            @block.gpsimd
            def _(pool):
                pool.iota(slotno, [[1, NPB * CAP]], base=0, channel_multiplier=0,
                          allow_small_or_imprecise_dtypes=True).then_inc(r["iota"], 1)
                pool.iota(em8, [[1, NE]], base=-NE, channel_multiplier=0,
                          allow_small_or_imprecise_dtypes=True).then_inc(r["iota"], 1)

            @block.scalar
            def _(act):
                link = linker(act, "act")
                norm_f.act_rstd(act, link)
                norm_f.act_evacuate(act)
                act_start(act, 0)
                act.wait_ge(r["d"], 1)
                act.activation(rs[:, 3, :], rs[:, 2, :], ACT.Exp).then_inc(r["ed"], 1)
                act_gathered(act, 0)
                act_pass(act, 0, 0, True, True)
                with act.Fori(1, NE - 1) as ex:
                    act_pass(act, ex, ex, False, True)
                act_pass(act, NE - 1, NE - 1, False, False)
                act_finish(act, NE - 1)

            @block.vector
            def _(dve):
                link = linker(dve, "dve")
                dve.wait_ge(s_gain_ffn1, 16)
                norm_f.dve_rows(dve)
                dve_start(dve, 0, 0, 2)
                dve.wait_ge(r["lg"], 1)
                dve.tensor_copy(rt[:, 0], PS[:, 2, 0:NT * NE].rearrange("p (t e) -> p t e", t=NT)).then_inc(r["lgo"], 1)
                dve.wait_ge(r["lgo"], 1)
                dve.wait_ge(r["iota"], 2)
                em8b = em8.unsqueeze(1).to_broadcast([P, NT, NE])

                def bc(v):
                    return v.unsqueeze(2).to_broadcast([P, NT, NE])

                for i in range(2):
                    lg, eq, first, mask = rt[:, 3 * i], rt[:, 1], rs[:, 4 + i, :], rt[:, 4 + i]
                    link(dve.tensor_reduce(rs[:, i, :], lg, X_AXIS, ALU.max))
                    link(dve.tensor_tensor(eq, lg, bc(rs[:, i, :]), ALU.is_equal))
                    link(dve.tensor_tensor(eq, eq, em8b, ALU.mult))
                    link(dve.tensor_reduce(first, eq, X_AXIS, ALU.min))
                    link(dve.tensor_tensor(mask, em8b, bc(first), ALU.is_equal))
                    if i == 0:
                        link(dve.scalar_tensor_tensor(out=rt[:, 3], in0=mask, scalar=NEG, in1=lg, op0=ALU.mult, op1=ALU.add))
                dve.tensor_tensor(rs[:, 2, :], rs[:, 1, :], rs[:, 0, :], ALU.subtract).then_inc(r["d"], 1)
                dve.tensor_tensor(rt[:, 6], rt[:, 4], rt[:, 5], ALU.add).then_inc(r["mask"], 1)
                dve.wait_ge(r["ed"], 1)
                link(dve.tensor_scalar(rs[:, 6, :], rs[:, 3, :], 1.0, None, ALU.add))
                link(dve.reciprocal(rs[:, 6, :], rs[:, 6, :]))
                link(dve.tensor_tensor(rs[:, 7, :], rs[:, 6, :], rs[:, 3, :], ALU.mult))
                link(dve.tensor_tensor(rt[:, 4], rt[:, 4], bc(rs[:, 6, :]), ALU.mult))
                link(dve.tensor_tensor(rt[:, 5], rt[:, 5], bc(rs[:, 7, :]), ALU.mult))
                link(dve.tensor_tensor(wgt[:, :, 0:NE], rt[:, 4], rt[:, 5], ALU.add))
                dve.wait_ge(r["pos"], 1)
                link(dve.memset(posn[:], -1.0))
                link(dve.scalar_tensor_tensor(out=rt[:, 7], in0=PS[:, 3, 0:NT * NE].rearrange("p (t e) -> p t e", t=NT), scalar=1.0,
                                              in1=rt[:, 6], op0=ALU.add, op1=ALU.mult))
                link(dve.tensor_scalar(posn[:, :, 0:NE], rt[:, 7], -1.0, None, ALU.add))
                link(dve.tensor_copy(cntf[:, 0:NE], PS[0:1, 3, 2 * NT * NE:2 * NT * NE + NE]))
                link(dve.tensor_reduce(cntf[:, NE:NE + 1], cntf[:, 0:NE], X_AXIS, ALU.max))
                dve.tensor_copy(cnt[:], cntf[:]).then_inc(r["cnt"], 1)
                dve_select(dve, 0, 0)
                dve_start(dve, 0, 2)
                dve_gathered(dve, 0)
                dve_pass(dve, 0, 0, True, True)
                with dve.Fori(1, NE - 1) as ex:
                    dve_pass(dve, ex, ex, False, True)
                dve_pass(dve, NE - 1, NE - 1, False, False)
                dve_finish(dve, NE - 1)

            @block.tensor
            def _(pe):
                norm_f.pe(pe)
                norm_f.ready(pe, NT)
                pe.wait_ge(r["router"], 16)
                for t in range(NT):
                    for c in range(KC):
                        mm = pe.matmul(PS[:, 2, t * NE:(t + 1) * NE], hT[:, c, t * P:(t + 1) * P], router[:, c, :],
                                       start=(c == 0), stop=(c == KC - 1))
                mm.then_inc(r["lg"], 1)
                pe.wait_ge(r["mask"], 1)
                pe.matmul(PS[:, 3, 0:NE], upstrict[:], rt[:, 6, 0], start=True, stop=True)
                pe.matmul(PS[:, 3, NE:2 * NE], upstrict[:], rt[:, 6, 1], start=True, stop=False)
                pe.matmul(PS[:, 3, NE:2 * NE], ones[:], rt[:, 6, 0], start=False, stop=True)
                pe.matmul(PS[:, 3, 4 * NE:5 * NE], ones[:], rt[:, 6, 0], start=True, stop=False)
                pe.matmul(PS[:, 3, 4 * NE:5 * NE], ones[:], rt[:, 6, 1], start=False, stop=True).then_inc(r["pos"], 1)
                pe_gather(pe, 0)
                pe_pass(pe, 0, True, True)
                with pe.Fori(1, NE - 1) as ex:
                    pe_pass(pe, ex, False, True)
                pe_pass(pe, NE - 1, False, False)
                pe_finish(pe, NE - 1)

        def overflow(eng, one_pass):
            most = eng.value_load(cnt[0:1, NE:NE + 1], min_val=0, max_val=S)
            with eng.If(most > CAP):
                done = eng.alloc_register("passes_done")
                eng.reg_mov(done, NE)
                with eng.Fori(0, NE) as ex:
                    for b in range(1, NPB):
                        tokens = eng.value_load(cnt[0:1, bass.ds(ex, 1)], min_val=0, max_val=S)
                        with eng.If(tokens > b * CAP):
                            n = eng.snap(done, min_val=NE, max_val=2 * S * NT)
                            one_pass(ex, b, n)
                            eng.reg_add(done, done, 1)
                        with eng.Else():
                            eng.nop()
                        eng.nop()
                eng.nop()
            with eng.Else():
                eng.nop()
            eng.nop()

        with nc.Block() as block:
            @block.sync
            def _(sp):
                def one_pass(ex, b, n):
                    sp_start(sp, n, ex)
                    sp_pass(sp, n, ex, True, False)
                overflow(sp, one_pass)

            @block.scalar
            def _(act):
                def one_pass(ex, b, n):
                    act_start(act, n)
                    act_gathered(act, n)
                    act_pass(act, n, ex, True, False)
                    act_finish(act, n)
                overflow(act, one_pass)

            @block.vector
            def _(dve):
                def one_pass(ex, b, n):
                    after(dve, "gather", n, 1, 0)
                    after(dve, "selw", n, NT, 0)
                    dve_select(dve, ex, b)
                    dve_start(dve, n)
                    dve_gathered(dve, n)
                    dve_pass(dve, n, ex, True, False)
                    dve_finish(dve, n)
                overflow(dve, one_pass)

            @block.tensor
            def _(pe):
                def one_pass(ex, b, n):
                    after(pe, "x", n, 4, 0)
                    pe_gather(pe, n)
                    pe_pass(pe, n, True, False)
                    pe_finish(pe, n)
                overflow(pe, one_pass)


        with nc.Block() as block:
            @block.sync
            def _(sp):
                sp.dma_start(out[0].rearrange("(t p) d -> p t d", p=P), X[:]).then_inc(s_y, 16)
                sp.wait_ge(s_y, 16)


_INS = ['x', 'mem', 'mix_norm', 'ffn_norm', 'mem_norm', 'w_mem_kv', 'xa_q_norm', 'xa_k_norm', 'w_out',
        'sb_w_in', 'sb_q_norm', 'sb_k_norm', 'dn_w_in', 'dn_conv', 'dn_a_log', 'dn_dt_bias', 'dn_o_norm',
        'ffd_w_gate', 'ffd_w_up', 'ffd_w_down', 'moe_router', 'moe_w_gate', 'moe_w_up', 'moe_w_down']
_OUTS = [((1, S, D), 'float32')]


def kernel(**inputs):
    import numpy as _np
    import concourse.bacc as _bacc
    from concourse import mybir as _mybir
    from concourse.bass_utils import run_bass_kernel_spmd as _run

    nc = _bacc.Bacc("TRN2", target_bir_lowering=False, num_devices=1)
    arrays, args = {}, []
    for name in _INS:
        a = _np.ascontiguousarray(inputs[name])
        arrays[f"in_{name}_dram"] = a
        args.append(nc.dram_tensor(f"in_{name}_dram", a.shape, _mybir.dt.from_np(a.dtype), kind="ExternalInput").ap())
    for i, (shape, dtype) in enumerate(_OUTS):
        dt = _mybir.dt.from_np(_np.dtype(dtype))
        args.append(nc.dram_tensor(f"out_{i}_dram", shape, dt, kind="ExternalOutput").ap())
    hybrid_kernel(nc, *args)
    r = _run(nc, [arrays], core_ids=[0])
    got = tuple(r.results[0][f"out_{i}_dram"] for i in range(len(_OUTS)))
    return got[0]
```
